# Optimizing a Trainium2 kernel written in Bass

```python
import jax
import jax.numpy as jnp
from jax import lax
import numpy as np

D_MODEL = 1024
BATCH = 1
SEQ = 1024
DEPTH = 1
DEC_BATCH = 8
DEC_SEQ = 1
PAST_LEN = 2048
PAGE_SIZE = 128

HEAD_DIM = 64
RET_WIDTH = D_MODEL // 2
RET_HEADS = RET_WIDTH // HEAD_DIM
NSA_WIDTH = D_MODEL - RET_WIDTH
NSA_HEADS = NSA_WIDTH // HEAD_DIM
NSA_KV_HEADS = 2
NSA_GROUP = NSA_HEADS // NSA_KV_HEADS
KV_WIDTH = NSA_KV_HEADS * HEAD_DIM
MIX_WIDTH = RET_WIDTH + NSA_WIDTH
N_BRANCH = 3
IN_SPLITS = (RET_WIDTH, RET_WIDTH, RET_WIDTH, RET_WIDTH, NSA_WIDTH,
             KV_WIDTH, KV_WIDTH, KV_WIDTH, KV_WIDTH, KV_WIDTH, KV_WIDTH,
             NSA_HEADS * N_BRANCH)
IN_WIDTH = 4 * RET_WIDTH + NSA_WIDTH + 6 * KV_WIDTH + NSA_HEADS * N_BRANCH
D_FF = 4 * D_MODEL
CMP_BLOCK = 64
CMP_HIDDEN = HEAD_DIM
N_SELECT = 16
WINDOW = 512
Q_BLOCK = 128
RET_CHUNK = 128
ROPE_BASE = 10000.0
EPS = 1e-6
NEG = -1e30
SCALE = HEAD_DIM ** -0.5

kernel_name = 'hymba_retnet_nsa_step'

def rmsnorm(x, w):
    xf = x.astype(jnp.float32)
    y = xf * lax.rsqrt(jnp.mean(xf * xf, axis=-1, keepdims=True) + EPS)
    return (y * w).astype(x.dtype)

def rope(x, pos):
    half = HEAD_DIM // 2
    inv = ROPE_BASE ** (-jnp.arange(half, dtype=jnp.float32) / half)
    ang = pos.astype(jnp.float32)[:, None] * inv
    cos, sin = jnp.cos(ang)[:, None, :], jnp.sin(ang)[:, None, :]
    x1, x2 = x[..., :half].astype(jnp.float32), x[..., half:].astype(jnp.float32)
    return jnp.concatenate([x1 * cos - x2 * sin, x1 * sin + x2 * cos], -1).astype(x.dtype)

def mix_inputs(x, pos, ln_w, w_in):
    B, T, _ = x.shape
    h = rmsnorm(x, ln_w)
    parts = jnp.split(h @ w_in, np.cumsum(IN_SPLITS)[:-1].tolist(), axis=-1)
    rq, rk, rv, rg, nq, ck, cv, sk, sv, wk, wv, gt = parts
    rq = rope(rq.reshape(B, T, RET_HEADS, HEAD_DIM), pos)
    rk = rope(rk.reshape(B, T, RET_HEADS, HEAD_DIM), pos) * SCALE
    rv = rv.reshape(B, T, RET_HEADS, HEAD_DIM)
    nq = nq.reshape(B, T, NSA_KV_HEADS, NSA_GROUP, HEAD_DIM)
    kv = [t.reshape(B, T, NSA_KV_HEADS, HEAD_DIM) for t in (ck, cv, sk, sv, wk, wv)]
    gates = jax.nn.sigmoid(gt.astype(jnp.float32)).reshape(
        B, T, NSA_KV_HEADS, NSA_GROUP, N_BRANCH).astype(x.dtype)
    return (rq, rk, rv, rg, nq, gates, kv[0], kv[1], kv[2], kv[3], kv[4], kv[5])

def retention_chunkwise(q, k, v, s0, chunk):
    B, T, H, d = q.shape
    n = T // chunk
    lg = jnp.log1p(-jnp.exp2(-5.0 - jnp.arange(H, dtype=jnp.float32)))
    i = jnp.arange(chunk, dtype=jnp.float32)
    diff = i[:, None] - i[None, :]
    inner = jnp.where(diff >= 0, jnp.exp(lg[:, None, None] * jnp.maximum(diff, 0.0)), 0.0)
    q_dec = jnp.exp(lg[None, :] * (i[:, None] + 1.0))[None, :, :, None]
    k_dec = jnp.exp(lg[None, :] * (chunk - 1.0 - i[:, None]))[None, :, :, None]
    c_dec = jnp.exp(lg * chunk)[None, :, None, None]

    def blocks(t):
        return t.astype(jnp.float32).reshape(B, n, chunk, H, d).swapaxes(0, 1)

    def step(s, xs):
        qc, kc, vc = xs
        a = jnp.einsum('bihd,bjhd->bhij', qc, kc) * inner
        o = jnp.einsum('bhij,bjhd->bihd', a, vc) + jnp.einsum('bihd,bhde->bihe', qc, s) * q_dec
        s = s * c_dec + jnp.einsum('bjhd,bjhe->bhde', kc * k_dec, vc)
        return s, o

    s, o = lax.scan(step, s0.astype(jnp.float32), (blocks(q), blocks(k), blocks(v)))
    return o.swapaxes(0, 1).reshape(B, T, H, d).astype(q.dtype), s.astype(s0.dtype)

def retention_out(o, g, gn_w):
    B, T, H, d = o.shape
    of = o.astype(jnp.float32)
    mu = jnp.mean(of, -1, keepdims=True)
    var = jnp.mean(jnp.square(of - mu), -1, keepdims=True)
    y = ((of - mu) * lax.rsqrt(var + EPS)).reshape(B, T, H * d) * gn_w
    return (jax.nn.silu(g.astype(jnp.float32)) * y).astype(o.dtype)

def compress(rows, pos_emb, w1, w2):
    B, T, G, d = rows.shape
    nb = T // CMP_BLOCK
    blk = rows[:, :nb * CMP_BLOCK].reshape(B, nb, CMP_BLOCK, G, d) + pos_emb[:, None, :]
    h = jax.nn.gelu(jnp.einsum('bnlgd,ldf->bngf', blk, w1))
    return jnp.einsum('bngf,fd->bngd', h, w2)

def cmp_attend(q, kc, vc, pos_q):
    nb = kc.shape[1]
    s = jnp.einsum('bqgrd,bngd->bqgrn', q, kc).astype(jnp.float32) * SCALE
    valid = ((jnp.arange(nb) + 1) * CMP_BLOCK - 1)[None, :] <= pos_q[:, None]
    vm = valid[None, :, None, None, :]
    p = jnp.where(vm, jax.nn.softmax(jnp.where(vm, s, NEG), axis=-1), 0.0)
    o = jnp.einsum('bqgrn,bngd->bqgrd', p.astype(vc.dtype), vc)
    return o, p

def select_blocks(p, pos_q):
    nb = p.shape[-1]
    imp = jnp.sum(p, axis=3)
    cur = (pos_q // CMP_BLOCK).astype(jnp.int32)
    cand = jnp.arange(nb)[None, :] < cur[:, None]
    imp = jnp.where(cand[None, :, None, :], imp, -1.0)
    val, idx = lax.top_k(imp, min(N_SELECT - 1, nb))
    cur_b = jnp.broadcast_to(cur[None, :, None, None], idx.shape[:-1] + (1,))
    idx = jnp.concatenate([cur_b, idx.astype(jnp.int32)], -1)
    ok = jnp.concatenate([jnp.ones(cur_b.shape, dtype=bool), val >= 0.0], -1)
    return idx, ok

def sel_attend(q, kg, vg, pos_q, tok, ok):
    s = jnp.einsum('...qgrd,...qgskd->...qgrsk', q, kg).astype(jnp.float32) * SCALE
    mask = jnp.expand_dims(ok[..., None] & (tok <= pos_q[:, None, None, None]), -3)
    s = jnp.where(mask, s, NEG)
    p = jax.nn.softmax(s.reshape(s.shape[:-2] + (-1,)), axis=-1).reshape(s.shape)
    return jnp.einsum('...qgrsk,...qgskd->...qgrd', p.astype(vg.dtype), vg)

def sel_prompt(q, k_rows, v_rows, idx, ok):
    B, T, G, R, d = q.shape
    nq = T // Q_BLOCK
    S = idx.shape[-1]
    g_ix = jnp.arange(G)[None, :, None, None]
    offs = jnp.arange(CMP_BLOCK, dtype=jnp.int32)

    def one(args):
        i, qi, ii, oi = args
        b = i // nq
        pos_q = (i % nq) * Q_BLOCK + jnp.arange(Q_BLOCK, dtype=jnp.int32)
        tok = ii[..., None] * CMP_BLOCK + offs
        kb = k_rows[b][tok, g_ix]
        vb = v_rows[b][tok, g_ix]
        return sel_attend(qi, kb, vb, pos_q, tok, oi)

    out = lax.map(one, (jnp.arange(B * nq), q.reshape(B * nq, Q_BLOCK, G, R, d),
                        idx.reshape(B * nq, Q_BLOCK, G, S), ok.reshape(B * nq, Q_BLOCK, G, S)))
    return out.reshape(B, T, G, R, d)

def sel_sample(q, pool_k, pool_v, page_table, new_k, new_v, idx, ok, pos_q):
    DB, Qn, G, _ = new_k.shape
    past_len = page_table.shape[1] * PAGE_SIZE
    tok = idx[..., None] * CMP_BLOCK + jnp.arange(CMP_BLOCK, dtype=jnp.int32)
    b_ix = jnp.arange(DB)[:, None, None, None, None]
    g_ix = jnp.arange(G)[None, None, :, None, None]
    tp = jnp.minimum(tok, past_len - 1)
    phys = page_table[b_ix, tp // PAGE_SIZE]
    tn = jnp.clip(tok - past_len, 0, Qn - 1)
    is_past = (tok < past_len)[..., None]
    kg = jnp.where(is_past, pool_k[phys, tp % PAGE_SIZE, g_ix], new_k[b_ix, tn, g_ix])
    vg = jnp.where(is_past, pool_v[phys, tp % PAGE_SIZE, g_ix], new_v[b_ix, tn, g_ix])
    return sel_attend(q, kg, vg, pos_q, tok, ok)

def window_attend(q, k, v, pos_q, pos_k):
    s = jnp.einsum('...qgrd,...kgd->...qgrk', q, k).astype(jnp.float32) * SCALE
    dpos = pos_q[..., :, None] - pos_k[..., None, :]
    mask = (dpos >= 0) & (dpos < WINDOW) & (pos_k[..., None, :] >= 0)
    s = jnp.where(mask[..., :, None, None, :], s, NEG)
    p = jax.nn.softmax(s, axis=-1)
    return jnp.einsum('...qgrk,...kgd->...qgrd', p.astype(v.dtype), v)

def window_prompt(q, k, v):
    B, T, G, R, d = q.shape
    nq = T // Q_BLOCK
    nw = WINDOW // Q_BLOCK
    kl = (nw + 1) * Q_BLOCK
    bi = jnp.arange(nq)[:, None] + jnp.arange(nw + 1)[None, :]
    pos_q = jnp.arange(T, dtype=jnp.int32).reshape(nq, Q_BLOCK)
    pos_k = (jnp.arange(nq, dtype=jnp.int32)[:, None] - nw) * Q_BLOCK + jnp.arange(kl, dtype=jnp.int32)[None, :]

    def band(r):
        rp = jnp.pad(r, ((nw * Q_BLOCK, 0), (0, 0), (0, 0))).reshape(nq + nw, Q_BLOCK, G, d)
        return rp[bi].reshape(nq, kl, G, d)

    def one(args):
        qs, ks, vs = args
        return window_attend(qs.reshape(nq, Q_BLOCK, G, R, d), band(ks), band(vs), pos_q, pos_k)

    return lax.map(one, (q, k, v)).reshape(B, T, G, R, d)

def window_sample(q, buf_k, buf_v, new_k, new_v, pos_q, past_len):
    wb = buf_k.shape[1]
    qn = new_k.shape[1]
    k = jnp.concatenate([buf_k, new_k], 1)
    v = jnp.concatenate([buf_v, new_v], 1)
    pos_k = jnp.concatenate([past_len - wb + jnp.arange(wb, dtype=jnp.int32),
                             past_len + jnp.arange(qn, dtype=jnp.int32)])
    return window_attend(q, k, v, pos_q, pos_k), k[:, -wb:], v[:, -wb:]

def gather_pages(pool, page_table):
    DB, NP = page_table.shape
    return pool[page_table].reshape(DB, NP * PAGE_SIZE, NSA_KV_HEADS, HEAD_DIM)

def nsa_combine(gates, o_cmp, o_sel, o_win):
    B, T = o_cmp.shape[:2]
    o = gates[..., 0:1] * o_cmp + gates[..., 1:2] * o_sel + gates[..., 2:3] * o_win
    return o.reshape(B, T, NSA_WIDTH)

def finish(x, ret_y, nsa_y, w_o, ln_post_mix, ln_pre_ffn, w_up, w_down, ln_post_ffn):
    mix = jnp.concatenate([ret_y, nsa_y], -1) @ w_o
    h = x + rmsnorm(mix, ln_post_mix)
    f = jnp.square(jax.nn.relu(rmsnorm(h, ln_pre_ffn) @ w_up)) @ w_down
    return h + rmsnorm(f, ln_post_ffn)

def setup_inputs(seed: int = 0) -> dict:
    key = jax.random.key(seed)
    ks = jax.random.split(key, 32)
    f32 = jnp.float32
    n_pages = PAST_LEN // PAGE_SIZE
    n_phys = (DEC_BATCH * n_pages * 5) // 4
    win_len = min(WINDOW, PAST_LEN)

    def nrm(k, shape, s):
        return jax.random.normal(k, shape, f32) * s

    def gain(k, n):
        return 1.0 + 0.05 * jax.random.normal(k, (DEPTH, n), f32)

    page_table = jax.random.permutation(ks[0], n_phys)[:DEC_BATCH * n_pages].reshape(
        DEC_BATCH, n_pages).astype(jnp.int32)
    pool = (DEPTH, n_phys, PAGE_SIZE, NSA_KV_HEADS, HEAD_DIM)
    wbuf = (DEPTH, DEC_BATCH, win_len, NSA_KV_HEADS, HEAD_DIM)
    return {
        'x_prompt': nrm(ks[1], (BATCH, SEQ, D_MODEL), 1.0),
        'x_sample': nrm(ks[2], (DEC_BATCH, DEC_SEQ, D_MODEL), 1.0),
        'state_ret': nrm(ks[3], (DEPTH, DEC_BATCH, RET_HEADS, HEAD_DIM, HEAD_DIM), 1.0),
        'cache_cmp_k': nrm(ks[4], pool, 1.0),
        'cache_cmp_v': nrm(ks[5], pool, 1.0),
        'cache_sel_k': nrm(ks[6], pool, 1.0),
        'cache_sel_v': nrm(ks[7], pool, 1.0),
        'cache_win_k': nrm(ks[8], wbuf, 1.0),
        'cache_win_v': nrm(ks[9], wbuf, 1.0),
        'page_table': page_table,
        'ln_pre_mix': gain(ks[10], D_MODEL),
        'w_in': nrm(ks[11], (DEPTH, D_MODEL, IN_WIDTH), D_MODEL ** -0.5),
        'ret_gn_w': gain(ks[12], RET_WIDTH),
        'cmp_pos_k': nrm(ks[13], (DEPTH, CMP_BLOCK, HEAD_DIM), 0.1),
        'cmp_w1_k': nrm(ks[14], (DEPTH, CMP_BLOCK, HEAD_DIM, CMP_HIDDEN), (CMP_BLOCK * HEAD_DIM) ** -0.5),
        'cmp_w2_k': nrm(ks[15], (DEPTH, CMP_HIDDEN, HEAD_DIM), CMP_HIDDEN ** -0.5),
        'cmp_pos_v': nrm(ks[16], (DEPTH, CMP_BLOCK, HEAD_DIM), 0.1),
        'cmp_w1_v': nrm(ks[17], (DEPTH, CMP_BLOCK, HEAD_DIM, CMP_HIDDEN), (CMP_BLOCK * HEAD_DIM) ** -0.5),
        'cmp_w2_v': nrm(ks[18], (DEPTH, CMP_HIDDEN, HEAD_DIM), CMP_HIDDEN ** -0.5),
        'w_o': nrm(ks[19], (DEPTH, MIX_WIDTH, D_MODEL), MIX_WIDTH ** -0.5),
        'ln_post_mix': gain(ks[20], D_MODEL),
        'ln_pre_ffn': gain(ks[21], D_MODEL),
        'w_up': nrm(ks[22], (DEPTH, D_MODEL, D_FF), D_MODEL ** -0.5),
        'w_down': nrm(ks[23], (DEPTH, D_FF, D_MODEL), D_FF ** -0.5),
        'ln_post_ffn': gain(ks[24], D_MODEL),
    }

def reference(x_prompt, x_sample, state_ret, cache_cmp_k, cache_cmp_v, cache_sel_k, cache_sel_v,
              cache_win_k, cache_win_v, page_table, ln_pre_mix, w_in, ret_gn_w,
              cmp_pos_k, cmp_w1_k, cmp_w2_k, cmp_pos_v, cmp_w1_v, cmp_w2_v,
              w_o, ln_post_mix, ln_pre_ffn, w_up, w_down, ln_post_ffn):
    B, T, _ = x_prompt.shape
    DB, Tn, _ = x_sample.shape
    past_len = page_table.shape[1] * PAGE_SIZE
    pos_p = jnp.arange(T, dtype=jnp.int32)
    pos_s = past_len + jnp.arange(Tn, dtype=jnp.int32)
    win_p = min(WINDOW, T)
    xp, xs = x_prompt, x_sample
    rs_p, ck_p, cv_p, sk_p, sv_p, wk_p, wv_p = [], [], [], [], [], [], []
    rs_s, ck_s, cv_s, sk_s, sv_s, wk_s, wv_s = [], [], [], [], [], [], []
    for l in range(DEPTH):
        tail = (w_o[l], ln_post_mix[l], ln_pre_ffn[l], w_up[l], w_down[l], ln_post_ffn[l])
        rq, rk, rv, rg, nq, gates, ck, cv, sk, sv, wk, wv = mix_inputs(xp, pos_p, ln_pre_mix[l], w_in[l])
        s0 = jnp.zeros((B, RET_HEADS, HEAD_DIM, HEAD_DIM), xp.dtype)
        ro, rs = retention_chunkwise(rq, rk, rv, s0, min(RET_CHUNK, T))
        kc = compress(ck, cmp_pos_k[l], cmp_w1_k[l], cmp_w2_k[l])
        vc = compress(cv, cmp_pos_v[l], cmp_w1_v[l], cmp_w2_v[l])
        o_cmp, p = cmp_attend(nq, kc, vc, pos_p)
        idx, ok = select_blocks(p, pos_p)
        o_sel = sel_prompt(nq, sk, sv, idx, ok)
        o_win = window_prompt(nq, wk, wv)
        xp = finish(xp, retention_out(ro, rg, ret_gn_w[l]), nsa_combine(gates, o_cmp, o_sel, o_win), *tail)
        rs_p.append(rs); ck_p.append(ck); cv_p.append(cv); sk_p.append(sk); sv_p.append(sv)
        wk_p.append(wk[:, T - win_p:]); wv_p.append(wv[:, T - win_p:])
        rq, rk, rv, rg, nq, gates, ck, cv, sk, sv, wk, wv = mix_inputs(xs, pos_s, ln_pre_mix[l], w_in[l])
        ro, rs = retention_chunkwise(rq, rk, rv, state_ret[l], Tn)
        kc = compress(jnp.concatenate([gather_pages(cache_cmp_k[l], page_table), ck], 1),
                      cmp_pos_k[l], cmp_w1_k[l], cmp_w2_k[l])
        vc = compress(jnp.concatenate([gather_pages(cache_cmp_v[l], page_table), cv], 1),
                      cmp_pos_v[l], cmp_w1_v[l], cmp_w2_v[l])
        o_cmp, p = cmp_attend(nq, kc, vc, pos_s)
        idx, ok = select_blocks(p, pos_s)
        o_sel = sel_sample(nq, cache_sel_k[l], cache_sel_v[l], page_table, sk, sv, idx, ok, pos_s)
        o_win, nwk, nwv = window_sample(nq, cache_win_k[l], cache_win_v[l], wk, wv, pos_s, past_len)
        xs = finish(xs, retention_out(ro, rg, ret_gn_w[l]), nsa_combine(gates, o_cmp, o_sel, o_win), *tail)
        rs_s.append(rs); ck_s.append(ck); cv_s.append(cv); sk_s.append(sk); sv_s.append(sv)
        wk_s.append(nwk); wv_s.append(nwv)
    return (xp, xs,
            jnp.stack(rs_p), jnp.stack(ck_p), jnp.stack(cv_p), jnp.stack(sk_p), jnp.stack(sv_p),
            jnp.stack(wk_p), jnp.stack(wv_p),
            jnp.stack(rs_s), jnp.stack(ck_s), jnp.stack(cv_s), jnp.stack(sk_s), jnp.stack(sv_s),
            jnp.stack(wk_s), jnp.stack(wv_s))


_drawn_inputs = setup_inputs


def setup_inputs(seed=0):
    import zlib

    import numpy as np

    out = dict(_drawn_inputs(seed))
    spreads = {}
    factors = {'cmp_pos_k': 7.002}
    for name, (base, spread) in spreads.items():
        noise = np.random.default_rng([zlib.crc32(name.encode()), seed]).standard_normal(out[name].shape)
        drawn = base * np.exp(spread * noise) if base else spread * noise
        out[name] = jnp.asarray(drawn.astype(out[name].dtype))
    for name, factor in factors.items():
        out[name] = (out[name] * factor).astype(out[name].dtype)
    return out
```

```python
import math
from contextlib import ExitStack

import numpy as np

import concourse.bass as bass
from concourse import mybir

ALU = mybir.AluOpType
ACT = mybir.ActivationFunctionType
AX = mybir.AxisListType
F32 = mybir.dt.float32
F32R = mybir.dt.float32r
BF16 = mybir.dt.bfloat16
I32 = mybir.dt.int32

P = 128
D_MODEL, SEQ, DEC = 1024, 1024, 8
HD = 64
RH, NH, G, R = 8, 8, 2, 4
PAST, PAGE, WIN = 2048, 128, 512
D_FF = 4096
CB = 64
IN_W = 3352
EPS = 1e-6
NEG = -1e30
SCALE = HD ** -0.5
TOK = SEQ + DEC
TN = TOK // 3
KT = D_MODEL // P
NB = SEQ // P
NPG = PAST // PAGE
NBLK = PAST // CB
NSEL = 15
QUARTERS = 4
ROWS = DEC * NH

CP = 40

_COLS = [("ident", P), ("perm", P), ("headmean", P), ("ones", P), ("causal", P), ("winlow", P),
         ("cos", TOK), ("sin", TOK), ("inner", RH * P), ("qdec", 4 * P), ("kdec", RH), ("cdec", 4),
         ("gamma", 4), ("cmpbias", NB * CP), ("cmpvalid", NB * CP),
         ("winfirst", 1)]
_DEC_COLS = [("ownblocks", DEC * G * NBLK), ("ownrow", DEC), ("earlier", NBLK * NBLK), ("headrows", ROWS)]


def _places(columns):
    at, o = {}, 0
    for name, width in columns:
        at[name] = (o, o + width)
        o += width
    return at, o


CO, CW = _places(_COLS)
DO, DW = _places(_DEC_COLS)


def constants():
    main, decoded = np.zeros((P, CW), np.float32), np.zeros((ROWS, DW), np.float32)

    def put(name, a):
        a = np.asarray(a, np.float32)
        c, (lo, hi) = (main, CO[name]) if name in CO else (decoded, DO[name])
        c[:a.shape[0], lo:hi] = a.reshape(a.shape[0], hi - lo)

    p = np.arange(P)
    put("ident", np.eye(P))
    perm = np.zeros((P, P))
    perm[(p // HD) * HD + (p % HD + HD // 2) % HD, p] = 1.0
    put("perm", perm)
    put("headmean", (p[:, None] // HD == p[None, :] // HD) / HD)
    put("ones", np.ones((P, P)))
    put("causal", np.where(p[None, :] > p[:, None], NEG, 0.0))
    put("winlow", np.where(p[None, :] > p[:, None], 0.0, NEG))
    half = HD // 2
    inv = np.float32(10000.0) ** (-np.arange(half, dtype=np.float32) / np.float32(half))
    pos = np.concatenate([np.arange(SEQ), np.full(DEC, PAST)]).astype(np.float32)
    ang = (pos[None, :] * inv[p % half][:, None]).astype(np.float32)
    put("cos", np.cos(ang))
    put("sin", np.sin(ang) * np.where(p % HD < half, -1.0, 1.0)[:, None].astype(np.float32))
    lg = np.log1p(-np.exp2(-5.0 - np.arange(RH, dtype=np.float64)))
    diff = p[None, :] - p[:, None]
    inner = np.where(diff[:, None, :] >= 0, np.exp(lg[None, :, None] * np.maximum(diff[:, None, :], 0)), 0.0)
    put("inner", inner)
    lg2 = lg[2 * np.arange(4)[None, :] + (p // HD)[:, None]]
    put("qdec", np.exp(lg2[:, :, None] * (p[None, None, :] + 1)))
    put("kdec", np.exp(lg[None, :] * (P - 1 - p[:, None])))
    put("cdec", np.exp(lg2 * P))
    put("gamma", np.exp(lg2))
    posq = (np.arange(NB)[None, :] * P + p[:, None])[:, :, None]
    place = np.arange(CP)
    block = np.where(place % 32 < NB, 2 * (place % 32) + place // 32, SEQ)
    ok = (block[None, None, :] + 1) * CB - 1 <= posq
    put("cmpbias", np.where(ok, 0.0, NEG))
    put("cmpvalid", ok)
    row = np.arange(ROWS)
    own = row[:, None] // R == np.arange(DEC * G)[None, :]
    own = own.reshape(ROWS, 2, 1, 4, 1, G) & np.ones((1, 1, 2, 1, NPG, 1), bool)
    put("ownblocks", np.where(own, 0.0, NEG))
    nu = 2 * (np.arange(NBLK) % NPG) + np.arange(NBLK) // NPG
    put("earlier", np.broadcast_to(nu[None, None, :] < nu[None, :, None], (ROWS, NBLK, NBLK)))
    put("ownrow", row[:, None] // NH == np.arange(DEC)[None, :])
    put("headrows", row[:, None] // R == row[None, :] // R)
    put("winfirst", np.where(p[:, None] == 0, NEG, 0.0))
    return main, decoded


class Steps:

    def __init__(self, sem, base=0, it=None, per=0):
        self.sem, self.base, self.it, self.per, self.n = sem, base, it, per, 0

    def value(self, n):
        v = self.base + n
        return v if self.it is None else self.it * self.per + v

    def done(self, ins):
        ins.then_inc(self.sem, 1)
        self.n += 1
        return self.n

    def fence(self, eng):
        eng.wait_ge(self.sem, self.value(self.n))


class Stage(ExitStack):

    def __init__(self, nc, tag):
        super().__init__()
        self.nc, self.tag, self.taken = nc, tag, []
        self.callback(self.give_back)

    def semaphore(self, name):
        self.taken.append(self.nc.alloc_semaphore(name=f"{self.tag}_{name}"))
        return self.taken[-1]

    def give_back(self):
        self.nc.clear_and_free_semaphores(self.taken)
        self.nc.all_engine_barrier()


class Memory:

    def __init__(self, nc):
        self.nc = nc
        base = (int(nc.sbuf_base) + 31) // 32 * 32
        T1 = TOK * 4
        self.const = self.place("const", [P, CW], F32, base)
        o = base + (CW * 4 + 31) // 32 * 32
        self.lnT = self.place("lnT", [P, 36], F32, o)
        self.small = self.place("small", [P, 64], F32, o + 160)
        self.gate_tok = self.place("gate_tok", [P, NB + 1, 24], F32, o + 416)
        self.ident_bf = self.place("ident_bf", [P, P], BF16, o + 1280)
        self.causal_bf = self.place("causal_bf", [P, P], BF16, o + 1536)
        self.winlow_bf = self.place("winlow_bf", [P, P], BF16, o + 1792)
        o += 2048
        self.ring = o
        self.wraw = [self.place(f"wraw{i}", [P, KT, P], F32, o + 4096 * i) for i in range(2)]
        self.whi = [self.place(f"whi{i}", [P, KT, P], F32R, o + 8192 + 4096 * i) for i in range(2)]
        self.wlo = [self.place(f"wlo{i}", [P, KT, P], F32R, o + 16384 + 4096 * i) for i in range(2)]
        o += 24576
        self.mixT = self.place("mixT", [P, KT, TOK], F32, o)
        self.M = o
        o += KT * T1
        self.A = o
        self.hi = self.place("act_hi", [P, KT, TOK], F32R, o)
        self.lo = self.place("act_lo", [P, KT, TOK], F32R, o + KT * T1)
        o += 70208
        self.N = o
        self.nqT = self.place("nqT", [P, 4, TOK], F32, o)
        self.selkT = self.place("sel_kT", [P, G, TOK], F32, o + 4 * T1)
        self.winkT = self.place("win_kT", [P, G, TOK], F32, o + 6 * T1)
        o += 8 * T1
        tok = (NB + 1) * P * 4
        self.ck_tok, self.cv_tok, self.sv_tok, self.wv_tok, self.k_stage = (
            self.place(n, [P, NB + 1, P], F32, o + i * tok)
            for i, n in enumerate(("cmp_k_rows", "cmp_v_rows", "sel_v_rows", "win_v_rows", "k_rows_staged")))
        self.feat = self.place("feature_rows", [P, TOK], F32, o + 5 * tok)
        self.stage = o + 4 * tok
        lo = (base + CO["cos"][0] * 4 + 31) // 32 * 32
        self.kcsT = self.place("cmp_kT_decoded", [HD, 4 * P], F32, lo)
        self.kcpT = self.place("cmp_kT_prompt", [P, G, CP], F32, lo + 2048)
        self.vcs = self.place("cmp_v_decoded", [P, 4, P], F32, lo + 2400 - 32)
        self.vcp = self.place("cmp_v_prompt", [CP, P], F32, lo + 4416)
        self.tables = lo
        assert o + 5 * tok + T1 <= int(nc.sbuf_usable_end)

    def place(self, name, shape, dt, offset):
        return self.nc.alloc_sbuf_tensor_at(name, shape, dt, offset=offset)

    def c(self, name, rows=P):
        lo, hi = CO[name]
        return self.const[0:rows, lo:hi]


def matmul3(pe, out, w_hi, w_lo, x_hi, x_lo):
    pairs = [(w_hi, x_hi), (w_hi, x_lo), (w_lo, x_hi)]
    for kt in range(KT):
        for n, (w, x) in enumerate(pairs):
            last = pe.matmul(out, w[:, kt, :], x[:, kt, :], start=(kt == 0 and n == 0),
                             stop=(kt == KT - 1 and n == 2))
    return last


class Stream:

    def __init__(self, ctx, m, ps, x_hi=None, x_lo=None):
        self.m, self.ps = m, ps
        self.x_hi, self.x_lo = x_hi or m.hi, x_lo or m.lo
        s = ctx.semaphore
        self.raw_loaded = [s("raw_loaded0"), s("raw_loaded1")]
        self.hi_ready = s("w_hi_ready")
        self.lo_ready = s("w_lo_ready")
        self.tile_done = s("tile_done")
        self.bank_free = s("bank_free")

    def load(self, sp, n, slot, src):
        sp.wait_ge(self.lo_ready, n + 1)
        sp.dma_start(self.m.wraw[slot][:], src).then_inc(self.raw_loaded[slot], 16)

    def round_hi(self, act, n, slot, half):
        act.wait_ge(self.raw_loaded[slot], half * 16 + 16)
        act.wait_ge(self.tile_done, n * 3 + 3)
        act.activation(self.m.whi[slot][:], self.m.wraw[slot][:], ACT.Copy).then_inc(self.hi_ready, 1)

    def reduce_lo(self, dve, n, slot, half):
        dve.wait_ge(self.raw_loaded[slot], half * 16 + 16)
        dve.wait_ge(self.hi_ready, n + 1)
        dve.tensor_tensor(self.m.wlo[slot][:], self.m.wraw[slot][:], self.m.whi[slot][:].bitcast(F32),
                          ALU.subtract).then_inc(self.lo_ready, 1)

    def start_loads(self, dve):
        dve.sem_inc(self.lo_ready, 2)

    def start(self, pe):
        pe.sem_inc(self.tile_done, 6)
        pe.sem_inc(self.bank_free, 3)

    def multiply(self, pe, n, slot, x_hi=None, x_lo=None):
        pe.wait_ge(self.hi_ready, n + 1)
        pe.wait_ge(self.lo_ready, n + 3)
        x_hi, x_lo = x_hi or self.x_hi, x_lo or self.x_lo
        for t in range(3):
            pe.wait_ge(self.bank_free, n * 3 + (t + 1))
            cols = slice(t * TN, (t + 1) * TN)
            last = matmul3(pe, self.ps[:, t, 0:TN], self.m.whi[slot], self.m.wlo[slot],
                           x_hi[:, :, cols], x_lo[:, :, cols])
            last.then_inc(self.tile_done, 1)

    def tiles(self, eng, n):
        for t in range(3):
            eng.wait_ge(self.tile_done, n * 3 + (6 + t + 1))
            yield t, slice(t * TN, (t + 1) * TN), self.ps[:, t, 0:TN]

    def evacuated(self, n, t):
        return n * 3 + (3 + t + 1)


def stage_prepare(nc, m, ps, io):
    with Stage(nc, "prep") as ctx:
        s = ctx.semaphore
        const_loaded, ln_loaded, x_loaded, xs_loaded = s("const_loaded"), s("ln_loaded"), [s("x_loaded0"), s("x_loaded1")], s("xs_loaded")
        win_copied = s("win_copied")
        squares, mean_ready, root_ready = s("squares"), s("mean_ready"), s("root_ready")
        rstd_ready, scaled, turned = s("rstd_ready"), s("scaled"), s("turned")
        hi_done, lo_done, ln_turned, ln_ready = s("hi_done"), s("lo_done"), s("ln_turned"), s("ln_ready")
        casts = s("casts")
        x = m.place("x_rows", [P, NB, D_MODEL], F32, m.N)
        xs = m.place("x_decoded", [DEC, D_MODEL], F32, m.N + NB * D_MODEL * 4)
        junk = m.place("squares_out", [P, D_MODEL], F32, m.N + (NB + 1) * D_MODEL * 4)
        lnrows = m.place("ln_rows", [36, P], F32, m.N + (NB + 2) * D_MODEL * 4)
        sums = m.small[:, 0:NB + 1]
        rstd = m.small[:, 16:16 + NB + 1]
        units = [(kt, h) for kt in range(KT) for h in range(3)]

        def span(h):
            return (slice(0, 512), slice(512, 1024), slice(SEQ, TOK))[h]

        block = ctx.enter_context(nc.Block())

        @block.sync
        def _(sp):
            for h in range(2):
                sp.dma_start(x[:, 4 * h:4 * h + 4, :], io["x_prompt"][0, 512 * h:512 * h + 512, :]
                             .rearrange("(t p) d -> p t d", p=P)).then_inc(x_loaded[h], 16)
            sp.dma_start(m.const[:], io["const"]).then_inc(const_loaded, 16)

        @block.gpsimd
        def _(pool):
            pool.dma_start(xs[:], io["x_sample"][:, 0, :]).then_inc(xs_loaded, 16)
            for i, w in enumerate(("ln_pre_mix", "ln_post_mix", "ln_pre_ffn", "ln_post_ffn", "ret_gn_w")):
                src = io[w][0, :].rearrange("(k p) -> k p", p=P)
                pool.dma_start(lnrows[8 * i:8 * i + src.shape[0], :], src).then_inc(ln_loaded, 16)
            for old, new in (("cache_win_k", "win_k_sample"), ("cache_win_v", "win_v_sample")):
                pool.dma_start(io[new][0, :, 0:WIN - 1].rearrange("b t g d -> b (t g d)"),
                               io[old][0, :, 1:WIN].rearrange("b t g d -> b (t g d)")).then_inc(win_copied, 16)
            pool.wait_ge(win_copied, 32)

        @block.scalar
        def _(act):
            act.wait_ge(xs_loaded, 16)
            act.activation(junk[0:DEC, :], xs[:], ACT.Square, accum_out=sums[0:DEC, NB:NB + 1]).then_inc(squares, 1)
            for t in range(NB):
                if t % 4 == 0:
                    act.wait_ge(x_loaded[t // 4], 16)
                act.wait_ge(squares, t + 1)
                act.activation(junk[:], x[:, t, :], ACT.Square, accum_out=sums[:, t:t + 1]).then_inc(squares, 1)
            act.wait_ge(mean_ready, 2)
            act.activation(rstd[:, 0:NB], rstd[:, 0:NB], ACT.Sqrt).then_inc(root_ready, 1)
            act.activation(rstd[0:DEC, NB:NB + 1], rstd[0:DEC, NB:NB + 1], ACT.Sqrt).then_inc(root_ready, 1)
            act.wait_ge(ln_turned, 1)
            act.activation(m.lnT[:], ps[:, 7, 0:36], ACT.Copy).then_inc(ln_ready, 1)
            act.wait_ge(ln_ready, 1)
            for u, (kt, h) in enumerate(units):
                act.wait_ge(turned, u + 1)
                cols = span(h)
                act.activation(m.hi[:, kt, cols], ps[:, u % 6, 0:cols.stop - cols.start], ACT.Copy,
                               scale=m.lnT[:, kt:kt + 1]).then_inc(hi_done, 1)

        @block.vector
        def _(dve):
            dve.wait_ge(const_loaded, 16)
            for dst, name in ((m.ident_bf, "ident"), (m.causal_bf, "causal"), (m.winlow_bf, "winlow")):
                dve.tensor_copy(dst[:], m.c(name)).then_inc(casts, 1)
            dve.wait_ge(squares, NB + 1)
            dve.tensor_scalar(rstd[:, 0:NB], sums[:, 0:NB], 1.0 / D_MODEL, EPS, ALU.mult, ALU.add).then_inc(mean_ready, 1)
            dve.tensor_scalar(rstd[0:DEC, NB:NB + 1], sums[0:DEC, NB:NB + 1], 1.0 / D_MODEL, EPS, ALU.mult,
                              ALU.add).then_inc(mean_ready, 1)
            dve.wait_ge(root_ready, 2)
            dve.reciprocal(rstd[:, 0:NB], rstd[:, 0:NB]).then_inc(rstd_ready, 1)
            dve.reciprocal(rstd[0:DEC, NB:NB + 1], rstd[0:DEC, NB:NB + 1]).then_inc(rstd_ready, 1)
            dve.wait_ge(rstd_ready, 2)
            for t in range(NB):
                dve.tensor_scalar(x[:, t, :], x[:, t, :], rstd[:, t:t + 1], None, ALU.mult).then_inc(scaled, 1)
            dve.tensor_scalar(xs[:], xs[:], rstd[0:DEC, NB:NB + 1], None, ALU.mult).then_inc(scaled, 1)
            for u, (kt, h) in enumerate(units):
                dve.wait_ge(hi_done, u + 1)
                cols = span(h)
                dve.scalar_tensor_tensor(m.lo[:, kt, cols], ps[:, u % 6, 0:cols.stop - cols.start],
                                         m.lnT[:, kt:kt + 1], m.hi[:, kt, cols].bitcast(F32),
                                         ALU.mult, ALU.subtract).then_inc(lo_done, 1)

        @block.tensor
        def _(pe):
            pe.wait_ge(const_loaded, 16)
            pe.wait_ge(ln_loaded, 80)
            pe.transpose(ps[:, 7, 0:36], lnrows[:], m.c("ident")[0:36, 0:36]).then_inc(ln_turned, 1)
            for u, (kt, h) in enumerate(units):
                if u >= 6:
                    pe.wait_ge(lo_done, u - 5)
                if h < 2:
                    pe.wait_ge(scaled, 4 * h + 4)
                    for i in range(4):
                        last = pe.transpose(ps[:, u % 6, i * P:(i + 1) * P],
                                            x[:, 4 * h + i, kt * P:(kt + 1) * P], m.c("ident"))
                else:
                    pe.wait_ge(scaled, NB + 1)
                    last = pe.transpose(ps[:, u % 6, 0:DEC], xs[:, kt * P:(kt + 1) * P],
                                        m.c("ident")[0:DEC, 0:DEC])
                last.then_inc(turned, 1)


def stage_project(nc, m, ps, io):
    with Stage(nc, "proj") as ctx:
        s = ctx.semaphore
        w = Stream(ctx, m, ps)
        B = m.N
        T1 = TOK * 4
        qT = m.place("ret_qT", [P, TOK], F32, B)
        kT = m.place("ret_kT", [P, TOK], F32, B + T1)
        vT = m.place("ret_vT", [P, TOK], F32, B + 2 * T1)
        rope_tmp = m.place("rope_tmp", [P, TOK], F32, B + 3 * T1)
        o = B + 4 * T1
        qd = m.place("ret_q_decayed", [P, SEQ], F32, o)
        k_tok = m.place("ret_k_decayed", [P, NB, P], F32, o + 4096)
        v_tok = m.place("ret_v", [P, NB, P], F32, o + 8192)
        states = m.place("ret_states", [P, NB, P], F32, o + 12288)
        aT = [m.place(f"ret_aT{i}", [P, 2, P], F32, o + 16384 + 1024 * i) for i in range(2)]
        s_in = m.place("dec_state_in", [P, DEC, HD], F32, o + 18432)
        s_new = m.place("dec_state_new", [P, DEC, HD], F32, o + 20480)
        v_diag = m.place("dec_v_diag", [DEC, DEC, P], F32, o + 22528)
        kv_dec = m.place("dec_kv", [DEC, 2, P], F32, o + 26624)

        raw_src = io["w_in"][0].rearrange("(kt p) n -> p kt n", p=P)
        s_src = io["state_ret"][0].rearrange("b h d e -> h d b e")
        s_dst = io["ret_state_sample"][0].rearrange("b h d e -> h d b e")
        p_dst = io["ret_state_prompt"][0, 0]

        swapped = s("swapped")
        swap_read = s("swap_read")
        roped = s("roped")
        turned = s("turned")
        tok_ready = s("tok_ready")
        kv_made = s("kv_made")
        state_made = s("state_made")
        diag_made = s("diag_made")
        outer_made = s("outer_made")
        dec_state = s("dec_state")
        q_decayed = s("q_decayed")
        scores_made = s("scores_made")
        scores_masked = s("scores_masked")
        out_made = s("out_made")
        out_copied = s("out_copied")
        state_loaded, state_stored, pool_past = s("state_loaded"), s("state_stored"), s("pool_past")
        feat_turned, feat_copied, k_spread = s("feat_turned"), s("feat_copied"), s("k_spread")
        rows_stored, sk_stored = s("rows_stored"), s("sk_stored")
        tmpF = m.feat

        block = ctx.enter_context(nc.Block())
        COLS = [0, 512, 1024, 1536]
        TAIL = [2560, 2688, 2816, 2944, 3072, 3200, IN_W - P]
        NQ0, TAIL0 = 16, 20

        @block.sync
        def _(sp):
            with sp.Fori(0, 4) as j:
                for t, c in enumerate(COLS):
                    w.load(sp, j * 4 + t, t % 2, raw_src[:, :, bass.ds(j * P + c, P)])
            with sp.Fori(0, 2) as i:
                for t in range(2):
                    w.load(sp, i * 2 + (NQ0 + t), t, raw_src[:, :, bass.ds(i * (2 * P) + (2048 + t * P), P)])
            for i, c in enumerate(TAIL):
                w.load(sp, TAIL0 + i, i % 2, raw_src[:, :, c:c + P])

        @block.tensor
        def _(pe):
            w.start(pe)
            pe.sem_inc(out_copied, 3)
            with pe.Fori(0, 4) as j:
                for t in range(4):
                    w.multiply(pe, j * 4 + t, t % 2)
                pe.wait_ge(out_copied, j * 3 + 3)
                for t in range(3):
                    last = pe.matmul(ps[:, 3 + t, 0:TN], m.c("perm"), qT[:, t * TN:(t + 1) * TN], start=True, stop=True)
                last.then_inc(swapped, 1)
                pe.wait_ge(w.bank_free, j * 12 + (3 + 9))
                for i in range(NB):
                    last = pe.transpose(ps[:, 6 + i // 4, (i % 4) * P:(i % 4 + 1) * P], vT[:, i * P:(i + 1) * P], m.c("ident"))
                last.then_inc(turned, 1)
                pe.wait_ge(swap_read, j * 2 + 1)
                for t in range(3):
                    last = pe.matmul(ps[:, 3 + t, 0:TN], m.c("perm"), kT[:, t * TN:(t + 1) * TN], start=True, stop=True)
                last.then_inc(swapped, 1)
                pe.wait_ge(roped, j * 4 + 4)
                pe.transpose(ps[0:DEC, 3, 0:P], kT[:, SEQ:TOK], m.c("ident"))
                pe.transpose(ps[0:DEC, 3, P:2 * P], vT[:, SEQ:TOK], m.c("ident")).then_inc(turned, 1)
                pe.wait_ge(tok_ready, j * 4 + 1)
                for i in range(NB):
                    last = pe.transpose(ps[:, 6 + i // 4, (i % 4) * P:(i % 4 + 1) * P], kT[:, i * P:(i + 1) * P], m.c("ident"))
                last.then_inc(turned, 1)
                pe.wait_ge(diag_made, j + 1)
                for h in range(2):
                    last = pe.matmul(ps[:, 4 + h, :], kv_dec[:, 0, :], v_diag[:, 4 * h:4 * h + 4, :], start=True, stop=True)
                last.then_inc(outer_made, 1)
                pe.wait_ge(tok_ready, j * 4 + 4)
                for i in range(NB):
                    last = pe.matmul(ps[:, 6 + i // 4, (i % 4) * P:(i % 4 + 1) * P], k_tok[:, i, :], v_tok[:, i, :], start=True, stop=True)
                    if i % 4 == 3:
                        last.then_inc(kv_made, 1)

                def scores(i):
                    if i >= 2:
                        pe.wait_ge(scores_masked, j * 8 + (i - 1))
                    for h in range(2):
                        rows = slice(h * HD, (h + 1) * HD)
                        last = pe.matmul(ps[:, 3 - 2 * (i % 2) + h, 0:P], kT[rows, i * P:(i + 1) * P],
                                         qT[rows, i * P:(i + 1) * P], start=True, stop=True)
                    last.then_inc(scores_made, 1)

                pe.wait_ge(dec_state, j * 2 + 2)
                pe.wait_ge(w.bank_free, j * 12 + (3 + 12))
                scores(0)
                for b in range(DEC):
                    for h in range(2):
                        rows = slice(h * HD, (h + 1) * HD)
                        last = pe.matmul(ps[rows, 5, b:b + 1], s_new[rows, b, :], qT[rows, SEQ + b:SEQ + b + 1],
                                         start=True, stop=True)
                last.then_inc(out_made, 1)
                pe.wait_ge(state_made, j * 8 + 8)
                pe.wait_ge(q_decayed, j + 1)
                for i in range(NB):
                    if i + 1 < NB:
                        scores(i + 1)
                    pe.wait_ge(scores_masked, j * 8 + (i + 1))
                    for h in range(2):
                        rows = slice(h * HD, (h + 1) * HD)
                        out = ps[rows, 6 + i // 4, (i % 4) * P:(i % 4 + 1) * P]
                        last = pe.matmul(out, v_tok[:, i, rows], aT[i % 2][:, h, :], start=True, stop=(i == 0))
                        if i:
                            last = pe.matmul(out, states[rows, i - 1, rows], qd[rows, i * P:(i + 1) * P],
                                             start=False, stop=True)
                    if i % 4 == 3:
                        last.then_inc(out_made, 1)
            with pe.Fori(0, 2) as i:
                for t in range(2):
                    w.multiply(pe, i * 2 + (NQ0 + t), t)
            for c in range(7):
                w.multiply(pe, TAIL0 + c, c % 2)
                pe.wait_ge(w.bank_free, w.evacuated(TAIL0 + c, 2))
                if c:
                    pe.wait_ge(feat_copied, 2 * c)
                for i in range(NB):
                    pe.transpose(ps[:, 3 + i // 4, (i % 4) * P:(i % 4 + 1) * P], tmpF[:, i * P:(i + 1) * P], m.c("ident"))
                pe.transpose(ps[0:DEC, 5, 0:P], tmpF[:, SEQ:TOK], m.c("ident")).then_inc(feat_turned, 1)


        @block.scalar
        def _(act):
            def evacuate(n, dst, func=ACT.Copy, scale=1.0):
                for t, cols, tile in w.tiles(act, n):
                    act.activation(dst[:, cols], tile, func, scale=scale).then_inc(w.bank_free, 1)

            w.round_hi(act, 0, 0, 0)
            with act.Fori(0, 4) as j:
                w.round_hi(act, j * 4 + 1, 1, j * 2)
                evacuate(j * 4, qT)
                w.round_hi(act, j * 4 + 2, 0, j * 2 + 1)
                evacuate(j * 4 + 1, kT, scale=SCALE)
                w.round_hi(act, j * 4 + 3, 1, j * 2 + 1)
                evacuate(j * 4 + 2, vT)
                w.round_hi(act, j * 4 + 4, 0, j * 2 + 2)
                evacuate(j * 4 + 3, m.mixT[:, bass.ds(j + 4, 1), :].rearrange("p a n -> p (a n)"), ACT.Silu)
                act.wait_ge(turned, j * 3 + 1)
                act.activation(v_tok[:], ps[:, 6:8, :].rearrange("p a (b f) -> p (a b) f", f=P), ACT.Copy).then_inc(tok_ready, 1)
                act.wait_ge(turned, j * 3 + 2)
                act.activation(kv_dec[:], ps[0:DEC, 3, 0:2 * P].rearrange("p (a f) -> p a f", f=P), ACT.Copy).then_inc(tok_ready, 1)
                act.wait_ge(turned, j * 3 + 3)
                for h in range(2):
                    act.activation(k_tok[:, :, h * HD:(h + 1) * HD],
                                   ps[:, 6:8, :].rearrange("p a (b f) -> p (a b) f", f=P)[:, :, h * HD:(h + 1) * HD],
                                   ACT.Copy, scale=m.c("kdec")[:, bass.ds(j * 2 + h, 1)]).then_inc(tok_ready, 1)
                dst = m.mixT[:, bass.ds(j, 1), :].rearrange("p a n -> p (a n)")
                for n, (cols, src) in enumerate(((slice(SEQ, TOK), ps[:, 5, 0:DEC]), (slice(0, 512), ps[:, 6, :]),
                                                 (slice(512, SEQ), ps[:, 7, :]))):
                    act.wait_ge(out_made, j * 3 + (n + 1))
                    act.activation(dst[:, cols], src, ACT.Copy).then_inc(out_copied, 1)
            with act.Fori(0, 2) as i:
                for t in range(2):
                    w.round_hi(act, i * 2 + (NQ0 + t + 1), 1 - t, i + (8 + (t + 1) // 2))
                    evacuate(i * 2 + (NQ0 + t), m.nqT[:, bass.ds(i * 2 + t, 1), :].rearrange("p a n -> p (a n)"), scale=SCALE)
            for c in range(7):
                if c < 6:
                    w.round_hi(act, TAIL0 + c + 1, (c + 1) % 2, (TAIL0 + c + 1) // 2)
                if c:
                    act.wait_ge(feat_turned, c)
                    if c in (3, 5):
                        act.wait_ge(k_spread, 2 * (c - 1))
                evacuate(TAIL0 + c, tmpF, ACT.Sigmoid if c == 6 else ACT.Copy)

        @block.vector
        def _(dve):
            banks = ps[:, 3:6, 0:TN]
            tri = lambda a: a.rearrange("p (a n) -> p a n", a=3)
            w.start_loads(dve)
            w.reduce_lo(dve, 0, 0, 0)
            with dve.Fori(0, 4) as j:
                w.reduce_lo(dve, j * 4 + 1, 1, j * 2)
                w.reduce_lo(dve, j * 4 + 2, 0, j * 2 + 1)
                w.reduce_lo(dve, j * 4 + 3, 1, j * 2 + 1)
                for n, x in enumerate((qT, kT)):
                    dve.wait_ge(swapped, j * 2 + (n + 1))
                    if n:
                        dve.wait_ge(roped, j * 4 + 2)
                    dve.tensor_tensor(tri(rope_tmp[:]), banks, tri(m.c("sin")), ALU.mult).then_inc(swap_read, 1)
                    dve.tensor_tensor(x[:], x[:], m.c("cos"), ALU.mult).then_inc(roped, 1)
                    dve.wait_ge(swap_read, j * 2 + (n + 1))
                    dve.wait_ge(roped, j * 4 + (2 * n + 1))
                    dve.tensor_tensor(x[:], x[:], rope_tmp[:], ALU.add).then_inc(roped, 1)
                w.reduce_lo(dve, j * 4 + 4, 0, j * 2 + 2)
                dve.wait_ge(tok_ready, j * 4 + 2)
                dve.tensor_tensor(v_diag[:], kv_dec[:, 1:2, :].broadcast_to([DEC, DEC, P]),
                                  m.c("ident")[0:DEC, 0:DEC].unsqueeze(2).broadcast_to([DEC, DEC, P]),
                                  ALU.mult).then_inc(diag_made, 1)
                dve.tensor_tensor(qd[:].rearrange("p (b n) -> p b n", n=P), qT[:, 0:SEQ].rearrange("p (b n) -> p b n", n=P),
                                  m.c("qdec")[:, bass.ds(j * P, P)].unsqueeze(1).broadcast_to([P, NB, P]),
                                  ALU.mult).then_inc(q_decayed, 1)
                dve.wait_ge(state_loaded, j * 32 + 32)
                dve.wait_ge(outer_made, j + 1)
                for h in range(2):
                    rows = slice(h * HD, (h + 1) * HD)
                    dve.scalar_tensor_tensor(s_new[rows], s_in[rows], m.c("gamma")[rows, bass.ds(j, 1)],
                                             ps[rows, 4:6, :].rearrange("p a (b f) -> p (a b) f", f=P)[:, :, rows],
                                             ALU.mult, ALU.add).then_inc(dec_state, 1)
                for i in range(NB):
                    kv = ps[:, 6 + i // 4, (i % 4) * P:(i % 4 + 1) * P]
                    if i % 4 == 0:
                        dve.wait_ge(kv_made, j * 2 + (i // 4 + 1))
                    if i == 0:
                        dve.tensor_copy(states[:, 0, :], kv).then_inc(state_made, 1)
                    else:
                        dve.wait_ge(state_made, j * 8 + i)
                        dve.scalar_tensor_tensor(states[:, i, :], states[:, i - 1, :], m.c("cdec")[:, bass.ds(j, 1)],
                                                 kv, ALU.mult, ALU.add).then_inc(state_made, 1)
                for i in range(NB):
                    dve.wait_ge(scores_made, j * 8 + (i + 1))
                    dve.tensor_tensor(aT[i % 2][:], ps[:, 3 - 2 * (i % 2):5 - 2 * (i % 2), 0:P],
                                      m.c("inner")[:, bass.ds(j * (2 * P), 2 * P)].rearrange("p (a n) -> p a n", n=P),
                                      ALU.mult).then_inc(scores_masked, 1)
            with dve.Fori(0, 2) as i:
                for t in range(2):
                    w.reduce_lo(dve, i * 2 + (NQ0 + t + 1), 1 - t, i + (8 + (t + 1) // 2))
            dve.wait_ge(state_stored, 64 * 4)
            toks = [m.ck_tok, m.cv_tok, m.k_stage, m.sv_tok, m.k_stage, m.wv_tok]
            for c in range(7):
                if c < 6:
                    w.reduce_lo(dve, TAIL0 + c + 1, (c + 1) % 2, (TAIL0 + c + 1) // 2)
                if c in (2, 4):
                    dve.wait_ge(w.bank_free, w.evacuated(TAIL0 + c, 2))
                    kd = m.selkT if c == 2 else m.winkT
                    for g in range(G):
                        for h in range(2):
                            dve.tensor_copy(kd[h * HD:(h + 1) * HD, g, :], tmpF[g * HD:(g + 1) * HD, :]).then_inc(k_spread, 1)
                dve.wait_ge(feat_turned, c + 1)
                src = ps[:, 3:5, :].rearrange("p a (b f) -> p (a b) f", f=P)
                if c == 6:
                    dve.tensor_copy(m.gate_tok[:, 0:NB, :], src[:, :, P - 24:P]).then_inc(feat_copied, 1)
                    dve.tensor_copy(m.gate_tok[0:DEC, NB, :], ps[0:DEC, 5, P - 24:P]).then_inc(feat_copied, 1)
                else:
                    if c == 4:
                        dve.wait_ge(sk_stored, 32)
                    dve.tensor_copy(toks[c][:, 0:NB, :], src).then_inc(feat_copied, 1)
                    dve.tensor_copy(toks[c][0:DEC, NB, :], ps[0:DEC, 5, 0:P]).then_inc(feat_copied, 1)

        @block.gpsimd
        def _(pool):
            with pool.Fori(0, 4) as j:
                pool.wait_ge(out_copied, j * 3 + 3)
                pool.sem_inc(pool_past, 1)
                for h in range(2):
                    rows = slice(h * HD, (h + 1) * HD)
                    pool.dma_start(s_in[rows], s_src[bass.ds(j * 2 + h, 1)].rearrange("h d b e -> (h d) b e")).then_inc(state_loaded, 16)
                pool.wait_ge(dec_state, j * 2 + 2)
                pool.sem_inc(pool_past, 1)
                for h in range(2):
                    rows = slice(h * HD, (h + 1) * HD)
                    pool.dma_start(s_dst[bass.ds(j * 2 + h, 1)].rearrange("h d b e -> (h d) b e"), s_new[rows]).then_inc(state_stored, 16)
                pool.wait_ge(state_made, j * 8 + 8)
                pool.sem_inc(pool_past, 1)
                for h in range(2):
                    rows = slice(h * HD, (h + 1) * HD)
                    pool.dma_start(p_dst[bass.ds(j * 2 + h, 1)].rearrange("h d e -> (h d) e"), states[rows, NB - 1, rows]).then_inc(state_stored, 16)
                pool.wait_ge(state_stored, j * 64 + 64)
                pool.sem_inc(pool_past, 1)
            outs = [(m.ck_tok, "cmp_k"), (m.cv_tok, "cmp_v"), (m.k_stage, "sel_k"), (m.sv_tok, "sel_v"),
                    (m.k_stage, "win_k"), (m.wv_tok, "win_v")]
            for c, (tile, name) in enumerate(outs):
                pool.wait_ge(feat_copied, 2 * c + 2)
                stored = sk_stored if c == 2 else rows_stored
                first = 0 if c < 4 else NB - WIN // P
                pool.dma_start(io[name + "_prompt"][0, 0].rearrange("(t p) g d -> p t (g d)", p=P),
                               tile[:, first:NB, :]).then_inc(stored, 16)
                row = 0 if c < 4 else WIN - 1
                pool.dma_start(io[name + "_sample"][0, :, row].rearrange("b g d -> b (g d)"),
                               tile[0:DEC, NB, :]).then_inc(stored, 16)
            pool.wait_ge(rows_stored, 16 * 10)
            pool.wait_ge(sk_stored, 32)


def load_pages(eng, table, first, count, cache, slab_page, sem):
    with eng.Fori(0, count // 4) as i:
        pages = [eng.value_load(table[0:1, bass.ds(i * 4 + (first + k), 1)], min_val=0, max_val=159) for k in range(4)]
        for k, page in enumerate(pages):
            eng.dma_start(slab_page(i, k), cache[bass.ds(page, 1)].rearrange("a t g d -> t a (g d)")).then_inc(sem, 16)


def stage_decode(nc, m, ps, io):
    with Stage(nc, "dec") as ctx:
        s = ctx.semaphore
        table_loaded, const_loaded = s("table_loaded"), s("const_loaded")
        gates_out, gates_in = s("gates_out"), s("gates_in")
        k_loaded, v_loaded = [s("k_loaded0"), s("k_loaded1")], [s("v_loaded0"), s("v_loaded1")]
        k_pool_loaded, v_pool_loaded = [s("k_pool_loaded0"), s("k_pool_loaded1")], [s("v_pool_loaded0"), s("v_pool_loaded1")]
        cleared, q_ready = s("cleared"), s("q_ready")
        k_turned, k_copied, k_used = s("k_turned"), s("k_copied"), s("k_used")
        cmp_scores, cmp_exp, cmp_dve = s("cmp_scores"), s("cmp_exp"), s("cmp_dve")
        importance, scores_done, new_scores = s("importance"), s("scores_done"), s("new_scores")
        soft_dve, soft_exp, win_out = s("soft_dve"), s("soft_exp"), s("win_out")
        p_turned, p_copied, v_used, out_done, placed = s("p_turned"), s("p_copied"), s("v_used"), s("out_done"), s("placed")

        A = m.A
        kpages = [m.place(f"dec_k{i}", [P, 20, P], F32, A + 10240 * i) for i in range(2)]
        vpages = [m.place(f"dec_v{i}", [P, 20, P], F32, A + 20480 + 10240 * i) for i in range(2)]
        kT = m.place("dec_kT", [P, 5, 512], F32, A + 40960)
        p = m.place("dec_p", [ROWS, PAST + 1 + WIN + 1], F32, A + 51200)
        pc = m.place("dec_p_cmp", [ROWS, 4 * P], F32, A + 61472)
        pT = m.place("dec_pT", [P, 24, ROWS], F32, A + 63520)
        dc = m.place("dec_const", [ROWS, DW], F32, m.ring)
        o = m.ring + 6432
        qz = m.place("dec_q_by_batch", [P, DEC, ROWS], F32, o)
        gt = m.place("dec_rank_gt", [ROWS, NBLK, NBLK], F32, o + 2048)
        eq = m.place("dec_rank_eq", [ROWS, NBLK, NBLK], F32, o + 6144)
        o += 10240
        qc = m.place("dec_q_cmp", [HD, DEC, NH], F32, o)
        knew = m.place("dec_k_new", [P, 2, DEC], F32, o + 256)
        gates = m.place("dec_gates", [ROWS, 4], F32, o + 320)
        pn = m.place("dec_p_new", [ROWS, 2, DEC], F32, o + 352)
        pnT = m.place("dec_p_newT", [DEC, 2, ROWS], F32, o + 416)
        halves = m.place("dec_p_halves", [ROWS, 256], F32, o + 928)
        imp = m.place("dec_importance", [ROWS, 4, NBLK], F32, o + 1952)
        table = m.place("dec_page_table", [1, DEC * NPG], I32, o + 2464)
        col = m.place("dec_columns", [ROWS, 16], F32, o + 2976)
        scratch = nc.dram_tensor("gate_rows", [DEC, NH * 3], F32, kind="Internal").ap()

        def take(i):
            lo, hi = DO[i]
            return dc[:, lo:hi]

        block = ctx.enter_context(nc.Block())

        def page_loads(eng, first, q):
            eng.wait_ge(table_loaded, 16)
            for loaded, slabs, used, name in ((k_loaded if q else k_pool_loaded, kpages, k_turned, "k"),
                                              (v_loaded if q else v_pool_loaded, vpages, v_used, "v")):
                for b in range(DEC):
                    if b >= 2:
                        eng.wait_ge(used, 5 * (b - 1) if name == "k" else b - 1)
                    slab = slabs[b % 2]
                    load_pages(eng, table, b * NPG + first, 8, io[f"cache_sel_{name}"][0],
                               lambda i, k: slab[:, bass.ds(i * 4 + (first + k), 1), :], loaded[b % 2])
                    if q:
                        eng.dma_start(slab[:, NPG:20, :], io[f"cache_win_{name}"][0, b].rearrange("(j t) g d -> t j (g d)", t=P)).then_inc(loaded[b % 2], 16)

        @block.sync
        def _(sp):
            sp.dma_start(table[:], io["page_table"].rearrange("(a b) n -> a (b n)", a=1)).then_inc(table_loaded, 16)
            sp.dma_start(dc[:], io["dec_const"]).then_inc(const_loaded, 16)
            sp.dma_start(scratch, m.gate_tok[0:DEC, NB, :]).then_inc(gates_out, 16)
            sp.wait_ge(gates_out, 16)
            sp.dma_start(gates[:, 0:3], scratch.rearrange("b (h c) -> (b h) c", c=3)).then_inc(gates_in, 16)
            page_loads(sp, 0, True)

        @block.gpsimd
        def _(pool):
            page_loads(pool, 8, False)

        @block.tensor
        def _(pe):
            pe.wait_ge(q_ready, 20)
            pe.matmul(ps[0:ROWS, 7, :], qc[:].rearrange("p b h -> p (b h)"), m.kcsT[:], start=True, stop=True).then_inc(cmp_scores, 1)

            def score(n):
                b, c = divmod(n, 5)
                pe.wait_ge(k_copied, n + 1)
                pe.matmul(ps[0:ROWS, c, :], qz[:, b, :], kT[:, c, :], start=(b == 0), stop=(b == DEC - 1)).then_inc(k_used, 1)

            for n in range(5 * DEC):
                b, c = divmod(n, 5)
                if c == 0:
                    pe.wait_ge(k_loaded[b % 2], 16 * 9 * (b // 2 + 1))
                    pe.wait_ge(k_pool_loaded[b % 2], 16 * 8 * (b // 2 + 1))
                if n >= 2:
                    pe.wait_ge(k_copied, n - 1)
                for i in range(4):
                    last = pe.transpose(ps[:, 5 + n % 2, i * P:(i + 1) * P], kpages[b % 2][:, 4 * c + i, :], m.c("ident"))
                last.then_inc(k_turned, 1)
                if n:
                    score(n - 1)
                if n == 20:
                    pe.wait_ge(cmp_dve, 6)
                    pe.wait_ge(const_loaded, 16)
                    pe.matmul(ps[0:ROWS, 7, 0:NBLK], take("headrows"), imp[:, 0, :], start=True, stop=True).then_inc(importance, 1)
            score(5 * DEC - 1)
            pe.wait_ge(cmp_dve, 7)
            for w in range(2):
                for b in range(DEC):
                    last = pe.matmul(ps[0:ROWS, 7, w:w + 1], qz[:, b, :], knew[:, w, b:b + 1], start=(b == 0), stop=(b == DEC - 1))
            last.then_inc(new_scores, 1)
            pe.wait_ge(soft_dve, 15)
            for i in range(24):
                src = pc[:, (i - 20) * P:(i - 19) * P] if i >= 20 else p[:, i * P + (i >= NPG):(i + 1) * P + (i >= NPG)]
                last = pe.transpose(ps[:, i // 8, (i % 8) * ROWS:(i % 8 + 1) * ROWS], src, m.c("ident")[0:ROWS, 0:ROWS])
                if i % 8 == 7:
                    last.then_inc(p_turned, 1)
            for w in range(2):
                last = pe.transpose(ps[0:DEC, 3, w * ROWS:(w + 1) * ROWS], pn[:, w, :], m.c("ident")[0:ROWS, 0:ROWS])
            last.then_inc(p_turned, 1)
            pe.wait_ge(p_copied, 4)
            out = ps[:, 4, 0:ROWS]
            for c in range(4):
                pe.matmul(out, m.vcs[:, c, :], pT[:, 20 + c, :], start=(c == 0), stop=False, skip_group_check=True)
            for w, v in enumerate((m.sv_tok, m.wv_tok)):
                pe.matmul(out, v[0:DEC, NB, :], pnT[:, w, :], start=False, stop=False, skip_group_check=True)
            for b in range(DEC):
                pe.wait_ge(v_loaded[b % 2], 16 * 9 * (b // 2 + 1))
                pe.wait_ge(v_pool_loaded[b % 2], 16 * 8 * (b // 2 + 1))
                cols = slice(b * NH, (b + 1) * NH)
                for i in range(20):
                    last = pe.matmul(ps[:, 4, cols], vpages[b % 2][:, i, :], pT[:, i, cols], start=False,
                                     stop=(b == DEC - 1 and i == 19), skip_group_check=True)
                last.then_inc(v_used, 1)

        @block.scalar
        def _(act):
            for n in range(5 * DEC):
                act.wait_ge(k_turned, n + 1)
                if n >= 5:
                    act.wait_ge(k_used, n - 4)
                act.activation(kT[:, n % 5, :], ps[:, 5 + n % 2, :], ACT.Copy).then_inc(k_copied, 1)
                if n == 3:
                    act.wait_ge(cmp_dve, 3)
                    act.activation(pc[:], pc[:], ACT.Exp, bias=col[:, 1:2], accum_out=col[:, 2:3]).then_inc(cmp_exp, 1)
            act.wait_ge(k_used, 5 * DEC)
            act.activation(p[:, PAST + 1:PAST + 1 + WIN], ps[0:ROWS, 4, :], ACT.Copy).then_inc(win_out, 1)
            act.wait_ge(soft_dve, 6)
            act.activation(p[:, 0:PAST + 1], p[:, 0:PAST + 1], ACT.Exp, bias=col[:, 6:7], accum_out=col[:, 8:9]).then_inc(soft_exp, 1)
            act.wait_ge(soft_dve, 8)
            act.activation(p[:, PAST + 1:], p[:, PAST + 1:], ACT.Exp, bias=col[:, 7:8], accum_out=col[:, 9:10]).then_inc(soft_exp, 1)
            for i in range(3):
                act.wait_ge(p_turned, i + 1)
                act.activation(pT[:, 8 * i:8 * i + 8, :], ps[:, i, :].rearrange("p (a b) -> p a b", b=ROWS), ACT.Copy).then_inc(p_copied, 1)
            act.wait_ge(p_turned, 4)
            act.activation(pnT[:], ps[0:DEC, 3, 0:2 * ROWS].rearrange("p (a b) -> p a b", b=ROWS), ACT.Copy).then_inc(p_copied, 1)

        @block.vector
        def _(dve):
            dve.memset(qz[:], 0.0).then_inc(cleared, 1)
            for h in range(NH):
                src = m.nqT[(h % 2) * HD:(h % 2 + 1) * HD, h // 2, SEQ:TOK]
                dve.tensor_copy(qc[:, :, h], src).then_inc(q_ready, 1)
            dve.wait_ge(cleared, 1)
            for h in range(NH):
                g = h // R
                src = m.nqT[(h % 2) * HD:(h % 2 + 1) * HD, h // 2, SEQ:TOK]
                flat = qz[g * HD:(g + 1) * HD].rearrange("p b r -> p (b r)")
                dve.tensor_copy(flat[:, h:h + (ROWS + NH) * (DEC - 1) + 1:ROWS + NH], src).then_inc(q_ready, 1)
            for w, kd in enumerate((m.selkT, m.winkT)):
                for g in range(G):
                    dve.tensor_copy(knew[g * HD:(g + 1) * HD, w, :], kd[g * HD:(g + 1) * HD, g, SEQ:TOK]).then_inc(q_ready, 1)
            dve.wait_ge(gates_in, 16)
            dve.wait_ge(const_loaded, 16)
            dve.wait_ge(cmp_scores, 1)
            step = Steps(cmp_dve)
            step.done(dve.tensor_tensor(pc[:], ps[0:ROWS, 7, :], take("ownblocks"), ALU.add))
            step.fence(dve)
            step.done(dve.tensor_reduce(col[:, 0:1], pc[:], AX.X, ALU.max))
            step.fence(dve)
            step.done(dve.tensor_scalar(col[:, 1:2], col[:, 0:1], -1.0, None, ALU.mult))
            dve.wait_ge(cmp_exp, 1)
            dve.reciprocal(col[:, 3:4], col[:, 2:3]).then_inc(soft_dve, 1)
            dve.wait_ge(soft_dve, 1)
            step.done(dve.tensor_scalar(pc[:], pc[:], col[:, 3:4], None, ALU.mult))
            step.fence(dve)
            step.done(dve.tensor_tensor(halves[:], pc[:, 0:256], pc[:, 256:512], ALU.add))
            step.fence(dve)
            step.done(dve.tensor_reduce(imp[:, 0, :].rearrange("p (h q) -> p h q", h=2),
                                        halves[:].rearrange("p (h b q g) -> p h q b g", h=2, b=4, g=G), AX.XY, ALU.add))
            dve.wait_ge(importance, 1)
            step.done(dve.tensor_copy(imp[:, 1, :], ps[0:ROWS, 7, 0:NBLK]))
            step.fence(dve)
            mine = imp[:, 1, :].unsqueeze(2).broadcast_to([ROWS, NBLK, NBLK])
            others = imp[:, 1, :].unsqueeze(1).broadcast_to([ROWS, NBLK, NBLK])
            step.done(dve.tensor_tensor(gt[:], others, mine, ALU.is_gt))
            step.done(dve.tensor_tensor(eq[:], others, mine, ALU.is_equal))
            step.fence(dve)
            step.done(dve.tensor_tensor(eq[:], eq[:], take("earlier").rearrange("p (i j) -> p i j", j=NBLK), ALU.mult))
            step.fence(dve)
            step.done(dve.tensor_tensor(gt[:], gt[:], eq[:], ALU.add))
            step.fence(dve)
            step.done(dve.tensor_reduce(imp[:, 2, :], gt[:], AX.X, ALU.add))
            step.fence(dve)
            step.done(dve.tensor_scalar(imp[:, 3, :], imp[:, 2, :], NSEL - 0.5, NEG, ALU.is_gt, ALU.mult))
            step.fence(dve)
            dve.wait_ge(k_used, 5 * DEC)
            soft = Steps(soft_dve)
            soft.n = 1
            soft.done(dve.tensor_tensor(p[:, 0:PAST].rearrange("p (q h t) -> p q h t", q=NPG, h=2),
                                        ps[0:ROWS, 0:4, :].rearrange("p a (q h t) -> p (a q) h t", q=4, h=2),
                                        imp[:, 3, :].rearrange("p (h q) -> p q h", h=2).unsqueeze(3).broadcast_to([ROWS, NPG, 2, CB]),
                                        ALU.add))
            dve.wait_ge(new_scores, 1)
            soft.done(dve.tensor_copy(p[:, PAST:PAST + 1 + WIN + 1:WIN + 1], ps[0:ROWS, 7, 0:2]))
            dve.wait_ge(win_out, 1)
            soft.done(dve.memset(p[:, PAST + 1:PAST + 2], NEG))
            soft.fence(dve)
            soft.done(dve.tensor_reduce(col[:, 4:5], p[:, 0:PAST + 1], AX.X, ALU.max))
            soft.fence(dve)
            soft.done(dve.tensor_scalar(col[:, 6:7], col[:, 4:5], -1.0, None, ALU.mult))
            soft.done(dve.tensor_reduce(col[:, 5:6], p[:, PAST + 1:], AX.X, ALU.max))
            soft.fence(dve)
            soft.done(dve.tensor_scalar(col[:, 7:8], col[:, 5:6], -1.0, None, ALU.mult))
            soft.done(dve.tensor_scalar(pc[:], pc[:], gates[:, 0:1], None, ALU.mult))
            for w, cols in enumerate((slice(0, PAST + 1), slice(PAST + 1, PAST + WIN + 2))):
                dve.wait_ge(soft_exp, w + 1)
                soft.done(dve.reciprocal(col[:, 10 + w:11 + w], col[:, 8 + w:9 + w]))
                soft.fence(dve)
                soft.done(dve.tensor_scalar(p[:, cols], p[:, cols], col[:, 10 + w:11 + w], gates[:, 1 + w:2 + w], ALU.mult, ALU.mult))
                soft.fence(dve)
                soft.done(dve.tensor_scalar(pn[:, w, :], take("ownrow"), p[:, cols.stop - 1:cols.stop], None, ALU.mult))
            dve.wait_ge(v_used, DEC)
            for h in range(NH):
                g = h // R
                dve.tensor_copy(m.mixT[(h % 2) * HD:(h % 2 + 1) * HD, 4 + h // 2, SEQ:TOK],
                                ps[g * HD:(g + 1) * HD, 4, h:ROWS:NH]).then_inc(placed, 1)


def stage_compress(nc, m, ps, io):
    with Stage(nc, "comp") as ctx:
        s = ctx.semaphore
        table_loaded = s("table_loaded")
        w1_loaded = [s("w1k_loaded"), s("w1v_loaded")]
        w2_loaded, pos_loaded = s("w2_loaded"), [s("posk_loaded"), s("posv_loaded")]
        pages_loaded = [s(f"pages_loaded{r}") for r in range(4)]
        pool_pages_loaded = [s(f"pool_pages_loaded{r}") for r in range(4)]
        prompt_in = s("prompt_in")
        hidden_made = s("hidden_made")
        hidden_in = s("hidden_in")
        bias_ready = s("bias_ready")
        gelu_dve, tanh_done = s("gelu_dve"), s("tanh_done")
        second_made = s("second_made")
        second_out = s("second_out")
        zeroed = s("zeroed")
        mean_made, centered, squared = s("mean_made"), s("centered"), s("squared")
        var_made, var_in, root_done, norm_dve = s("var_made"), s("var_in"), s("root_done"), s("norm_dve")

        A = m.A
        pages = [m.place("slab0_pages", [P, 73, P], F32, A), m.place("slab1_pages", [P, 64, P], F32, A + 73 * 512)]
        slab = [a[:].rearrange("p q (g d) -> p (q g) d", g=G) for a in pages]
        w1 = [m.place("w1_k", [P, HD, HD], F32, m.ring), m.place("w1_v", [P, HD, HD], F32, m.M + 4 * TOK * 4)]
        w2 = m.place("w2", [P, 2, HD], F32, m.ring + 16384)
        xh = m.place("hidden_x", [P, 144], F32, m.ring + 16896)
        uh = m.place("hidden_u", [P, 144], F32, m.ring + 17472)
        hid = m.place("hidden_gelu", [P, 144], F32, m.ring + 18048)
        table = m.place("page_table", [1, DEC * NPG], I32, m.ring + 18624)
        bias = m.small[:, 32:34]
        sq = [m.place(f"gn_square{i}", [P, TN], F32, m.stage + 1376 * i) for i in range(2)]
        rs = [m.place(f"gn_rstd{i}", [P, TN], F32, m.stage + 2752 + 1376 * i) for i in range(2)]
        caches = [io["cache_cmp_k"][0], io["cache_cmp_v"][0]]
        rounds = [(kv, r) for kv in range(2) for r in range(2)]
        units = [(j, t) for j in range(4) for t in range(3)]

        block = ctx.enter_context(nc.Block())

        @block.sync
        def _(sp):
            sp.dma_start(table[:], io["page_table"].rearrange("(a b) n -> a (b n)", a=1)).then_inc(table_loaded, 16)
            for h in range(2):
                sp.dma_start(w1[0][h * HD:(h + 1) * HD], io["cmp_w1_k"][0]).then_inc(w1_loaded[0], 16)
                for i, n in enumerate(("cmp_w2_k", "cmp_w2_v")):
                    sp.dma_start(w2[h * HD:(h + 1) * HD, i, :], io[n][0]).then_inc(w2_loaded, 16)
                sp.dma_start(slab[0][h * HD:(h + 1) * HD, 144, :], io["cmp_pos_k"][0]).then_inc(pos_loaded[0], 16)
            sp.wait_ge(table_loaded, 16)
            for n, (kv, r) in enumerate(rounds):
                if n >= 2:
                    sp.wait_ge(hidden_made, n - 1)
                if n == 2:
                    for h in range(2):
                        sp.dma_start(slab[0][h * HD:(h + 1) * HD, 144, :], io["cmp_pos_v"][0]).then_inc(pos_loaded[1], 16)
                load_pages(sp, table, r * 64, 32, caches[kv], lambda i, k: pages[r][:, bass.ds(i * 4 + k, 1), :], pages_loaded[n])

        @block.gpsimd
        def _(pool):
            def load(n):
                kv, r = rounds[n]
                load_pages(pool, table, r * 64 + 32, 32, caches[kv], lambda i, k: pages[r][:, bass.ds(i * 4 + (32 + k), 1), :], pool_pages_loaded[n])

            pool.memset(m.kcpT[:], 0.0).then_inc(zeroed, 1)
            pool.memset(m.vcp[:], 0.0).then_inc(zeroed, 1)
            pool.tensor_copy(slab[0][:, 128:144, :], m.ck_tok[:, 0:NB, :].rearrange("p b (g d) -> p (b g) d", g=G)).then_inc(prompt_in, 1)
            pool.wait_ge(table_loaded, 16)
            load(0)
            load(1)
            pool.wait_ge(norm_dve, 4 * len(units))
            for h in range(2):
                pool.dma_start(w1[1][h * HD:(h + 1) * HD], io["cmp_w1_v"][0]).then_inc(w1_loaded[1], 16)
            pool.wait_ge(hidden_made, 1)
            pool.tensor_copy(slab[0][:, 128:144, :], m.cv_tok[:, 0:NB, :].rearrange("p b (g d) -> p (b g) d", g=G)).then_inc(prompt_in, 1)

            load(2)
            pool.wait_ge(hidden_made, 2)
            load(3)

        @block.tensor
        def _(pe):
            def mean(u):
                j, t = units[u]
                if u >= 2:
                    pe.wait_ge(centered, u - 1)
                pe.matmul(ps[:, u % 2, 0:TN], m.c("headmean"), m.mixT[:, j, t * TN:(t + 1) * TN],
                          start=True, stop=True).then_inc(mean_made, 1)

            mean(0)
            for u in range(len(units)):
                if u + 1 < len(units):
                    mean(u + 1)
                pe.wait_ge(squared, u + 1)
                if u >= 2:
                    pe.wait_ge(var_in, u - 1)
                pe.matmul(ps[:, 2 + u % 2, 0:TN], m.c("headmean"), sq[u % 2][:], start=True, stop=True).then_inc(var_made, 1)
            pe.wait_ge(w2_loaded, 64)
            for n, (kv, r) in enumerate(rounds):
                width = 128 if r else 145
                if r == 0:
                    pe.wait_ge(w1_loaded[kv], 32)
                    pe.wait_ge(pos_loaded[kv], 32)
                    pe.wait_ge(prompt_in, kv + 1)
                pe.wait_ge(pages_loaded[n], 16 * 32)
                pe.wait_ge(pool_pages_loaded[n], 16 * 32)
                if n >= 2:
                    pe.wait_ge(hidden_in, n - 1)
                for d in range(HD):
                    for h in range(2):
                        rows = slice(h * HD, (h + 1) * HD)
                        last = pe.matmul(ps[rows, 4 + n % 2, 0:width], w1[kv][rows, d, :], slab[r][rows, 0:width, d],
                                         start=(d == 0), stop=(d == HD - 1))
                last.then_inc(hidden_made, 1)
                pe.wait_ge(gelu_dve, 4 * (n + 1))
                if n:
                    pe.wait_ge(second_out, (6, 8, 12)[n - 1])
                if kv == 0:
                    for h in range(2):
                        rows = slice(h * HD, (h + 1) * HD)
                        w = 128 if r else 144
                        last = pe.matmul(ps[0:HD, 6 + h, 0:w], w2[rows, 0, :], hid[rows, 0:w], start=True, stop=True)
                else:
                    for h in range(2):
                        rows = slice(h * HD, (h + 1) * HD)
                        last = pe.matmul(ps[:, 6 + h, 0:HD], hid[rows, 0:128], w2[rows, 1, :], start=True, stop=True)
                        if r == 0:
                            for g in range(G):
                                last = pe.matmul(ps[32 * h:32 * h + NB, 6 + h, HD * (1 + g):HD * (2 + g)], hid[rows, 128 + g:144:2],
                                                 w2[rows, 1, :], start=True, stop=True)
                last.then_inc(second_made, 1)

        @block.scalar
        def _(act):
            for u in range(len(units)):
                j, t = units[u]
                act.wait_ge(centered, u + 1)
                if u >= 2:
                    act.wait_ge(var_made, u - 1)
                act.activation(sq[u % 2][:], m.mixT[:, j, t * TN:(t + 1) * TN], ACT.Square).then_inc(squared, 1)
                act.wait_ge(var_in, u + 1)
                act.activation(rs[u % 2][:], rs[u % 2][:], ACT.Sqrt).then_inc(root_done, 1)
            act.wait_ge(zeroed, 2)
            for n, (kv, r) in enumerate(rounds):
                w = 128 if r else 144
                act.wait_ge(bias_ready, kv + 1)
                act.wait_ge(hidden_made, n + 1)
                if n:
                    act.wait_ge(gelu_dve, 4 * n)
                act.activation(xh[:, 0:w], ps[:, 4 + n % 2, 0:w], ACT.Identity, bias=bias[:, kv:kv + 1]).then_inc(hidden_in, 1)
                act.wait_ge(gelu_dve, 4 * n + 3)
                act.activation(uh[:, 0:w], uh[:, 0:w], ACT.Tanh, scale=math.sqrt(2.0 / math.pi)).then_inc(tanh_done, 1)
                act.wait_ge(second_made, n + 1)
                for h in range(2):
                    src = ps[:, 6 + h, :]
                    if kv == 0:
                        act.activation(m.kcsT[0:HD, (2 * r + h) * P:(2 * r + h + 1) * P], src[0:HD, 0:128], ACT.Copy, scale=0.5).then_inc(second_out, 1)
                        if r == 0:
                            for b in range(2):
                                act.activation(m.kcpT[b * HD:(b + 1) * HD, :, 32 * h:32 * h + NB],
                                               src[0:HD, 128:144].rearrange("p (n g) -> p g n", g=G), ACT.Copy, scale=0.5).then_inc(second_out, 1)
                    else:
                        for b in range(2):
                            act.activation(m.vcs[:, 2 * r + h, b * HD:(b + 1) * HD], src[:, 0:HD], ACT.Copy, scale=0.5).then_inc(second_out, 1)
                        if r == 0:
                            act.activation(m.vcp[32 * h:32 * h + NB, :], src[32 * h:32 * h + NB, HD:3 * HD], ACT.Copy, scale=0.5).then_inc(second_out, 1)

        @block.vector
        def _(dve):
            for u in range(len(units)):
                j, t = units[u]
                cols = slice(t * TN, (t + 1) * TN)
                o = m.mixT[:, j, cols]
                dve.wait_ge(mean_made, u + 1)
                dve.tensor_tensor(o, o, ps[:, u % 2, 0:TN], ALU.subtract).then_inc(centered, 1)
                dve.tensor_scalar(m.mixT[:, 4 + j, cols], m.mixT[:, 4 + j, cols], m.lnT[:, 32 + j:33 + j], None, ALU.mult).then_inc(norm_dve, 1)
                dve.wait_ge(var_made, u + 1)
                dve.tensor_scalar(rs[u % 2][:], ps[:, 2 + u % 2, 0:TN], EPS, None, ALU.add).then_inc(var_in, 1)
                dve.wait_ge(root_done, u + 1)
                dve.reciprocal(rs[u % 2][:], rs[u % 2][:]).then_inc(norm_dve, 1)
                dve.wait_ge(norm_dve, 4 * u + 2)
                dve.tensor_tensor(o, o, rs[u % 2][:], ALU.mult).then_inc(norm_dve, 1)
                dve.wait_ge(norm_dve, 4 * u + 3)
                dve.tensor_tensor(o, o, m.mixT[:, 4 + j, cols], ALU.mult).then_inc(norm_dve, 1)
            for n, (kv, r) in enumerate(rounds):
                w = 128 if r else 144
                if r == 0:
                    dve.wait_ge(hidden_made, n + 1)
                    dve.tensor_copy(bias[:, kv:kv + 1], ps[:, 4 + n % 2, 144:145]).then_inc(bias_ready, 1)
                dve.wait_ge(hidden_in, n + 1)
                dve.tensor_tensor(uh[:, 0:w], xh[:, 0:w], xh[:, 0:w], ALU.mult).then_inc(gelu_dve, 1)
                dve.wait_ge(gelu_dve, 4 * n + 1)
                dve.tensor_scalar(uh[:, 0:w], uh[:, 0:w], 0.044715, 1.0, ALU.mult, ALU.add).then_inc(gelu_dve, 1)
                dve.wait_ge(gelu_dve, 4 * n + 2)
                dve.tensor_tensor(uh[:, 0:w], uh[:, 0:w], xh[:, 0:w], ALU.mult).then_inc(gelu_dve, 1)
                dve.wait_ge(tanh_done, n + 1)
                if n:
                    dve.wait_ge(second_made, n)
                dve.scalar_tensor_tensor(hid[:, 0:w], uh[:, 0:w], 1.0, xh[:, 0:w], ALU.add, ALU.mult).then_inc(gelu_dve, 1)


def stage_attend(nc, m, ps, io):
    with Stage(nc, "att") as ctx:
        s = ctx.semaphore
        casts, sel_scores, win_scores, maxima = s("casts"), s("sel_scores"), s("win_scores"), s("maxima")
        exps, coef, scaled = s("exps"), s("coef"), s("scaled")
        k_hi, k_lo, q_hi, q_lo, half_out = s("k_hi"), s("k_lo"), s("q_hi"), s("q_lo"), s("half_out")
        turned, copied = s("turned"), s("copied")
        cmp_turned, cmp_copied, out_made, out_copied = s("cmp_turned"), s("cmp_copied"), s("out_made"), s("out_copied")

        PW = SEQ + WIN + P + CP
        p = [m.place(f"att_p{i}", [P, PW], F32, m.ring + 6816 * i) for i in range(3)]
        pcm = [m.place(f"att_p_cmp{i}", [P, R, CP], F32, m.ring + 20448 + 640 * i) for i in range(2)]
        col = m.place("att_columns", [P, 3, 12], F32, m.ring + 21728)
        bias_bf = m.place("att_cmp_bias", [P, NB, CP], BF16, m.ring + 21888)
        q_split = [m.place(f"att_q_split{i}", [P, NH // 2, 2, P], F32R, m.A + 57344 + 4096 * i) for i in range(2)]
        half = m.place("att_out_half", [HD, 4, P], F32, m.A + 65536)
        tok = (NB + 1) * P * 4
        o = m.N + 8 * TOK * 4
        sel_hi = m.place("sel_kT_hi", [P, G, SEQ], F32R, o)
        win_hi = m.place("win_kT_hi", [P, G, SEQ], F32R, o + 4 * tok)
        sel_lo = m.place("sel_kT_lo", [P, G, TOK], F32R, m.N + 4 * TOK * 4)
        win_lo = m.place("win_kT_lo", [P, G, TOK], F32R, m.N + 6 * TOK * 4)
        pT = [m.place(f"att_pT{i}", [P, 13, R, P], F32, m.A + 26624 * i) for i in range(2)]
        pcT = [m.place(f"att_p_cmpT{i}", [CP, R, P], F32, m.A + 53248 + 2048 * i) for i in range(2)]
        steps = [(i, g, r) for i in range(NB) for g in range(G) for r in range(R)]
        KW = WIN // P + 1

        def window(i):
            return max(0, i - KW + 1), i + 1

        groups, first_group = [], []
        for k, (i, g, r) in enumerate(steps):
            n = i + 1 + min(i + 1, KW)
            first_group.append(len(groups))
            groups += [(k, a, min(a + 4, n)) for a in range(0, n, 4)]
        first_group.append(len(groups))

        def block_cols(i, a):
            return slice(a * P, (a + 1) * P) if a <= i else slice(SEQ + (a - i - 1) * P, SEQ + (a - i) * P)

        block = ctx.enter_context(nc.Block())

        @block.tensor
        def _(pe):
            def keys(bank, g, a, w, hi, lo, q):
                for n, k in enumerate((hi, lo)):
                    if w == P:
                        last = pe.matmul(ps[:, bank, 0:2 * P].rearrange("p (a n) -> p a n", n=P), q,
                                         k[:, g, a:a + P].unsqueeze(1).broadcast_to([P, 2, P]), start=(n == 0), stop=(n == 1))
                    else:
                        last = pe.matmul(ps[:, bank, 0:w], q, k[:, g, a:a + w], start=(n == 0), stop=(n == 1))
                return last

            def sel_keys(k):
                i, g, r = steps[k]
                h = g * R + r
                q = q_split[i % 2][:, h // 2, h % 2, :]
                if g == 0 and r == 0:
                    pe.wait_ge(q_lo, 2 * i + 2)
                if k:
                    pe.wait_ge(exps, 3 * k - 2)
                for a in range(0, (i + 1) * P, 512):
                    keys(a // 512, g, a, min(512, (i + 1) * P - a), sel_hi, sel_lo, q)
                pe.matmul(ps[:, i // 4, (i % 4) * P:(i % 4 + 1) * P], m.ident_bf[:], m.causal_bf[:], start=False, stop=True,
                          skip_group_check=True).then_inc(sel_scores, 1)

            def other_keys(k):
                i, g, r = steps[k]
                h = g * R + r
                q = q_split[i % 2][:, h // 2, h % 2, :]
                if k:
                    pe.wait_ge(exps, 3 * k)
                lo, hi = window(i)
                for a in range(lo, hi, 4):
                    keys(2 + (a - lo) // 4, g, a * P, min(hi - a, 4) * P, win_hi, win_lo, q)
                    if a == lo and i >= KW - 1:
                        pe.matmul(ps[:, 2, 0:P], m.ident_bf[:], m.winlow_bf[:], start=False, stop=True, skip_group_check=True)
                    if a + 4 >= hi:
                        at = hi - 1 - lo
                        pe.matmul(ps[:, 2 + at // 4, (at % 4) * P:(at % 4 + 1) * P], m.ident_bf[:], m.causal_bf[:],
                                  start=False, stop=True, skip_group_check=True)
                rows = slice((h % 2) * HD, (h % 2 + 1) * HD)
                pe.matmul(ps[:, 3, 256:256 + CP], m.nqT[rows, h // 2, i * P:(i + 1) * P], m.kcpT[rows, g, :],
                          start=(i < KW - 1), stop=True, skip_group_check=True)
                pe.matmul(ps[:, 3, 256:256 + CP], m.ident_bf[:], bias_bf[:, i, :], start=False, stop=True,
                          skip_group_check=True).then_inc(win_scores, 1)

            def turn(k):
                i, g, r = steps[k]
                pe.wait_ge(scaled, 3 * (k + 1))
                for n in range(first_group[k], first_group[k + 1]):
                    _, a, b = groups[n]
                    if n >= 2:
                        pe.wait_ge(copied, n - 1)
                    for x in range(a, b):
                        last = pe.transpose(ps[:, 4 + n % 2, (x - a) * P:(x - a + 1) * P], p[k % 3][:, block_cols(i, x)], m.c("ident"))
                    last.then_inc(turned, 1)
                if r == R - 1:
                    grp = k // R
                    if grp >= 2:
                        pe.wait_ge(out_copied, 2 * (grp - 1))
                    for x in range(R):
                        last = pe.transpose(ps[0:CP, 6 + grp % 2, x * P:(x + 1) * P], pcm[grp % 2][:, x, :], m.c("ident"))
                    last.then_inc(cmp_turned, 1)

            def output(grp):
                i, g, _ = steps[grp * R]
                n = i + 1 + min(i + 1, KW)
                lo, _ = window(i)
                pe.wait_ge(copied, first_group[(grp + 1) * R])
                pe.wait_ge(cmp_copied, grp + 1)
                rows = slice(g * HD, (g + 1) * HD)
                out = [ps[e * HD:(e + 1) * HD, 6 + grp % 2, :] for e in range(2)]
                pe.matmul(out[1], m.vcp[:, rows], pcT[grp % 2][:], start=True, stop=False)
                for x in range(n):
                    v = m.sv_tok[:, x, rows] if x <= i else m.wv_tok[:, lo + x - i - 1, rows]
                    last = pe.matmul(out[x % 2], v, pT[grp % 2][:, x, :, :], start=(x == 0), stop=(x >= n - 2))
                last.then_inc(out_made, 1)

            pe.wait_ge(casts, 1)
            pe.wait_ge(k_lo, 2)
            for k in range(len(steps) + 2):
                if k < len(steps):
                    sel_keys(k)
                if k >= 2:
                    turn(k - 2)
                if k < len(steps):
                    other_keys(k)
                if k % R == 3 and k > R:
                    output(k // R - 1)
            output(len(steps) // R - 1)

        @block.scalar
        def _(act):
            def split_q(i):
                for e in range(2):
                    rows = slice(e * HD, (e + 1) * HD)
                    act.activation(q_split[i % 2][rows, :, e, :], m.nqT[rows, :, i * P:(i + 1) * P], ACT.Copy).then_inc(q_hi, 1)

            act.activation(sel_hi[:], m.selkT[:, :, 0:SEQ], ACT.Copy).then_inc(k_hi, 1)
            act.activation(win_hi[:], m.winkT[:, :, 0:SEQ], ACT.Copy).then_inc(k_hi, 1)
            split_q(0)
            for k in range(len(steps) + 2):
                if k % 8 == 2 and k // 8 + 1 < NB:
                    split_q(k // 8 + 1)
                if k >= 2:
                    t = k - 2
                    for n in range(first_group[t], first_group[t + 1]):
                        _, a, b = groups[n]
                        act.wait_ge(turned, n + 1)
                        if t % R == 0 and t // R >= 2:
                            act.wait_ge(out_made, t // R - 1)
                        act.activation(pT[(t // R) % 2][:, a:b, t % R, :],
                                       ps[:, 4 + n % 2, 0:(b - a) * P].rearrange("p (a n) -> p a n", n=P), ACT.Copy).then_inc(copied, 1)
                    if t % R == R - 1:
                        grp = t // R
                        act.wait_ge(cmp_turned, grp + 1)
                        act.activation(pcT[grp % 2][:], ps[0:CP, 6 + grp % 2, :].rearrange("p (a n) -> p a n", n=P), ACT.Copy).then_inc(cmp_copied, 1)
                if k < len(steps):
                    i, g, r = steps[k]
                    grp = k // R
                    if k >= 3:
                        act.wait_ge(turned, first_group[k - 2])
                    if k >= 2 * R and r == 0:
                        act.wait_ge(cmp_turned, grp - 1)
                    c = col[:, k % 3, :]
                    act.wait_ge(maxima, 3 * k + 1)
                    w = (i + 1) * P
                    act.activation(p[k % 3][:, 0:w], ps[:, 0:2, :].rearrange("p a n -> p (a n)")[:, 0:w], ACT.Exp,
                                   bias=c[:, 1:2], accum_out=c[:, 4:5]).then_inc(exps, 1)
                    act.wait_ge(maxima, 3 * k + 3)
                    w = min(i + 1, KW) * P
                    act.activation(p[k % 3][:, SEQ:SEQ + w], ps[:, 2:4, :].rearrange("p a n -> p (a n)")[:, 0:w], ACT.Exp,
                                   bias=c[:, 2:3], accum_out=c[:, 5:6]).then_inc(exps, 1)
                    act.activation(pcm[grp % 2][:, r, :], ps[:, 3, 256:256 + CP], ACT.Exp, bias=c[:, 0:1],
                                   accum_out=c[:, 3:4]).then_inc(exps, 1)

        @block.vector
        def _(dve):
            def split_q(i):
                for e in range(2):
                    rows, other = slice(e * HD, (e + 1) * HD), slice((1 - e) * HD, (2 - e) * HD)
                    dve.wait_ge(q_hi, 2 * i + e + 1)
                    dve.tensor_tensor(q_split[i % 2][other, :, e, :], m.nqT[rows, :, i * P:(i + 1) * P],
                                      q_split[i % 2][rows, :, e, :].bitcast(F32), ALU.subtract).then_inc(q_lo, 1)

            def add_halves(grp):
                i, g, _ = steps[grp * R]
                dve.wait_ge(out_made, grp + 1)
                if grp:
                    dve.wait_ge(out_copied, 2 * grp)
                dve.tensor_copy(half[:], ps[HD:P, 6 + grp % 2, :].rearrange("p (a n) -> p a n", n=P)).then_inc(half_out, 1)
                dve.wait_ge(half_out, grp + 1)
                for e in range(2):
                    dve.tensor_tensor(m.mixT[e * HD:(e + 1) * HD, 4 + 2 * g:6 + 2 * g, i * P:(i + 1) * P],
                                      ps[0:HD, 6 + grp % 2, :].rearrange("p (a e n) -> p e a n", e=2, n=P)[:, e],
                                      half[:].rearrange("p (a e) n -> p e a n", e=2)[:, e], ALU.add).then_inc(out_copied, 1)

            dve.tensor_copy(bias_bf[:], m.c("cmpbias").rearrange("p (a n) -> p a n", n=CP)).then_inc(casts, 1)
            for n, (k, hi, lo) in enumerate(((m.selkT, sel_hi, sel_lo), (m.winkT, win_hi, win_lo))):
                dve.wait_ge(k_hi, n + 1)
                dve.tensor_tensor(lo[:, :, 0:SEQ], k[:, :, 0:SEQ], hi[:].bitcast(F32), ALU.subtract).then_inc(k_lo, 1)
            split_q(0)
            for k in range(len(steps) + 2):
                if k < len(steps):
                    i, g, r = steps[k]
                    c = col[:, k % 3, :]
                    dve.wait_ge(sel_scores, k + 1)
                    if k >= 3:
                        dve.wait_ge(scaled, 3 * (k - 2))
                    dve.tensor_reduce(c[:, 1:2], ps[:, 0:2, :].rearrange("p a n -> p (a n)")[:, 0:(i + 1) * P], AX.X, ALU.max, negate=True).then_inc(maxima, 1)
                if 1 <= k <= len(steps):
                    t = k - 1
                    i, g, r = steps[t]
                    h = g * R + r
                    c = col[:, t % 3, :]
                    dve.wait_ge(exps, 3 * (t + 1))
                    dve.reciprocal(c[:, 6:9], c[:, 3:6]).then_inc(coef, 1)
                    dve.wait_ge(coef, 2 * t + 1)
                    dve.tensor_tensor(c[:, 9:12], c[:, 6:9], m.gate_tok[:, i, 3 * h:3 * h + 3], ALU.mult).then_inc(coef, 1)
                    dve.wait_ge(coef, 2 * t + 2)
                    w = (i + 1) * P
                    dve.tensor_scalar(p[t % 3][:, 0:w], p[t % 3][:, 0:w], c[:, 10:11], None, ALU.mult).then_inc(scaled, 1)
                    w = min(i + 1, KW) * P
                    dve.tensor_scalar(p[t % 3][:, SEQ:SEQ + w], p[t % 3][:, SEQ:SEQ + w], c[:, 11:12], None, ALU.mult).then_inc(scaled, 1)
                    pc = pcm[(t // R) % 2][:, r, :]
                    dve.scalar_tensor_tensor(pc, pc, c[:, 9:10], m.c("cmpvalid")[:, i * CP:(i + 1) * CP], ALU.mult, ALU.mult).then_inc(scaled, 1)
                if k % 8 == 3 and k // 8 + 1 < NB:
                    split_q(k // 8 + 1)
                if k < len(steps):
                    i, g, r = steps[k]
                    c = col[:, k % 3, :]
                    dve.wait_ge(win_scores, k + 1)
                    dve.tensor_reduce(c[:, 2:3], ps[:, 2:4, :].rearrange("p a n -> p (a n)")[:, 0:min(i + 1, KW) * P], AX.X, ALU.max, negate=True).then_inc(maxima, 1)
                    dve.tensor_reduce(c[:, 0:1], ps[:, 3, 256:256 + CP], AX.X, ALU.max, negate=True).then_inc(maxima, 1)
                if k % R == 0 and k > R:
                    add_halves(k // R - 2)
            add_halves(len(steps) // R - 1)


def rstd_tiles(m, ps, bank, acc, rep, sums_in, spread, mean_in, root, ready):

    def pe_part(pe):
        for t in range(3):
            sums_in(pe, t)
            pe.matmul(ps[:, bank + t, 0:TN], m.c("ones"), acc[:, t * TN:(t + 1) * TN], start=True, stop=True).then_inc(spread, 1)

    def dve_part(dve):
        for t in range(3):
            dve.wait_ge(spread, t + 1)
            dve.tensor_scalar(rep[:, t * TN:(t + 1) * TN], ps[:, bank + t, 0:TN], 1.0 / D_MODEL, EPS, ALU.mult,
                              ALU.add).then_inc(mean_in, 1)
        for t in range(3):
            dve.wait_ge(root, t + 1)
            dve.reciprocal(rep[:, t * TN:(t + 1) * TN], rep[:, t * TN:(t + 1) * TN]).then_inc(ready, 1)

    def act_part(act):
        for t in range(3):
            act.wait_ge(mean_in, t + 1)
            act.activation(rep[:, t * TN:(t + 1) * TN], rep[:, t * TN:(t + 1) * TN], ACT.Sqrt).then_inc(root, 1)

    return pe_part, act_part, dve_part


def stage_mix(nc, m, ps, io, h_rows):
    with Stage(nc, "mix") as ctx:
        s = ctx.semaphore
        w = Stream(ctx, m, ps)
        mix_hi, mix_lo = s("mix_hi"), s("mix_lo")
        x_loaded, xs_loaded = s("x_loaded"), s("xs_loaded")
        squared, summed = s("squared"), s("summed")
        spread1, mean1, root1, ready1 = s("spread1"), s("mean1"), s("root1"), s("ready1")
        spread2, mean2, root2, ready2 = s("spread2"), s("mean2"), s("root2"), s("ready2")
        x_turned, normed, h_ready, h_squared, h_summed = s("x_turned"), s("normed"), s("h_ready"), s("h_squared"), s("h_summed")
        scaled, n_hi, n_lo, h_stored = s("scaled"), s("n_hi"), s("n_lo"), s("h_stored")

        hT = m.place("mixed_then_h", [P, KT, TOK], F32, m.M)
        x = m.place("x_rows_again", [P, NB, D_MODEL], F32, m.N)
        xs = m.place("x_decoded_again", [DEC, D_MODEL], F32, m.N + 32768)
        o = m.N + 36864
        acc = m.place("square_sums", [P, TOK], F32, o)
        rep = m.place("rstd_everywhere", [P, TOK], F32, o + 4128)
        sq = [m.place(f"squares{i}", [P, TN], F32, o + 8256 + 1376 * i) for i in range(3)]
        acc2 = m.place("h_square_sums", [P, TOK], F32, o + 12384)
        tmp = [m.place(f"normed_h{i}", [P, 512], F32, o + 16512 + 2048 * i) for i in range(2)]
        nrm = [m.place(f"h_normed{i}", [P, TOK], F32, m.N + 4128 * i) for i in range(3)]
        src = io["w_o"][0].rearrange("(kt p) n -> p kt n", p=P)
        units = [(kt, h) for h in range(3) for kt in range(KT)]
        CH = KT

        def span(h):
            return (slice(0, 512), slice(512, 1024), slice(SEQ, TOK))[h]

        pe_rstd1, act_rstd1, dve_rstd1 = rstd_tiles(m, ps, 3, acc, rep, lambda pe, t: pe.wait_ge(summed, 3 * KT + 3),
                                                    spread1, mean1, root1, ready1)
        pe_rstd2, act_rstd2, dve_rstd2 = rstd_tiles(m, ps, 3, acc2, rep, lambda pe, t: pe.wait_ge(h_summed, len(units)),
                                                    spread2, mean2, root2, ready2)
        def add_h(dve, u):
            kt, h = units[u]
            cols = span(h)
            dve.wait_ge(h_squared, u + 1)
            if u:
                dve.wait_ge(h_summed, u)
            dve.tensor_tensor(acc2[:, cols], acc2[:, cols], tmp[u % 2][:, 0:cols.stop - cols.start], ALU.add).then_inc(h_summed, 1)

        block = ctx.enter_context(nc.Block())

        @block.sync
        def _(sp):
            sp.dma_start(x[:], io["x_prompt"][0].rearrange("(t p) d -> p t d", p=P)).then_inc(x_loaded, 16)
            sp.dma_start(xs[:], io["x_sample"][:, 0, :]).then_inc(xs_loaded, 16)
            with sp.Fori(0, CH // 2) as i:
                for t in range(2):
                    w.load(sp, i * 2 + t, t, src[:, :, bass.ds(i * (2 * P) + t * P, P)])
            for kt in range(KT):
                sp.wait_ge(h_ready, 2 * KT + kt + 1)
                sp.dma_start(h_rows[:, kt], hT[:, kt, :]).then_inc(h_stored, 16)
            sp.wait_ge(h_stored, 16 * KT)

        @block.tensor
        def _(pe):
            w.start(pe)
            pe.wait_ge(mix_lo, KT)
            with pe.Fori(0, CH // 2) as i:
                for t in range(2):
                    w.multiply(pe, i * 2 + t, t)
            pe_rstd1(pe)
            pe.wait_ge(x_loaded, 16)
            pe.wait_ge(xs_loaded, 16)
            for u, (kt, h) in enumerate(units):
                if u >= 2:
                    pe.wait_ge(h_ready, u - 1)
                if h < 2:
                    for i in range(4):
                        last = pe.transpose(ps[:, 6 + u % 2, i * P:(i + 1) * P], x[:, 4 * h + i, kt * P:(kt + 1) * P], m.c("ident"))
                else:
                    last = pe.transpose(ps[:, 6 + u % 2, 0:DEC], xs[:, kt * P:(kt + 1) * P], m.c("ident")[0:DEC, 0:DEC])
                last.then_inc(x_turned, 1)
            pe.wait_ge(ready1, 3)
            pe_rstd2(pe)

        @block.scalar
        def _(act):
            for kt in range(KT):
                act.activation(m.hi[:, kt, :], m.mixT[:, kt, :], ACT.Copy).then_inc(mix_hi, 1)
            w.round_hi(act, 0, 0, 0)

            def evacuate(n, kt):
                dst = hT[:, kt, :] if isinstance(kt, int) else hT[:, bass.ds(kt, 1), :].rearrange("p a n -> p (a n)")
                for t, cols, tile in w.tiles(act, n):
                    act.wait_ge(summed, n * 3 + (t + 1))
                    act.activation(sq[t][:], tile, ACT.Square).then_inc(squared, 1)
                    act.activation(dst[:, cols], tile, ACT.Copy).then_inc(w.bank_free, 1)

            act.wait_ge(mix_lo, KT)
            with act.Fori(0, CH // 2 - 1) as i:
                for t in range(2):
                    w.round_hi(act, i * 2 + (t + 1), 1 - t, i + t)
                    evacuate(i * 2 + t, i * 2 + t)
            w.round_hi(act, CH - 1, 1, CH // 2 - 1)
            evacuate(CH - 2, CH - 2)
            evacuate(CH - 1, CH - 1)
            act_rstd1(act)
            for u, (kt, h) in enumerate(units):
                cols = span(h)
                act.wait_ge(h_ready, u + 1)
                if u >= 2:
                    act.wait_ge(h_summed, u - 1)
                act.activation(tmp[u % 2][:, 0:cols.stop - cols.start], hT[:, kt, cols], ACT.Square).then_inc(h_squared, 1)
            act_rstd2(act)
            for kt in range(KT):
                act.wait_ge(scaled, kt + 1)
                act.activation(m.hi[:, kt, :], nrm[kt % 3][:], ACT.Copy).then_inc(n_hi, 1)

        @block.vector
        def _(dve):
            w.start_loads(dve)
            dve.sem_inc(summed, 3)
            for kt in range(KT):
                dve.wait_ge(mix_hi, kt + 1)
                dve.tensor_tensor(m.lo[:, kt, :], m.mixT[:, kt, :], m.hi[:, kt, :].bitcast(F32), ALU.subtract).then_inc(mix_lo, 1)
            w.reduce_lo(dve, 0, 0, 0)

            def add_squares(n):
                for t in range(3):
                    cols = slice(t * TN, (t + 1) * TN)
                    dve.wait_ge(squared, n * 3 + (t + 1))
                    dve.wait_ge(summed, n * 3 + (t + 1))
                    dve.tensor_tensor(acc[:, cols], acc[:, cols], sq[t][:], ALU.add).then_inc(summed, 1)

            dve.memset(acc[:], 0.0).then_inc(normed, 1)
            dve.memset(acc2[:], 0.0).then_inc(normed, 1)
            dve.wait_ge(normed, 2)
            with dve.Fori(0, CH // 2 - 1) as i:
                for t in range(2):
                    w.reduce_lo(dve, i * 2 + (t + 1), 1 - t, i + t)
                    add_squares(i * 2 + t)
            w.reduce_lo(dve, CH - 1, 1, CH // 2 - 1)
            add_squares(CH - 2)
            add_squares(CH - 1)
            dve_rstd1(dve)
            dve.wait_ge(ready1, 3)
            dve.wait_ge(w.bank_free, 3 + 3 * CH)
            for u, (kt, h) in enumerate(units):
                cols = span(h)
                wd = cols.stop - cols.start
                dve.scalar_tensor_tensor(hT[:, kt, cols], hT[:, kt, cols], m.lnT[:, 8 + kt:9 + kt], rep[:, cols],
                                         ALU.mult, ALU.mult).then_inc(normed, 1)
                dve.wait_ge(normed, 3 + u)
                dve.wait_ge(x_turned, u + 1)
                dve.tensor_tensor(hT[:, kt, cols], hT[:, kt, cols], ps[:, 6 + u % 2, 0:wd], ALU.add).then_inc(h_ready, 1)
                if u:
                    add_h(dve, u - 1)
            add_h(dve, len(units) - 1)
            dve_rstd2(dve)
            dve.wait_ge(ready2, 3)
            for kt in range(KT + 1):
                if kt < KT:
                    if kt >= 3:
                        dve.wait_ge(n_lo, kt - 2)
                    dve.scalar_tensor_tensor(nrm[kt % 3][:], hT[:, kt, :], m.lnT[:, 16 + kt:17 + kt], rep[:],
                                             ALU.mult, ALU.mult).then_inc(scaled, 1)
                if kt:
                    dve.wait_ge(n_hi, kt)
                    dve.wait_ge(scaled, kt)
                    dve.tensor_tensor(m.lo[:, kt - 1, :], nrm[(kt - 1) % 3][:], m.hi[:, kt - 1, :].bitcast(F32), ALU.subtract).then_inc(n_lo, 1)


def stage_mlp(nc, m, ps, io):
    with Stage(nc, "mlp") as ctx:
        s = ctx.semaphore
        w = Stream(ctx, m, ps)
        cleared, squared, f_hi, f_lo = s("cleared"), s("squared"), s("f_hi"), s("f_lo")
        T8 = KT * TOK * 4
        fhi = m.place("hidden_hi", [P, KT, TOK], F32R, m.M)
        flo = m.place("hidden_lo", [P, KT, TOK], F32R, m.A + 2 * T8)
        y = m.y_handle = m.place("mlp_out", [P, KT, TOK], F32, m.A + 3 * T8)
        assert m.A + 4 * T8 <= int(nc.sbuf_usable_end)
        r = [m.place(f"relu{i}", [P, TN], F32, m.tables + 1376 * i) for i in range(3)]
        f = [m.place(f"relu_squared{i}", [P, TN], F32, m.tables + 4128 + 1376 * i) for i in range(3)]
        up = io["w_up"][0].rearrange("(kt p) n -> p kt n", p=P)
        down = io["w_down"][0].rearrange("(kt p) n -> p kt n", p=P)
        PAIRS = KT // 2
        block = ctx.enter_context(nc.Block())

        def quarters(eng, up_chunk, down_chunk):
            def quarter(q, last):
                with eng.Fori(0, PAIRS) as i:
                    for t in range(2):
                        up_chunk(q, i, t)
                with eng.Fori(0, PAIRS - last) as i:
                    for t in range(2):
                        down_chunk(q, i, t, False)
                if last:
                    for t in range(2):
                        down_chunk(q, PAIRS - 1, t, t == 1)

            with eng.Fori(0, QUARTERS - 1) as q:
                quarter(q, False)
            quarter(QUARTERS - 1, 1)

        def n_up(q, i, t):
            return q * 16 + (i * 2 + t)

        def n_down(q, i, t):
            return q * 16 + (i * 2 + (8 + t))

        def tile_of(buf, i, t, cols):
            return buf[:, bass.ds(i * 2 + t, 1), cols].rearrange("p a n -> p (a n)")

        @block.sync
        def _(sp):
            def load_up(q, i, t):
                w.load(sp, n_up(q, i, t), t, up[:, :, bass.ds(q * D_MODEL + i * (2 * P) + t * P, P)])

            def load_down(q, i, t, last):
                w.load(sp, n_down(q, i, t), t, down[:, bass.ds(q * KT, KT), bass.ds(i * (2 * P) + t * P, P)])

            quarters(sp, load_up, load_down)

        @block.tensor
        def _(pe):
            w.start(pe)

            def down_chunk(q, i, t, last):
                pe.wait_ge(f_lo, q * 24 + 27)
                w.multiply(pe, n_down(q, i, t), t, fhi, flo)

            quarters(pe, lambda q, i, t: w.multiply(pe, n_up(q, i, t), t), down_chunk)

        @block.scalar
        def _(act):
            w.round_hi(act, 0, 0, 0)

            def up_chunk(q, i, t):
                w.round_hi(act, n_up(q, i, t + 1), 1 - t, q * 8 + (i + t))
                for x in range(3):
                    cols = slice(x * TN, (x + 1) * TN)
                    done = q * 24 + (i * 6 + (3 * t + x + 1))
                    act.wait_ge(w.bank_free, q * 48 + (i * 6 + (3 * t + x + 4)))
                    act.wait_ge(f_lo, done)
                    act.activation(f[x][:], r[x][:], ACT.Square).then_inc(squared, 1)
                    act.wait_ge(squared, done)
                    act.activation(tile_of(fhi, i, t, cols), f[x][:], ACT.Copy).then_inc(f_hi, 1)

            def down_chunk(q, i, t, last):
                if not last:
                    w.round_hi(act, n_down(q, i, t + 1), 1 - t, q * 8 + (i + (4 + t)))

            quarters(act, up_chunk, down_chunk)

        @block.vector
        def _(dve):
            w.start_loads(dve)
            dve.memset(y[:], 0.0).then_inc(cleared, 1)
            dve.sem_inc(f_lo, 3)
            dve.wait_ge(cleared, 1)
            w.reduce_lo(dve, 0, 0, 0)

            def up_chunk(q, i, t):
                w.reduce_lo(dve, n_up(q, i, t + 1), 1 - t, q * 8 + (i + t))
                for x in range(4):
                    if x < 3:
                        dve.wait_ge(w.tile_done, q * 48 + (i * 6 + (3 * t + x + 7)))
                        dve.tensor_scalar(r[x][:], ps[:, x, 0:TN], 0.0, None, ALU.max).then_inc(w.bank_free, 1)
                    if x:
                        cols = slice((x - 1) * TN, x * TN)
                        dve.wait_ge(f_hi, q * 24 + (i * 6 + (3 * t + x)))
                        dve.tensor_tensor(tile_of(flo, i, t, cols), f[x - 1][:], tile_of(fhi, i, t, cols).bitcast(F32),
                                          ALU.subtract).then_inc(f_lo, 1)

            def down_chunk(q, i, t, last):
                if not last:
                    w.reduce_lo(dve, n_down(q, i, t + 1), 1 - t, q * 8 + (i + (4 + t)))
                for x, cols, tile in w.tiles(dve, n_down(q, i, t)):
                    dst = tile_of(y, i, t, cols)
                    dve.wait_ge(w.bank_free, q * 48 + (i * 6 + (3 * t + x + 25)))
                    dve.tensor_tensor(dst, dst, tile, ALU.add).then_inc(w.bank_free, 1)

            quarters(dve, up_chunk, down_chunk)


def stage_out(nc, m, ps, io, h_rows):
    with Stage(nc, "out") as ctx:
        s = ctx.semaphore
        h_loaded = [s("h_loaded0"), s("h_loaded1")]
        squared, summed, cleared = s("squared"), s("summed"), s("cleared")
        spread, mean, root, ready = s("spread"), s("mean"), s("root"), s("ready")
        normed, y_ready, turned, copied, stored = s("normed"), s("y_ready"), s("turned"), [s("copied_act"), s("copied_dve")], s("stored")
        T8 = KT * TOK * 4
        y = m.y_handle
        h = m.place("h_again", [P, KT, TOK], F32, m.M)
        acc = m.place("out_square_sums", [P, TOK], F32, m.A)
        rep = m.place("out_rstd", [P, TOK], F32, m.A + 4128)
        sq = [m.place(f"out_squares{i}", [P, TOK], F32, m.A + 8256 + 4128 * i) for i in range(2)]
        rows = m.place("y_rows", [P, NB, D_MODEL], F32, m.A + 16512)
        rows_dec = m.place("y_rows_decoded", [DEC, D_MODEL], F32, m.A + 16512 + 32768)
        pe_rstd, act_rstd, dve_rstd = rstd_tiles(m, ps, 0, acc, rep, lambda pe, t: pe.wait_ge(summed, KT), spread, mean, root, ready)
        units = [(b, c) for b in range(NB + 1) for c in range(2)]
        block = ctx.enter_context(nc.Block())

        @block.sync
        def _(sp):
            for i in range(2):
                sp.dma_start(h[:, 4 * i:4 * i + 4, :], h_rows[:, 4 * i:4 * i + 4]).then_inc(h_loaded[i], 16)
            for b in range(NB + 1):
                for e in range(2):
                    sp.wait_ge(copied[e], b + 1)
                if b < NB:
                    sp.dma_start(io["y_prompt"][0, b * P:(b + 1) * P, :], rows[:, b, :]).then_inc(stored, 16)
                else:
                    sp.dma_start(io["y_sample"][:, 0, :], rows_dec[:]).then_inc(stored, 16)
            sp.wait_ge(stored, 16 * (NB + 1))

        @block.scalar
        def _(act):
            for kt in range(KT):
                if kt >= 2:
                    act.wait_ge(summed, kt - 1)
                act.activation(sq[kt % 2][:], y[:, kt, :], ACT.Square).then_inc(squared, 1)
            act_rstd(act)
            for b in range(NB + 1):
                act.wait_ge(turned, 2 * b + 1)
                n = P if b < NB else DEC
                act.activation(rows[:, b, 0:512] if b < NB else rows_dec[:, 0:512], ps[0:n, 3 + (2 * b) % 4, :], ACT.Copy).then_inc(copied[0], 1)

        @block.vector
        def _(dve):
            dve.memset(acc[:], 0.0).then_inc(cleared, 1)
            dve.wait_ge(cleared, 1)
            for kt in range(KT):
                dve.wait_ge(squared, kt + 1)
                if kt:
                    dve.wait_ge(summed, kt)
                dve.tensor_tensor(acc[:], acc[:], sq[kt % 2][:], ALU.add).then_inc(summed, 1)
            dve_rstd(dve)
            dve.wait_ge(ready, 3)
            for kt in range(KT):
                dve.scalar_tensor_tensor(y[:, kt, :], y[:, kt, :], m.lnT[:, 24 + kt:25 + kt], rep[:], ALU.mult, ALU.mult).then_inc(normed, 1)
                dve.wait_ge(normed, kt + 1)
                if kt % 4 == 0:
                    dve.wait_ge(h_loaded[kt // 4], 16)
                dve.tensor_tensor(y[:, kt, :], y[:, kt, :], h[:, kt, :], ALU.add).then_inc(y_ready, 1)
            for b in range(NB + 1):
                dve.wait_ge(turned, 2 * b + 2)
                n = P if b < NB else DEC
                dve.tensor_copy(rows[:, b, 512:1024] if b < NB else rows_dec[:, 512:1024], ps[0:n, 3 + (2 * b + 1) % 4, :]).then_inc(copied[1], 1)

        @block.tensor
        def _(pe):
            pe_rstd(pe)
            for u, (b, c) in enumerate(units):
                pe.wait_ge(y_ready, 4 * c + 4)
                if u >= 4:
                    pe.wait_ge(copied[c], b - 1)
                cols = slice(b * P, (b + 1) * P) if b < NB else slice(SEQ, TOK)
                n = P if b < NB else DEC
                for i in range(4):
                    last = pe.transpose(ps[0:n, 3 + u % 4, i * P:(i + 1) * P], y[:, 4 * c + i, cols], m.c("ident"))
                last.then_inc(turned, 1)


def build(nc, io):
    m = Memory(nc)
    h_rows = nc.dram_tensor("h_features", [P, KT, TOK], F32, kind="Internal").ap()
    with ExitStack() as ctx:
        ps = ctx.enter_context(nc.psum_tensor("psum", [P, 8, 512], F32))
        stage_prepare(nc, m, ps, io)
        stage_project(nc, m, ps, io)
        stage_compress(nc, m, ps, io)
        stage_decode(nc, m, ps, io)
        stage_attend(nc, m, ps, io)
        stage_mix(nc, m, ps, io, h_rows)
        stage_mlp(nc, m, ps, io)
        stage_out(nc, m, ps, io, h_rows)


_INS = ["x_prompt", "x_sample", "state_ret", "cache_cmp_k", "cache_cmp_v", "cache_sel_k", "cache_sel_v",
        "cache_win_k", "cache_win_v", "page_table", "ln_pre_mix", "w_in", "ret_gn_w", "cmp_pos_k", "cmp_w1_k",
        "cmp_w2_k", "cmp_pos_v", "cmp_w1_v", "cmp_w2_v", "w_o", "ln_post_mix", "ln_pre_ffn", "w_up", "w_down",
        "ln_post_ffn"]
_ROWS_P, _ROWS_S = (1, 1, SEQ, G, HD), (1, DEC, 1, G, HD)
_OUTS = [("y_prompt", (1, SEQ, D_MODEL)), ("y_sample", (DEC, 1, D_MODEL)),
         ("ret_state_prompt", (1, 1, RH, HD, HD)),
         ("cmp_k_prompt", _ROWS_P), ("cmp_v_prompt", _ROWS_P), ("sel_k_prompt", _ROWS_P), ("sel_v_prompt", _ROWS_P),
         ("win_k_prompt", (1, 1, WIN, G, HD)), ("win_v_prompt", (1, 1, WIN, G, HD)),
         ("ret_state_sample", (1, DEC, RH, HD, HD)),
         ("cmp_k_sample", _ROWS_S), ("cmp_v_sample", _ROWS_S), ("sel_k_sample", _ROWS_S), ("sel_v_sample", _ROWS_S),
         ("win_k_sample", (1, DEC, WIN, G, HD)), ("win_v_sample", (1, DEC, WIN, G, HD))]


def kernel(**inputs):
    import numpy as _np
    import concourse.bacc as _bacc
    from concourse import mybir as _mybir
    from concourse.bass_utils import run_bass_kernel_spmd as _run

    nc = _bacc.Bacc("TRN2", target_bir_lowering=False, num_devices=1)
    arrays, io = {}, {}
    for name in _INS:
        a = _np.ascontiguousarray(inputs[name])
        arrays[f"in_{name}"] = a
        io[name] = nc.dram_tensor(f"in_{name}", a.shape, _mybir.dt.from_np(a.dtype), kind="ExternalInput").ap()
    arrays["in_const"], arrays["in_dec_const"] = constants()
    io["const"] = nc.dram_tensor("in_const", (P, CW), F32, kind="ExternalInput").ap()
    io["dec_const"] = nc.dram_tensor("in_dec_const", (ROWS, DW), F32, kind="ExternalInput").ap()
    for name, shape in _OUTS:
        io[name] = nc.dram_tensor(f"out_{name}", shape, F32, kind="ExternalOutput").ap()
    build(nc, io)
    r = _run(nc, [arrays], core_ids=[0])
    return tuple(r.results[0][f"out_{name}"] for name, _ in _OUTS)
```

```python
import math
from contextlib import ExitStack

import numpy as np

import concourse.bass as bass
from concourse import mybir

ALU = mybir.AluOpType
ACT = mybir.ActivationFunctionType
AX = mybir.AxisListType
F32 = mybir.dt.float32
F32R = mybir.dt.float32r
BF16 = mybir.dt.bfloat16
I32 = mybir.dt.int32

P = 128
D_MODEL, SEQ, DEC = 1024, 1024, 8
HD = 64
RH, NH, G, R = 8, 8, 2, 4
PAST, PAGE, WIN = 2048, 128, 512
D_FF = 4096
CB = 64
IN_W = 3352
EPS = 1e-6
NEG = -1e30
SCALE = HD ** -0.5
TOK = SEQ + DEC
TN = TOK // 3
KT = D_MODEL // P
NB = SEQ // P
NPG = PAST // PAGE
NBLK = PAST // CB
NSEL = 15
QUARTERS = 4
ROWS = DEC * NH

CP = 40

_COLS = [("ident", P), ("perm", P), ("headmean", P), ("ones", P), ("causal", P), ("winlow", P),
         ("cos", TOK), ("sin", TOK), ("inner", RH * P), ("qdec", 4 * P), ("kdec", RH), ("cdec", 4),
         ("gamma", 4), ("cmpbias", NB * CP), ("cmpvalid", NB * CP)]
_DEC_COLS = [("ownblocks", DEC * G * NBLK), ("ownrow", DEC), ("earlier", NBLK * NBLK), ("headrows", ROWS)]


def _places(columns):
    at, o = {}, 0
    for name, width in columns:
        at[name] = (o, o + width)
        o += width
    return at, o


CO, CW = _places(_COLS)
DO, DW = _places(_DEC_COLS)


def constants():
    main, decoded = np.zeros((P, CW), np.float32), np.zeros((ROWS, DW), np.float32)

    def put(name, a):
        a = np.asarray(a, np.float32)
        c, (lo, hi) = (main, CO[name]) if name in CO else (decoded, DO[name])
        c[:a.shape[0], lo:hi] = a.reshape(a.shape[0], hi - lo)

    p = np.arange(P)
    put("ident", np.eye(P))
    perm = np.zeros((P, P))
    perm[(p // HD) * HD + (p % HD + HD // 2) % HD, p] = 1.0
    put("perm", perm)
    put("headmean", (p[:, None] // HD == p[None, :] // HD) / HD)
    put("ones", np.ones((P, P)))
    put("causal", np.where(p[None, :] > p[:, None], NEG, 0.0))
    put("winlow", np.where(p[None, :] > p[:, None], 0.0, NEG))
    half = HD // 2
    inv = np.float32(10000.0) ** (-np.arange(half, dtype=np.float32) / np.float32(half))
    pos = np.concatenate([np.arange(SEQ), np.full(DEC, PAST)]).astype(np.float32)
    ang = (pos[None, :] * inv[p % half][:, None]).astype(np.float32)
    put("cos", np.cos(ang))
    put("sin", np.sin(ang) * np.where(p % HD < half, -1.0, 1.0)[:, None].astype(np.float32))
    lg = np.log1p(-np.exp2(-5.0 - np.arange(RH, dtype=np.float64)))
    diff = p[None, :] - p[:, None]
    inner = np.where(diff[:, None, :] >= 0, np.exp(lg[None, :, None] * np.maximum(diff[:, None, :], 0)), 0.0)
    put("inner", inner)
    lg2 = lg[2 * np.arange(4)[None, :] + (p // HD)[:, None]]
    put("qdec", np.exp(lg2[:, :, None] * (p[None, None, :] + 1)))
    put("kdec", np.exp(lg[None, :] * (P - 1 - p[:, None])))
    put("cdec", np.exp(lg2 * P))
    put("gamma", np.exp(lg2))
    posq = (np.arange(NB)[None, :] * P + p[:, None])[:, :, None]
    place = np.arange(CP)
    block = np.where(place % 32 < NB, 2 * (place % 32) + place // 32, SEQ)
    ok = (block[None, None, :] + 1) * CB - 1 <= posq
    put("cmpbias", np.where(ok, 0.0, NEG))
    put("cmpvalid", ok)
    row = np.arange(ROWS)
    own = row[:, None] // R == np.arange(DEC * G)[None, :]
    own = own.reshape(ROWS, 2, 1, 4, 1, G) & np.ones((1, 1, 2, 1, NPG, 1), bool)
    put("ownblocks", np.where(own, 0.0, NEG))
    nu = 2 * (np.arange(NBLK) % NPG) + np.arange(NBLK) // NPG
    put("earlier", np.broadcast_to(nu[None, None, :] < nu[None, :, None], (ROWS, NBLK, NBLK)))
    put("ownrow", row[:, None] // NH == np.arange(DEC)[None, :])
    put("headrows", row[:, None] // R == row[None, :] // R)
    return main, decoded


class Steps:

    def __init__(self, sem, n=0):
        self.sem, self.n = sem, n

    def done(self, ins):
        ins.then_inc(self.sem, 1)
        self.n += 1

    def fence(self, eng):
        eng.wait_ge(self.sem, self.n)


class Stage(ExitStack):

    def __init__(self, nc, tag):
        super().__init__()
        self.nc, self.tag, self.taken = nc, tag, []
        self.callback(self.give_back)

    def semaphore(self, name):
        self.taken.append(self.nc.alloc_semaphore(name=f"{self.tag}_{name}"))
        return self.taken[-1]

    def give_back(self):
        self.nc.clear_and_free_semaphores(self.taken)
        self.nc.all_engine_barrier()


class Memory:

    def __init__(self, nc):
        self.nc = nc
        base = (int(nc.sbuf_base) + 31) // 32 * 32
        T1 = TOK * 4
        self.const = self.place("const", [P, CW], F32, base)
        o = base + (CW * 4 + 31) // 32 * 32
        self.lnT = self.place("lnT", [P, 36], F32, o)
        self.small = self.place("small", [P, 64], F32, o + 160)
        self.gate_tok = self.place("gate_tok", [P, NB + 1, 24], F32, o + 416)
        self.ident_bf = self.place("ident_bf", [P, P], BF16, o + 1280)
        self.causal_bf = self.place("causal_bf", [P, P], BF16, o + 1536)
        self.winlow_bf = self.place("winlow_bf", [P, P], BF16, o + 1792)
        o += 2048
        self.ring = o
        self.wraw = [self.place(f"wraw{i}", [P, KT, P], F32, o + 4096 * i) for i in range(2)]
        self.whi = [self.place(f"whi{i}", [P, KT, P], F32R, o + 8192 + 4096 * i) for i in range(2)]
        self.wlo = [self.place(f"wlo{i}", [P, KT, P], F32R, o + 16384 + 4096 * i) for i in range(2)]
        o += 24576
        self.mixT = self.place("mixT", [P, KT, TOK], F32, o)
        self.M = o
        o += KT * T1
        self.A = o
        self.hi = self.place("act_hi", [P, KT, TOK], F32R, o)
        self.lo = self.place("act_lo", [P, KT, TOK], F32R, o + KT * T1)
        o += 70208
        self.N = o
        self.nqT = self.place("nqT", [P, 4, TOK], F32, o)
        self.selkT = self.place("sel_kT", [P, G, TOK], F32, o + 4 * T1)
        self.winkT = self.place("win_kT", [P, G, TOK], F32, o + 6 * T1)
        o += 8 * T1
        tok = (NB + 1) * P * 4
        self.ck_tok, self.cv_tok, self.sv_tok, self.wv_tok, self.k_stage = (
            self.place(n, [P, NB + 1, P], F32, o + i * tok)
            for i, n in enumerate(("cmp_k_rows", "cmp_v_rows", "sel_v_rows", "win_v_rows", "k_rows_staged")))
        self.feat = self.place("feature_rows", [P, TOK], F32, o + 5 * tok)
        self.stage = o + 4 * tok
        lo = (base + CO["cos"][0] * 4 + 31) // 32 * 32
        self.kcsT = self.place("cmp_kT_decoded", [HD, 4 * P], F32, lo)
        self.kcpT = self.place("cmp_kT_prompt", [P, G, CP], F32, lo + 2048)
        self.vcs = self.place("cmp_v_decoded", [P, 4, P], F32, lo + 2400 - 32)
        self.vcp = self.place("cmp_v_prompt", [CP, P], F32, lo + 4416)
        self.tables = lo
        self.rstd_ffn = self.place("rstd_ffn", [P, TOK], F32, (base + CO["inner"][0] * 4 + 31) // 32 * 32)
        self.h_again = self.place("h_again", [P, KT, TOK], F32, self.A)
        self.y_squares = self.place("y_square_sums", [P, TOK], F32, self.tables)
        assert o + 5 * tok + T1 <= int(nc.sbuf_usable_end)

    def place(self, name, shape, dt, offset):
        return self.nc.alloc_sbuf_tensor_at(name, shape, dt, offset=offset)

    def c(self, name, rows=P):
        lo, hi = CO[name]
        return self.const[0:rows, lo:hi]


def matmul3(pe, out, w_hi, w_lo, x_hi, x_lo):
    pairs = [(w_hi, x_hi), (w_hi, x_lo), (w_lo, x_hi)]
    for kt in range(KT):
        for n, (w, x) in enumerate(pairs):
            last = pe.matmul(out, w[:, kt, :], x[:, kt, :], start=(kt == 0 and n == 0),
                             stop=(kt == KT - 1 and n == 2))
    return last


class Stream:

    def __init__(self, ctx, m, ps, x_hi=None, x_lo=None):
        self.m, self.ps = m, ps
        self.x_hi, self.x_lo = x_hi or m.hi, x_lo or m.lo
        s = ctx.semaphore
        self.raw_loaded = [s("raw_loaded0"), s("raw_loaded1")]
        self.hi_ready = s("w_hi_ready")
        self.lo_ready = s("w_lo_ready")
        self.tile_done = s("tile_done")
        self.bank_free = s("bank_free")

    def load(self, sp, n, slot, src):
        sp.wait_ge(self.lo_ready, n + 1)
        sp.dma_start(self.m.wraw[slot][:], src).then_inc(self.raw_loaded[slot], 16)

    def round_hi(self, act, n, slot, half):
        act.wait_ge(self.raw_loaded[slot], half * 16 + 16)
        act.wait_ge(self.tile_done, n * 3 + 3)
        act.activation(self.m.whi[slot][:], self.m.wraw[slot][:], ACT.Copy).then_inc(self.hi_ready, 1)

    def reduce_lo(self, dve, n, slot, half):
        dve.wait_ge(self.raw_loaded[slot], half * 16 + 16)
        dve.wait_ge(self.hi_ready, n + 1)
        dve.tensor_tensor(self.m.wlo[slot][:], self.m.wraw[slot][:], self.m.whi[slot][:].bitcast(F32),
                          ALU.subtract).then_inc(self.lo_ready, 1)

    def start_loads(self, dve):
        dve.sem_inc(self.lo_ready, 2)

    def start(self, pe):
        pe.sem_inc(self.tile_done, 6)
        pe.sem_inc(self.bank_free, 3)

    def multiply(self, pe, n, slot, x_hi=None, x_lo=None):
        pe.wait_ge(self.hi_ready, n + 1)
        pe.wait_ge(self.lo_ready, n + 3)
        x_hi, x_lo = x_hi or self.x_hi, x_lo or self.x_lo
        for t in range(3):
            pe.wait_ge(self.bank_free, n * 3 + (t + 1))
            cols = slice(t * TN, (t + 1) * TN)
            last = matmul3(pe, self.ps[:, t, 0:TN], self.m.whi[slot], self.m.wlo[slot],
                           x_hi[:, :, cols], x_lo[:, :, cols])
            last.then_inc(self.tile_done, 1)

    def tiles(self, eng, n):
        for t in range(3):
            eng.wait_ge(self.tile_done, n * 3 + (6 + t + 1))
            yield t, slice(t * TN, (t + 1) * TN), self.ps[:, t, 0:TN]

    def evacuated(self, n, t):
        return n * 3 + (3 + t + 1)


def stage_prepare(nc, m, ps, io):
    with Stage(nc, "prep") as ctx:
        s = ctx.semaphore
        const_loaded, ln_loaded, x_loaded, xs_loaded = s("const_loaded"), s("ln_loaded"), [s(f"x_loaded{i}") for i in range(4)], s("xs_loaded")
        ident_loaded = s("ident_loaded")
        win_copied = s("win_copied")
        squares, mean_ready, root_ready = s("squares"), s("mean_ready"), s("root_ready")
        rstd_ready, scaled, turned = s("rstd_ready"), s("scaled"), s("turned")
        hi_done, lo_done, ln_turned, ln_ready = s("hi_done"), s("lo_done"), s("ln_turned"), s("ln_ready")
        casts = s("casts")
        x = m.place("x_rows", [P, NB, D_MODEL], F32, m.N)
        xs = m.place("x_decoded", [DEC, D_MODEL], F32, m.N + NB * D_MODEL * 4)
        junk = m.place("squares_out", [P, D_MODEL], F32, m.N + (NB + 1) * D_MODEL * 4)
        lnrows = m.place("ln_rows", [36, P], F32, m.N + (NB + 2) * D_MODEL * 4)
        sums = m.small[:, 0:NB + 1]
        rstd = m.small[:, 16:16 + NB + 1]
        units = [(kt, h) for h in range(3) for kt in range(KT)]

        def span(h):
            return (slice(0, 512), slice(512, 1024), slice(SEQ, TOK))[h]

        block = ctx.enter_context(nc.Block())

        @block.sync
        def _(sp):
            for i in range(4):
                sp.dma_start(x[:, 2 * i:2 * i + 2, :], io["x_prompt"][0, 2 * P * i:2 * P * (i + 1), :]
                             .rearrange("(t p) d -> p t d", p=P)).then_inc(x_loaded[i], 16)
                if i == 0:
                    sp.dma_start(m.const[:, 0:P], io["const"][:, 0:P]).then_inc(ident_loaded, 16)
            sp.dma_start(m.const[:, P:], io["const"][:, P:]).then_inc(const_loaded, 16)

        @block.gpsimd
        def _(pool):
            pool.dma_start(xs[:], io["x_sample"][:, 0, :]).then_inc(xs_loaded, 16)
            for i, w in enumerate(("ln_pre_mix", "ln_post_mix", "ln_pre_ffn", "ln_post_ffn", "ret_gn_w")):
                src = io[w][0, :].rearrange("(k p) -> k p", p=P)
                pool.dma_start(lnrows[8 * i:8 * i + src.shape[0], :], src).then_inc(ln_loaded, 16)
            pool.wait_ge(x_loaded[3], 16)
            for old, new in (("cache_win_k", "win_k_sample"), ("cache_win_v", "win_v_sample")):
                pool.dma_start(io[new][0, :, 0:WIN - 1].rearrange("b t g d -> b (t g d)"),
                               io[old][0, :, 1:WIN].rearrange("b t g d -> b (t g d)")).then_inc(win_copied, 16)
            pool.wait_ge(win_copied, 32)

        @block.scalar
        def _(act):
            act.wait_ge(xs_loaded, 16)
            act.activation(junk[0:DEC, :], xs[:], ACT.Square, accum_out=sums[0:DEC, NB:NB + 1]).then_inc(squares, 1)
            for t in range(NB):
                if t % 2 == 0:
                    act.wait_ge(x_loaded[t // 2], 16)
                act.wait_ge(squares, t + 1)
                act.activation(junk[:], x[:, t, :], ACT.Square, accum_out=sums[:, t:t + 1]).then_inc(squares, 1)
                if t % 4 == 3:
                    act.wait_ge(mean_ready, t // 4 + 1)
                    act.activation(rstd[:, t - 3:t + 1], rstd[:, t - 3:t + 1], ACT.Sqrt).then_inc(root_ready, 1)
            act.wait_ge(mean_ready, 3)
            act.activation(rstd[0:DEC, NB:NB + 1], rstd[0:DEC, NB:NB + 1], ACT.Sqrt).then_inc(root_ready, 1)
            act.wait_ge(ln_turned, 1)
            act.activation(m.lnT[:], ps[:, 7, 0:36], ACT.Copy).then_inc(ln_ready, 1)
            act.wait_ge(ln_ready, 1)
            for u, (kt, h) in enumerate(units):
                act.wait_ge(turned, u + 1)
                cols = span(h)
                act.activation(m.hi[:, kt, cols], ps[:, u % 6, 0:cols.stop - cols.start], ACT.Copy,
                               scale=m.lnT[:, kt:kt + 1]).then_inc(hi_done, 1)

        @block.vector
        def _(dve):
            for h in range(2):
                part = slice(4 * h, 4 * h + 4)
                dve.wait_ge(squares, 4 * h + 5)
                dve.tensor_scalar(rstd[:, part], sums[:, part], 1.0 / D_MODEL, EPS, ALU.mult, ALU.add).then_inc(mean_ready, 1)
                dve.wait_ge(root_ready, h + 1)
                dve.reciprocal(rstd[:, part], rstd[:, part]).then_inc(rstd_ready, 1)
                dve.wait_ge(rstd_ready, h + 1)
                for t in range(4 * h, 4 * h + 4):
                    dve.tensor_scalar(x[:, t, :], x[:, t, :], rstd[:, t:t + 1], None, ALU.mult).then_inc(scaled, 1)
            dve.tensor_scalar(rstd[0:DEC, NB:NB + 1], sums[0:DEC, NB:NB + 1], 1.0 / D_MODEL, EPS, ALU.mult,
                              ALU.add).then_inc(mean_ready, 1)
            dve.wait_ge(root_ready, 3)
            dve.reciprocal(rstd[0:DEC, NB:NB + 1], rstd[0:DEC, NB:NB + 1]).then_inc(rstd_ready, 1)
            dve.wait_ge(rstd_ready, 3)
            dve.tensor_scalar(xs[:], xs[:], rstd[0:DEC, NB:NB + 1], None, ALU.mult).then_inc(scaled, 1)
            for u, (kt, h) in enumerate(units):
                dve.wait_ge(hi_done, u + 1)
                cols = span(h)
                dve.scalar_tensor_tensor(m.lo[:, kt, cols], ps[:, u % 6, 0:cols.stop - cols.start],
                                         m.lnT[:, kt:kt + 1], m.hi[:, kt, cols].bitcast(F32),
                                         ALU.mult, ALU.subtract).then_inc(lo_done, 1)
            dve.wait_ge(const_loaded, 16)
            for dst, name in ((m.ident_bf, "ident"), (m.causal_bf, "causal"), (m.winlow_bf, "winlow")):
                dve.tensor_copy(dst[:], m.c(name)).then_inc(casts, 1)

        @block.tensor
        def _(pe):
            pe.wait_ge(ident_loaded, 16)
            pe.wait_ge(ln_loaded, 80)
            pe.transpose(ps[:, 7, 0:36], lnrows[:], m.c("ident")[0:36, 0:36]).then_inc(ln_turned, 1)
            for u, (kt, h) in enumerate(units):
                if u >= 6:
                    pe.wait_ge(lo_done, u - 5)
                if h < 2:
                    pe.wait_ge(scaled, 4 * h + 4)
                    for i in range(4):
                        last = pe.transpose(ps[:, u % 6, i * P:(i + 1) * P],
                                            x[:, 4 * h + i, kt * P:(kt + 1) * P], m.c("ident"))
                else:
                    pe.wait_ge(scaled, NB + 1)
                    last = pe.transpose(ps[:, u % 6, 0:DEC], xs[:, kt * P:(kt + 1) * P],
                                        m.c("ident")[0:DEC, 0:DEC])
                last.then_inc(turned, 1)


def stage_project(nc, m, ps, io):
    with Stage(nc, "proj") as ctx:
        s = ctx.semaphore
        w = Stream(ctx, m, ps)
        B = m.N
        T1 = TOK * 4
        qT = m.place("ret_qT", [P, TOK], F32, B)
        kT = m.place("ret_kT", [P, TOK], F32, B + T1)
        vT = m.place("ret_vT", [P, TOK], F32, B + 2 * T1)
        rope_tmp = m.place("rope_tmp", [P, TOK], F32, B + 3 * T1)
        o = B + 4 * T1
        qd = m.place("ret_q_decayed", [P, SEQ], F32, o)
        k_tok = m.place("ret_k_decayed", [P, NB, P], F32, o + 4096)
        v_tok = m.place("ret_v", [P, NB, P], F32, o + 8192)
        states = m.place("ret_states", [P, NB, P], F32, o + 12288)
        aT = [m.place(f"ret_aT{i}", [P, 2, P], F32, o + 16384 + 1024 * i) for i in range(2)]
        s_in = m.place("dec_state_in", [P, DEC, HD], F32, o + 18432)
        s_new = m.place("dec_state_new", [P, DEC, HD], F32, o + 20480)
        v_diag = m.place("dec_v_diag", [DEC, DEC, P], F32, o + 22528)
        kv_dec = m.place("dec_kv", [DEC, 2, P], F32, o + 26624)

        raw_src = io["w_in"][0].rearrange("(kt p) n -> p kt n", p=P)
        s_src = io["state_ret"][0].rearrange("b h d e -> h d b e")
        s_dst = io["ret_state_sample"][0].rearrange("b h d e -> h d b e")
        p_dst = io["ret_state_prompt"][0, 0]

        swapped = s("swapped")
        swap_read = s("swap_read")
        roped = s("roped")
        turned = s("turned")
        tok_ready = s("tok_ready")
        kv_made = s("kv_made")
        state_made = s("state_made")
        diag_made = s("diag_made")
        outer_made = s("outer_made")
        dec_state = s("dec_state")
        q_decayed = s("q_decayed")
        scores_made = s("scores_made")
        scores_masked = s("scores_masked")
        out_made = s("out_made")
        out_copied = s("out_copied")
        state_loaded, state_stored, pool_past = s("state_loaded"), s("state_stored"), s("pool_past")
        feat_turned, feat_copied, k_spread = s("feat_turned"), s("feat_copied"), s("k_spread")
        rows_stored, sk_stored = s("rows_stored"), s("sk_stored")
        tmpF = m.feat

        block = ctx.enter_context(nc.Block())
        COLS = [0, 512, 1024, 1536]
        TAIL = [2560, 2688, 2816, 2944, 3072, 3200, IN_W - P]
        NQ0, TAIL0 = 16, 20

        @block.sync
        def _(sp):
            with sp.Fori(0, 4) as j:
                for t, c in enumerate(COLS):
                    w.load(sp, j * 4 + t, t % 2, raw_src[:, :, bass.ds(j * P + c, P)])
            with sp.Fori(0, 2) as i:
                for t in range(2):
                    w.load(sp, i * 2 + (NQ0 + t), t, raw_src[:, :, bass.ds(i * (2 * P) + (2048 + t * P), P)])
            for i, c in enumerate(TAIL):
                w.load(sp, TAIL0 + i, i % 2, raw_src[:, :, c:c + P])

        @block.tensor
        def _(pe):
            w.start(pe)
            pe.sem_inc(out_copied, 3)
            with pe.Fori(0, 4) as j:
                def swap_halves(x, n):
                    pe.wait_ge(w.bank_free, j * 12 + (3 + 3 * (n + 1)))
                    for t in range(3):
                        last = pe.matmul(ps[:, 3 + t, 0:TN], m.c("perm"), x[:, t * TN:(t + 1) * TN], start=True, stop=True)
                    last.then_inc(swapped, 1)

                w.multiply(pe, j * 4, 0)
                w.multiply(pe, j * 4 + 1, 1)
                pe.wait_ge(out_copied, j * 3 + 3)
                swap_halves(qT, 0)
                w.multiply(pe, j * 4 + 2, 0)
                pe.wait_ge(swap_read, j * 2 + 1)
                swap_halves(kT, 1)
                w.multiply(pe, j * 4 + 3, 1)
                pe.wait_ge(w.bank_free, j * 12 + (3 + 9))
                for i in range(NB):
                    last = pe.transpose(ps[:, 6 + i // 4, (i % 4) * P:(i % 4 + 1) * P], vT[:, i * P:(i + 1) * P], m.c("ident"))
                last.then_inc(turned, 1)
                pe.wait_ge(roped, j * 4 + 4)
                pe.transpose(ps[0:DEC, 3, 0:P], kT[:, SEQ:TOK], m.c("ident"))
                pe.transpose(ps[0:DEC, 3, P:2 * P], vT[:, SEQ:TOK], m.c("ident")).then_inc(turned, 1)
                pe.wait_ge(tok_ready, j * 4 + 1)
                for i in range(NB):
                    last = pe.transpose(ps[:, 6 + i // 4, (i % 4) * P:(i % 4 + 1) * P], kT[:, i * P:(i + 1) * P], m.c("ident"))
                last.then_inc(turned, 1)
                pe.wait_ge(diag_made, j + 1)
                for h in range(2):
                    last = pe.matmul(ps[:, 4 + h, :], kv_dec[:, 0, :], v_diag[:, 4 * h:4 * h + 4, :], start=True, stop=True)
                last.then_inc(outer_made, 1)
                pe.wait_ge(tok_ready, j * 4 + 4)
                for i in range(NB):
                    last = pe.matmul(ps[:, 6 + i // 4, (i % 4) * P:(i % 4 + 1) * P], k_tok[:, i, :], v_tok[:, i, :], start=True, stop=True)
                    if i % 4 == 3:
                        last.then_inc(kv_made, 1)

                def scores(i):
                    if i >= 2:
                        pe.wait_ge(scores_masked, j * 8 + (i - 1))
                    for h in range(2):
                        rows = slice(h * HD, (h + 1) * HD)
                        last = pe.matmul(ps[:, 3 - 2 * (i % 2) + h, 0:P], kT[rows, i * P:(i + 1) * P],
                                         qT[rows, i * P:(i + 1) * P], start=True, stop=True)
                    last.then_inc(scores_made, 1)

                pe.wait_ge(dec_state, j * 2 + 2)
                pe.wait_ge(w.bank_free, j * 12 + (3 + 12))
                scores(0)
                for b in range(DEC):
                    for h in range(2):
                        rows = slice(h * HD, (h + 1) * HD)
                        last = pe.matmul(ps[rows, 5, b:b + 1], s_new[rows, b, :], qT[rows, SEQ + b:SEQ + b + 1],
                                         start=True, stop=True)
                last.then_inc(out_made, 1)
                pe.wait_ge(state_made, j * 8 + 8)
                pe.wait_ge(q_decayed, j + 1)
                for i in range(NB):
                    if i + 1 < NB:
                        scores(i + 1)
                    pe.wait_ge(scores_masked, j * 8 + (i + 1))
                    for h in range(2):
                        rows = slice(h * HD, (h + 1) * HD)
                        out = ps[rows, 6 + i // 4, (i % 4) * P:(i % 4 + 1) * P]
                        last = pe.matmul(out, v_tok[:, i, rows], aT[i % 2][:, h, :], start=True, stop=(i == 0))
                        if i:
                            last = pe.matmul(out, states[rows, i - 1, rows], qd[rows, i * P:(i + 1) * P],
                                             start=False, stop=True)
                    if i % 4 == 3:
                        last.then_inc(out_made, 1)
            with pe.Fori(0, 2) as i:
                for t in range(2):
                    w.multiply(pe, i * 2 + (NQ0 + t), t)
            for c in range(7):
                w.multiply(pe, TAIL0 + c, c % 2)
                pe.wait_ge(w.bank_free, w.evacuated(TAIL0 + c, 2))
                if c:
                    pe.wait_ge(feat_copied, 2 * c)
                for i in range(NB):
                    pe.transpose(ps[:, 3 + i // 4, (i % 4) * P:(i % 4 + 1) * P], tmpF[:, i * P:(i + 1) * P], m.c("ident"))
                pe.transpose(ps[0:DEC, 5, 0:P], tmpF[:, SEQ:TOK], m.c("ident")).then_inc(feat_turned, 1)


        @block.scalar
        def _(act):
            def evacuate(n, dst, func=ACT.Copy, scale=1.0):
                for t, cols, tile in w.tiles(act, n):
                    act.activation(dst[:, cols], tile, func, scale=scale).then_inc(w.bank_free, 1)

            w.round_hi(act, 0, 0, 0)
            with act.Fori(0, 4) as j:
                w.round_hi(act, j * 4 + 1, 1, j * 2)
                evacuate(j * 4, qT)
                w.round_hi(act, j * 4 + 2, 0, j * 2 + 1)
                evacuate(j * 4 + 1, kT, scale=SCALE)
                w.round_hi(act, j * 4 + 3, 1, j * 2 + 1)
                evacuate(j * 4 + 2, vT)
                w.round_hi(act, j * 4 + 4, 0, j * 2 + 2)
                evacuate(j * 4 + 3, m.mixT[:, bass.ds(j + 4, 1), :].rearrange("p a n -> p (a n)"), ACT.Silu)
                act.wait_ge(turned, j * 3 + 1)
                act.activation(v_tok[:], ps[:, 6:8, :].rearrange("p a (b f) -> p (a b) f", f=P), ACT.Copy).then_inc(tok_ready, 1)
                act.wait_ge(turned, j * 3 + 2)
                act.activation(kv_dec[:], ps[0:DEC, 3, 0:2 * P].rearrange("p (a f) -> p a f", f=P), ACT.Copy).then_inc(tok_ready, 1)
                act.wait_ge(turned, j * 3 + 3)
                for h in range(2):
                    act.activation(k_tok[:, :, h * HD:(h + 1) * HD],
                                   ps[:, 6:8, :].rearrange("p a (b f) -> p (a b) f", f=P)[:, :, h * HD:(h + 1) * HD],
                                   ACT.Copy, scale=m.c("kdec")[:, bass.ds(j * 2 + h, 1)]).then_inc(tok_ready, 1)
                dst = m.mixT[:, bass.ds(j, 1), :].rearrange("p a n -> p (a n)")
                for n, (cols, src) in enumerate(((slice(SEQ, TOK), ps[:, 5, 0:DEC]), (slice(0, 512), ps[:, 6, :]),
                                                 (slice(512, SEQ), ps[:, 7, :]))):
                    act.wait_ge(out_made, j * 3 + (n + 1))
                    act.activation(dst[:, cols], src, ACT.Copy).then_inc(out_copied, 1)
            with act.Fori(0, 2) as i:
                for t in range(2):
                    w.round_hi(act, i * 2 + (NQ0 + t + 1), 1 - t, i + (8 + (t + 1) // 2))
                    evacuate(i * 2 + (NQ0 + t), m.nqT[:, bass.ds(i * 2 + t, 1), :].rearrange("p a n -> p (a n)"), scale=SCALE)
            for c in range(7):
                if c < 6:
                    w.round_hi(act, TAIL0 + c + 1, (c + 1) % 2, (TAIL0 + c + 1) // 2)
                if c:
                    act.wait_ge(feat_turned, c)
                    if c in (3, 5):
                        act.wait_ge(k_spread, 2 * (c - 1))
                evacuate(TAIL0 + c, tmpF, ACT.Sigmoid if c == 6 else ACT.Copy)

        @block.vector
        def _(dve):
            banks = ps[:, 3:6, 0:TN]
            tri = lambda a: a.rearrange("p (a n) -> p a n", a=3)
            w.start_loads(dve)
            w.reduce_lo(dve, 0, 0, 0)
            with dve.Fori(0, 4) as j:
                w.reduce_lo(dve, j * 4 + 1, 1, j * 2)
                w.reduce_lo(dve, j * 4 + 2, 0, j * 2 + 1)
                for n, x in enumerate((qT, kT)):
                    if n:
                        w.reduce_lo(dve, j * 4 + 3, 1, j * 2 + 1)
                    dve.wait_ge(swapped, j * 2 + (n + 1))
                    if n:
                        dve.wait_ge(roped, j * 4 + 2)
                    dve.tensor_tensor(tri(rope_tmp[:]), banks, tri(m.c("sin")), ALU.mult).then_inc(swap_read, 1)
                    dve.tensor_tensor(x[:], x[:], m.c("cos"), ALU.mult).then_inc(roped, 1)
                    dve.wait_ge(swap_read, j * 2 + (n + 1))
                    dve.wait_ge(roped, j * 4 + (2 * n + 1))
                    dve.tensor_tensor(x[:], x[:], rope_tmp[:], ALU.add).then_inc(roped, 1)
                w.reduce_lo(dve, j * 4 + 4, 0, j * 2 + 2)
                dve.wait_ge(tok_ready, j * 4 + 2)
                dve.tensor_tensor(v_diag[:], kv_dec[:, 1:2, :].broadcast_to([DEC, DEC, P]),
                                  m.c("ident")[0:DEC, 0:DEC].unsqueeze(2).broadcast_to([DEC, DEC, P]),
                                  ALU.mult).then_inc(diag_made, 1)
                dve.tensor_tensor(qd[:].rearrange("p (b n) -> p b n", n=P), qT[:, 0:SEQ].rearrange("p (b n) -> p b n", n=P),
                                  m.c("qdec")[:, bass.ds(j * P, P)].unsqueeze(1).broadcast_to([P, NB, P]),
                                  ALU.mult).then_inc(q_decayed, 1)
                dve.wait_ge(state_loaded, j * 32 + 32)
                dve.wait_ge(outer_made, j + 1)
                for h in range(2):
                    rows = slice(h * HD, (h + 1) * HD)
                    dve.scalar_tensor_tensor(s_new[rows], s_in[rows], m.c("gamma")[rows, bass.ds(j, 1)],
                                             ps[rows, 4:6, :].rearrange("p a (b f) -> p (a b) f", f=P)[:, :, rows],
                                             ALU.mult, ALU.add).then_inc(dec_state, 1)
                for i in range(NB):
                    kv = ps[:, 6 + i // 4, (i % 4) * P:(i % 4 + 1) * P]
                    if i % 4 == 0:
                        dve.wait_ge(kv_made, j * 2 + (i // 4 + 1))
                    if i == 0:
                        dve.tensor_copy(states[:, 0, :], kv).then_inc(state_made, 1)
                    else:
                        dve.wait_ge(state_made, j * 8 + i)
                        dve.scalar_tensor_tensor(states[:, i, :], states[:, i - 1, :], m.c("cdec")[:, bass.ds(j, 1)],
                                                 kv, ALU.mult, ALU.add).then_inc(state_made, 1)
                for i in range(NB):
                    dve.wait_ge(scores_made, j * 8 + (i + 1))
                    dve.tensor_tensor(aT[i % 2][:], ps[:, 3 - 2 * (i % 2):5 - 2 * (i % 2), 0:P],
                                      m.c("inner")[:, bass.ds(j * (2 * P), 2 * P)].rearrange("p (a n) -> p a n", n=P),
                                      ALU.mult).then_inc(scores_masked, 1)
            with dve.Fori(0, 2) as i:
                for t in range(2):
                    w.reduce_lo(dve, i * 2 + (NQ0 + t + 1), 1 - t, i + (8 + (t + 1) // 2))
            dve.wait_ge(state_stored, 64 * 4)
            toks = [m.ck_tok, m.cv_tok, m.k_stage, m.sv_tok, m.k_stage, m.wv_tok]
            for c in range(7):
                if c < 6:
                    w.reduce_lo(dve, TAIL0 + c + 1, (c + 1) % 2, (TAIL0 + c + 1) // 2)
                if c in (2, 4):
                    dve.wait_ge(w.bank_free, w.evacuated(TAIL0 + c, 2))
                    kd = m.selkT if c == 2 else m.winkT
                    for g in range(G):
                        for h in range(2):
                            dve.tensor_copy(kd[h * HD:(h + 1) * HD, g, :], tmpF[g * HD:(g + 1) * HD, :]).then_inc(k_spread, 1)
                dve.wait_ge(feat_turned, c + 1)
                src = ps[:, 3:5, :].rearrange("p a (b f) -> p (a b) f", f=P)
                if c == 6:
                    dve.tensor_copy(m.gate_tok[:, 0:NB, :], src[:, :, P - 24:P]).then_inc(feat_copied, 1)
                    dve.tensor_copy(m.gate_tok[0:DEC, NB, :], ps[0:DEC, 5, P - 24:P]).then_inc(feat_copied, 1)
                else:
                    if c == 4:
                        dve.wait_ge(sk_stored, 32)
                    dve.tensor_copy(toks[c][:, 0:NB, :], src).then_inc(feat_copied, 1)
                    dve.tensor_copy(toks[c][0:DEC, NB, :], ps[0:DEC, 5, 0:P]).then_inc(feat_copied, 1)

        @block.gpsimd
        def _(pool):
            with pool.Fori(0, 4) as j:
                pool.wait_ge(out_copied, j * 3 + 3)
                pool.sem_inc(pool_past, 1)
                for h in range(2):
                    rows = slice(h * HD, (h + 1) * HD)
                    pool.dma_start(s_in[rows], s_src[bass.ds(j * 2 + h, 1)].rearrange("h d b e -> (h d) b e")).then_inc(state_loaded, 16)
                pool.wait_ge(dec_state, j * 2 + 2)
                pool.sem_inc(pool_past, 1)
                for h in range(2):
                    rows = slice(h * HD, (h + 1) * HD)
                    pool.dma_start(s_dst[bass.ds(j * 2 + h, 1)].rearrange("h d b e -> (h d) b e"), s_new[rows]).then_inc(state_stored, 16)
                pool.wait_ge(state_made, j * 8 + 8)
                pool.sem_inc(pool_past, 1)
                for h in range(2):
                    rows = slice(h * HD, (h + 1) * HD)
                    pool.dma_start(p_dst[bass.ds(j * 2 + h, 1)].rearrange("h d e -> (h d) e"), states[rows, NB - 1, rows]).then_inc(state_stored, 16)
                pool.wait_ge(state_stored, j * 64 + 64)
                pool.sem_inc(pool_past, 1)
            outs = [(m.ck_tok, "cmp_k"), (m.cv_tok, "cmp_v"), (m.k_stage, "sel_k"), (m.sv_tok, "sel_v"),
                    (m.k_stage, "win_k"), (m.wv_tok, "win_v")]
            for c, (tile, name) in enumerate(outs):
                pool.wait_ge(feat_copied, 2 * c + 2)
                stored = sk_stored if c == 2 else rows_stored
                first = 0 if c < 4 else NB - WIN // P
                pool.dma_start(io[name + "_prompt"][0, 0].rearrange("(t p) g d -> p t (g d)", p=P),
                               tile[:, first:NB, :]).then_inc(stored, 16)
                row = 0 if c < 4 else WIN - 1
                pool.dma_start(io[name + "_sample"][0, :, row].rearrange("b g d -> b (g d)"),
                               tile[0:DEC, NB, :]).then_inc(stored, 16)
            pool.wait_ge(rows_stored, 16 * 10)
            pool.wait_ge(sk_stored, 32)


def load_pages(eng, table, first, count, cache, slab_page, sem, turn=4):
    with eng.Fori(0, count // turn) as i:
        pages = [eng.value_load(table[0:1, bass.ds(i * turn + (first + k), 1)], min_val=0, max_val=159) for k in range(turn)]
        for k, page in enumerate(pages):
            eng.dma_start(slab_page(i, k), cache[bass.ds(page, 1)].rearrange("a t g d -> t a (g d)")).then_inc(sem, 16)


def stage_decode(nc, m, ps, io):
    with Stage(nc, "dec") as ctx:
        s = ctx.semaphore
        table_loaded, const_loaded = s("table_loaded"), s("const_loaded")
        gates_out, gates_in = s("gates_out"), s("gates_in")
        k_loaded = {who: [s(f"k_{who}_loaded{i}") for i in range(4)] for who in ("sp", "pool", "act")}
        v_loaded = {who: [s(f"v_{who}_loaded{i}") for i in range(4)] for who in ("sp", "pool", "act")}
        cleared, q_ready = s("cleared"), s("q_ready")
        k_turned, k_copied, k_used = s("k_turned"), s("k_copied"), s("k_used")
        cmp_scores, cmp_exp, cmp_dve = s("cmp_scores"), s("cmp_exp"), s("cmp_dve")
        importance, new_scores = s("importance"), s("new_scores")
        soft_dve, soft_exp, win_out = s("soft_dve"), s("soft_exp"), s("win_out")
        p_turned, p_copied, v_used, placed = s("p_turned"), s("p_copied"), s("v_used"), s("placed")
        odd_in, odd_out, out_dve, out_turned = s("odd_in"), s("odd_out"), s("out_dve"), s("out_turned")

        A = m.A
        pages = [m.place(f"dec_pages{i}", [P, 20, P], F32, A + 10240 * i) for i in range(4)]
        kT = m.place("dec_kT", [P, 5, 512], F32, A + 40960)
        p = m.place("dec_p", [ROWS, PAST + 1 + WIN + 1], F32, A + 51200)
        pc = m.place("dec_p_cmp", [ROWS, 4 * P], F32, A + 61472)
        pT = m.place("dec_pT", [P, 24, ROWS], F32, A + 63520)
        dc = m.place("dec_const", [ROWS, DW], F32, m.ring)
        o = m.ring + 6432
        qz = m.place("dec_q_by_batch", [P, DEC, ROWS], F32, o)
        gt = m.place("dec_rank_gt", [ROWS, NBLK, NBLK], F32, o + 2048)
        eq = m.place("dec_rank_eq", [ROWS, NBLK, NBLK], F32, o + 6144)
        o_odd = m.place("dec_out_odd", [ROWS, DEC, P], F32, o + 2048)
        o_sum = m.place("dec_out_sum", [ROWS, DEC, P], F32, o + 6144)
        o_row = m.place("dec_out_row", [ROWS, P], F32, o)
        o += 10240
        qc = m.place("dec_q_cmp", [HD, DEC, NH], F32, o)
        knew = m.place("dec_k_new", [P, 2, DEC], F32, o + 256)
        gates = m.place("dec_gates", [ROWS, 4], F32, o + 320)
        pn = m.place("dec_p_new", [ROWS, 2, DEC], F32, o + 352)
        pnT = m.place("dec_p_newT", [DEC, 2, ROWS], F32, o + 416)
        halves = m.place("dec_p_halves", [ROWS, 256], F32, o + 928)
        imp = m.place("dec_importance", [ROWS, 4, NBLK], F32, o + 1952)
        table = m.place("dec_page_table", [1, DEC * NPG], I32, o + 2464)
        col = m.place("dec_columns", [ROWS, 16], F32, o + 2976)
        scratch = nc.dram_tensor("gate_rows", [DEC, NH * 3], F32, kind="Internal").ap()

        def take(i):
            lo, hi = DO[i]
            return dc[:, lo:hi]

        block = ctx.enter_context(nc.Block())

        SHARES = {"sp": (0, 5), "pool": (5, 6), "act": (11, 5)}

        def load_batch(eng, who, slab, name, b, loaded):
            first, count = SHARES[who]
            load_pages(eng, table, b * NPG + first, count, io[f"cache_sel_{name}"][0],
                       lambda i, k: slab[:, bass.ds(i * count + (first + k), 1), :], loaded, turn=count)
            if who == "sp":
                eng.dma_start(slab[:, NPG:20, :], io[f"cache_win_{name}"][0, b].rearrange("(j t) g d -> t j (g d)", t=P)).then_inc(loaded, 16)

        def load_k(eng, who, b):
            if b >= 4:
                eng.wait_ge(k_turned, 5 * (b - 3))
            load_batch(eng, who, pages[b % 4], "k", b, k_loaded[who][b % 4])

        def load_v(eng, who, b):
            if b < 4:
                eng.wait_ge(k_turned, 5 * (b + 5))
            else:
                eng.wait_ge(v_used, b - 3)
            load_batch(eng, who, pages[b % 4], "v", b, v_loaded[who][b % 4])

        def wait_loaded(eng, loaded, slab, times):
            for who, (_, count) in SHARES.items():
                eng.wait_ge(loaded[who][slab], 16 * (count + (who == "sp")) * times)

        @block.sync
        def _(sp):
            sp.dma_start(table[:], io["page_table"].rearrange("(a b) n -> a (b n)", a=1)).then_inc(table_loaded, 16)
            sp.dma_start(dc[:], io["dec_const"]).then_inc(const_loaded, 16)
            sp.dma_start(scratch, m.gate_tok[0:DEC, NB, :]).then_inc(gates_out, 16)
            sp.wait_ge(gates_out, 16)
            sp.dma_start(gates[:, 0:3], scratch.rearrange("b (h c) -> (b h) c", c=3)).then_inc(gates_in, 16)
            sp.wait_ge(table_loaded, 16)
            for b in range(DEC):
                load_k(sp, "sp", b)
            for b in range(DEC):
                load_v(sp, "sp", b)

        @block.gpsimd
        def _(pool):
            pool.wait_ge(table_loaded, 16)
            for b in range(DEC):
                load_k(pool, "pool", b)
            for b in range(DEC):
                load_v(pool, "pool", b)

        @block.tensor
        def _(pe):
            pe.wait_ge(q_ready, 20)
            pe.matmul(ps[0:ROWS, 7, :], qc[:].rearrange("p b h -> p (b h)"), m.kcsT[:], start=True, stop=True).then_inc(cmp_scores, 1)

            def score(n):
                b, c = divmod(n, 5)
                pe.wait_ge(k_copied, n + 1)
                half = slice((c % 2) * ROWS, (c % 2 + 1) * ROWS)
                pe.matmul(ps[half, c, :], qz[:, b, :], kT[:, c, :], start=(b == 0), stop=(b == DEC - 1)).then_inc(k_used, 1)

            for n in range(5 * DEC):
                b, c = divmod(n, 5)
                if c == 0:
                    wait_loaded(pe, k_loaded, b % 4, b // 4 + 1)
                if n >= 2:
                    pe.wait_ge(k_copied, n - 1)
                for i in range(4):
                    last = pe.transpose(ps[:, 5 + n % 2, i * P:(i + 1) * P], pages[b % 4][:, 4 * c + i, :], m.c("ident"))
                last.then_inc(k_turned, 1)
                if c in (2, 4):
                    score(n - 2)
                    score(n - 1)
                elif c == 0 and n:
                    score(n - 1)
                if n == 20:
                    pe.wait_ge(cmp_dve, 6)
                    pe.wait_ge(const_loaded, 16)
                    pe.matmul(ps[0:ROWS, 7, 0:NBLK], take("headrows"), imp[:, 0, :], start=True, stop=True).then_inc(importance, 1)
            score(5 * DEC - 1)
            pe.wait_ge(cmp_dve, 7)
            for w in range(2):
                for b in range(DEC):
                    last = pe.matmul(ps[0:ROWS, 7, w:w + 1], qz[:, b, :], knew[:, w, b:b + 1], start=(b == 0), stop=(b == DEC - 1))
            last.then_inc(new_scores, 1)
            pe.wait_ge(soft_dve, 18)
            for i in range(24):
                src = pc[:, (i - 20) * P:(i - 19) * P] if i >= 20 else p[:, i * P + (i >= NPG):(i + 1) * P + (i >= NPG)]
                last = pe.transpose(ps[:, i // 8, (i % 8) * ROWS:(i % 8 + 1) * ROWS], src, m.c("ident")[0:ROWS, 0:ROWS])
                if i % 8 == 7:
                    last.then_inc(p_turned, 1)
            for w in range(2):
                last = pe.transpose(ps[0:DEC, 3, w * ROWS:(w + 1) * ROWS], pn[:, w, :], m.c("ident")[0:ROWS, 0:ROWS])
            last.then_inc(p_turned, 1)
            pe.wait_ge(p_copied, 4)
            common = ps[0:ROWS, 4, 0:P]
            for c in range(4):
                pe.matmul(common, pT[:, 20 + c, :], m.vcs[:, c, :], start=(c == 0), stop=False)
            for w, v in enumerate((m.sv_tok, m.wv_tok)):
                pe.matmul(common, pnT[:, w, :], v[0:DEC, NB, :], start=False, stop=(w == 1))
            for b in range(DEC):
                wait_loaded(pe, v_loaded, b % 4, b // 4 + 1)
                for i in range(20):
                    e = i % 2
                    last = pe.matmul(ps[e * ROWS:(e + 1) * ROWS, 5 + b // 4, (b % 4) * P:(b % 4 + 1) * P], pT[:, i, :],
                                     pages[b % 4][:, i, :], start=(i < 2), stop=(i >= 18))
                last.then_inc(v_used, 1)
            pe.wait_ge(out_dve, 5)
            pe.transpose(ps[:, 3, 0:ROWS], o_row[:], m.c("ident")[0:ROWS, 0:ROWS]).then_inc(out_turned, 1)

        @block.scalar
        def _(act):
            act.wait_ge(table_loaded, 16)
            for b in range(DEC):
                load_k(act, "act", b)
                if b == 1:
                    act.wait_ge(cmp_dve, 3)
                    act.activation(pc[:], pc[:], ACT.Exp, bias=col[:, 1:2], accum_out=col[:, 2:3]).then_inc(cmp_exp, 1)
            for b in range(4):
                load_v(act, "act", b)
            act.wait_ge(k_used, 5 * DEC)
            for c in (1, 3):
                act.activation(p[:, c * 512:(c + 1) * 512], ps[ROWS:P, c, :], ACT.Copy).then_inc(odd_in, 1)
            act.activation(p[:, PAST + 1:PAST + 1 + WIN], ps[0:ROWS, 4, :], ACT.Copy).then_inc(win_out, 1)
            act.wait_ge(soft_dve, 9)
            act.activation(p[:, 0:PAST + 1], p[:, 0:PAST + 1], ACT.Exp, bias=col[:, 6:7], accum_out=col[:, 8:9]).then_inc(soft_exp, 1)
            act.wait_ge(soft_dve, 11)
            act.activation(p[:, PAST + 1:], p[:, PAST + 1:], ACT.Exp, bias=col[:, 7:8], accum_out=col[:, 9:10]).then_inc(soft_exp, 1)
            for i in range(3):
                act.wait_ge(p_turned, i + 1)
                act.activation(pT[:, 8 * i:8 * i + 8, :], ps[:, i, :].rearrange("p (a b) -> p a b", b=ROWS), ACT.Copy).then_inc(p_copied, 1)
            act.wait_ge(p_turned, 4)
            act.activation(pnT[:], ps[0:DEC, 3, 0:2 * ROWS].rearrange("p (a b) -> p a b", b=ROWS), ACT.Copy).then_inc(p_copied, 1)
            for b in range(4, DEC):
                load_v(act, "act", b)
            for i in range(2):
                act.wait_ge(v_used, 4 * i + 4)
                act.activation(o_odd[:, 4 * i:4 * i + 4, :], ps[ROWS:P, 5 + i, :].rearrange("p (b f) -> p b f", f=P), ACT.Copy).then_inc(odd_out, 1)

        @block.vector
        def _(dve):
            dve.memset(qz[:], 0.0).then_inc(cleared, 1)
            for h in range(NH):
                src = m.nqT[(h % 2) * HD:(h % 2 + 1) * HD, h // 2, SEQ:TOK]
                dve.tensor_copy(qc[:, :, h], src).then_inc(q_ready, 1)
            dve.wait_ge(cleared, 1)
            for h in range(NH):
                g = h // R
                src = m.nqT[(h % 2) * HD:(h % 2 + 1) * HD, h // 2, SEQ:TOK]
                flat = qz[g * HD:(g + 1) * HD].rearrange("p b r -> p (b r)")
                dve.tensor_copy(flat[:, h:h + (ROWS + NH) * (DEC - 1) + 1:ROWS + NH], src).then_inc(q_ready, 1)
            for w, kd in enumerate((m.selkT, m.winkT)):
                for g in range(G):
                    dve.tensor_copy(knew[g * HD:(g + 1) * HD, w, :], kd[g * HD:(g + 1) * HD, g, SEQ:TOK]).then_inc(q_ready, 1)

            def copy_k(first, last):
                for n in range(first, last):
                    dve.wait_ge(k_turned, n + 1)
                    if n >= 5:
                        dve.wait_ge(k_used, n - 4)
                    dve.tensor_copy(kT[:, n % 5, :], ps[:, 5 + n % 2, :]).then_inc(k_copied, 1)

            dve.wait_ge(gates_in, 16)
            dve.wait_ge(const_loaded, 16)
            dve.wait_ge(cmp_scores, 1)
            step = Steps(cmp_dve)
            step.done(dve.tensor_tensor(pc[:], ps[0:ROWS, 7, :], take("ownblocks"), ALU.add))
            step.fence(dve)
            step.done(dve.tensor_reduce(col[:, 0:1], pc[:], AX.X, ALU.max))
            step.fence(dve)
            step.done(dve.tensor_scalar(col[:, 1:2], col[:, 0:1], -1.0, None, ALU.mult))
            dve.wait_ge(cmp_exp, 1)
            dve.reciprocal(col[:, 3:4], col[:, 2:3]).then_inc(soft_dve, 1)
            dve.wait_ge(soft_dve, 1)
            step.done(dve.tensor_scalar(pc[:], pc[:], col[:, 3:4], None, ALU.mult))
            step.fence(dve)
            step.done(dve.tensor_tensor(halves[:], pc[:, 0:256], pc[:, 256:512], ALU.add))
            step.fence(dve)
            step.done(dve.tensor_reduce(imp[:, 0, :].rearrange("p (h q) -> p h q", h=2),
                                        halves[:].rearrange("p (h b q g) -> p h q b g", h=2, b=4, g=G), AX.XY, ALU.add))
            copy_k(0, 21)
            dve.wait_ge(importance, 1)
            step.done(dve.tensor_copy(imp[:, 1, :], ps[0:ROWS, 7, 0:NBLK]))
            step.fence(dve)
            mine = imp[:, 1, :].unsqueeze(2).broadcast_to([ROWS, NBLK, NBLK])
            others = imp[:, 1, :].unsqueeze(1).broadcast_to([ROWS, NBLK, NBLK])
            step.done(dve.tensor_tensor(gt[:], others, mine, ALU.is_gt))
            step.done(dve.tensor_tensor(eq[:], others, mine, ALU.is_equal))
            step.fence(dve)
            step.done(dve.tensor_tensor(eq[:], eq[:], take("earlier").rearrange("p (i j) -> p i j", j=NBLK), ALU.mult))
            step.fence(dve)
            step.done(dve.tensor_tensor(gt[:], gt[:], eq[:], ALU.add))
            step.fence(dve)
            step.done(dve.tensor_reduce(imp[:, 2, :], gt[:], AX.X, ALU.add))
            step.fence(dve)
            step.done(dve.tensor_scalar(imp[:, 3, :], imp[:, 2, :], NSEL - 0.5, NEG, ALU.is_gt, ALU.mult))
            step.fence(dve)
            copy_k(21, 5 * DEC)
            dve.wait_ge(k_used, 5 * DEC)
            soft = Steps(soft_dve, 1)
            for c in (0, 2, 1, 3):
                cols = slice(c * 512, (c + 1) * 512)
                if c % 2:
                    dve.wait_ge(odd_in, c // 2 + 1)
                scores = p[:, cols] if c % 2 else ps[0:ROWS, c, :]
                soft.done(dve.tensor_tensor(p[:, cols].rearrange("p (q h t) -> p q h t", q=4, h=2),
                                            scores.rearrange("p (q h t) -> p q h t", q=4, h=2),
                                            imp[:, 3, :].rearrange("p (h q) -> p q h", h=2)[:, 4 * c:4 * c + 4].unsqueeze(3)
                                            .broadcast_to([ROWS, 4, 2, CB]), ALU.add))
            dve.wait_ge(new_scores, 1)
            soft.done(dve.tensor_copy(p[:, PAST:PAST + 1 + WIN + 1:WIN + 1], ps[0:ROWS, 7, 0:2]))
            dve.wait_ge(win_out, 1)
            soft.done(dve.memset(p[:, PAST + 1:PAST + 2], NEG))
            soft.fence(dve)
            soft.done(dve.tensor_reduce(col[:, 4:5], p[:, 0:PAST + 1], AX.X, ALU.max))
            soft.fence(dve)
            soft.done(dve.tensor_scalar(col[:, 6:7], col[:, 4:5], -1.0, None, ALU.mult))
            soft.done(dve.tensor_reduce(col[:, 5:6], p[:, PAST + 1:], AX.X, ALU.max))
            soft.fence(dve)
            soft.done(dve.tensor_scalar(col[:, 7:8], col[:, 5:6], -1.0, None, ALU.mult))
            soft.done(dve.tensor_scalar(pc[:], pc[:], gates[:, 0:1], None, ALU.mult))
            for w, cols in enumerate((slice(0, PAST + 1), slice(PAST + 1, PAST + WIN + 2))):
                dve.wait_ge(soft_exp, w + 1)
                soft.done(dve.reciprocal(col[:, 10 + w:11 + w], col[:, 8 + w:9 + w]))
                soft.fence(dve)
                soft.done(dve.tensor_scalar(p[:, cols], p[:, cols], col[:, 10 + w:11 + w], gates[:, 1 + w:2 + w], ALU.mult, ALU.mult))
                soft.fence(dve)
                soft.done(dve.tensor_scalar(pn[:, w, :], take("ownrow"), p[:, cols.stop - 1:cols.stop], None, ALU.mult))
            out = Steps(out_dve)
            for i in range(2):
                dve.wait_ge(odd_out, i + 1)
                out.done(dve.tensor_tensor(o_sum[:, 4 * i:4 * i + 4, :], o_odd[:, 4 * i:4 * i + 4, :],
                                           ps[0:ROWS, 5 + i, :].rearrange("p (b f) -> p b f", f=P), ALU.add))
            out.fence(dve)
            out.done(dve.tensor_tensor(o_sum[:], o_sum[:], take("ownrow").unsqueeze(2).broadcast_to([ROWS, DEC, P]), ALU.mult))
            out.fence(dve)
            out.done(dve.tensor_reduce(o_row[:], o_sum[:].rearrange("p b f -> p f b"), AX.X, ALU.add))
            out.fence(dve)
            out.done(dve.tensor_tensor(o_row[:], o_row[:], ps[0:ROWS, 4, 0:P], ALU.add))
            dve.wait_ge(out_turned, 1)
            for h in range(NH):
                g = h // R
                dve.tensor_copy(m.mixT[(h % 2) * HD:(h % 2 + 1) * HD, 4 + h // 2, SEQ:TOK],
                                ps[g * HD:(g + 1) * HD, 3, h:ROWS:NH]).then_inc(placed, 1)


def stage_compress(nc, m, ps, io):
    with Stage(nc, "comp") as ctx:
        s = ctx.semaphore
        table_loaded = s("table_loaded")
        w1_loaded = [s("w1k_loaded"), s("w1v_loaded")]
        w2_loaded, pos_loaded = s("w2_loaded"), [s("posk_loaded"), s("posv_loaded")]
        pages_loaded = [s(f"pages_loaded{r}") for r in range(4)]
        pool_pages_loaded = [s(f"pool_pages_loaded{r}") for r in range(4)]
        act_pages_loaded = [s(f"act_pages_loaded{r}") for r in range(4)]
        prompt_in = s("prompt_in")
        hidden_made = s("hidden_made")
        hidden_in = s("hidden_in")
        bias_ready = s("bias_ready")
        gelu_dve, tanh_done = s("gelu_dve"), s("tanh_done")
        second_made = s("second_made")
        second_out = s("second_out")
        zeroed = s("zeroed")
        mean_made, centered, squared = s("mean_made"), s("centered"), s("squared")
        var_made, var_in, root_done, norm_dve = s("var_made"), s("var_in"), s("root_done"), s("norm_dve")
        gate_scaled = s("gate_scaled")

        A = m.A
        pages = [m.place("slab0_pages", [P, 73, P], F32, A), m.place("slab1_pages", [P, 64, P], F32, A + 73 * 512)]
        slab = [a[:].rearrange("p q (g d) -> p (q g) d", g=G) for a in pages]
        w1 = [m.place("w1_k", [P, HD, HD], F32, m.ring), m.place("w1_v", [P, HD, HD], F32, m.M + 4 * TOK * 4)]
        w2 = m.place("w2", [P, 2, HD], F32, m.ring + 16384)
        xh = m.place("hidden_x", [P, 144], F32, m.ring + 16896)
        uh = m.place("hidden_u", [P, 144], F32, m.ring + 17472)
        hid = m.place("hidden_gelu", [P, 144], F32, m.ring + 18048)
        table = m.place("page_table", [1, DEC * NPG], I32, m.ring + 18624)
        bias = m.small[:, 32:34]
        sq = [m.place(f"gn_square{i}", [P, TN], F32, m.stage + 1376 * i) for i in range(2)]
        rs = [m.place(f"gn_rstd{i}", [P, TN], F32, m.stage + 2752 + 1376 * i) for i in range(2)]
        caches = [io["cache_cmp_k"][0], io["cache_cmp_v"][0]]
        rounds = [(kv, r) for kv in range(2) for r in range(2)]
        units = [(j, t) for j in range(4) for t in range(3)]
        SHARES = [(32, 32, 0), (24, 24, 16), (24, 24, 16), (24, 24, 16)]

        def load_share(eng, n, which, sem):
            kv, r = rounds[n]
            first, count = sum(SHARES[n][:which]), SHARES[n][which]
            load_pages(eng, table, r * 64 + first, count, caches[kv],
                       lambda i, k: pages[r][:, bass.ds(i * 4 + (first + k), 1), :], sem[n])

        block = ctx.enter_context(nc.Block())

        @block.sync
        def _(sp):
            sp.dma_start(table[:], io["page_table"].rearrange("(a b) n -> a (b n)", a=1)).then_inc(table_loaded, 16)
            for h in range(2):
                sp.dma_start(w1[0][h * HD:(h + 1) * HD], io["cmp_w1_k"][0]).then_inc(w1_loaded[0], 16)
                for i, n in enumerate(("cmp_w2_k", "cmp_w2_v")):
                    sp.dma_start(w2[h * HD:(h + 1) * HD, i, :], io[n][0]).then_inc(w2_loaded, 16)
                sp.dma_start(slab[0][h * HD:(h + 1) * HD, 144, :], io["cmp_pos_k"][0]).then_inc(pos_loaded[0], 16)
            sp.wait_ge(table_loaded, 16)
            for n, (kv, r) in enumerate(rounds):
                if n >= 2:
                    sp.wait_ge(hidden_made, n - 1)
                if n == 2:
                    for h in range(2):
                        sp.dma_start(slab[0][h * HD:(h + 1) * HD, 144, :], io["cmp_pos_v"][0]).then_inc(pos_loaded[1], 16)
                load_share(sp, n, 0, pages_loaded)

        @block.gpsimd
        def _(pool):
            def load(n):
                load_share(pool, n, 1, pool_pages_loaded)

            pool.memset(m.kcpT[:], 0.0).then_inc(zeroed, 1)
            pool.memset(m.vcp[:], 0.0).then_inc(zeroed, 1)
            pool.tensor_copy(slab[0][:, 128:144, :], m.ck_tok[:, 0:NB, :].rearrange("p b (g d) -> p (b g) d", g=G)).then_inc(prompt_in, 1)
            pool.wait_ge(table_loaded, 16)
            load(0)
            load(1)
            pool.wait_ge(norm_dve, 3 * len(units))
            for h in range(2):
                pool.dma_start(w1[1][h * HD:(h + 1) * HD], io["cmp_w1_v"][0]).then_inc(w1_loaded[1], 16)
            pool.wait_ge(hidden_made, 1)
            pool.tensor_copy(slab[0][:, 128:144, :], m.cv_tok[:, 0:NB, :].rearrange("p b (g d) -> p (b g) d", g=G)).then_inc(prompt_in, 1)

            load(2)
            pool.wait_ge(hidden_made, 2)
            load(3)

        @block.tensor
        def _(pe):
            def mean(u):
                j, t = units[u]
                if u >= 2:
                    pe.wait_ge(centered, u - 1)
                pe.matmul(ps[:, u % 2, 0:TN], m.c("headmean"), m.mixT[:, j, t * TN:(t + 1) * TN],
                          start=True, stop=True).then_inc(mean_made, 1)

            mean(0)
            for u in range(len(units)):
                if u + 1 < len(units):
                    mean(u + 1)
                pe.wait_ge(squared, u + 1)
                if u >= 2:
                    pe.wait_ge(var_in, u - 1)
                pe.matmul(ps[:, 2 + u % 2, 0:TN], m.c("headmean"), sq[u % 2][:], start=True, stop=True).then_inc(var_made, 1)
            pe.wait_ge(w2_loaded, 64)
            for n, (kv, r) in enumerate(rounds):
                width = 128 if r else 145
                if r == 0:
                    pe.wait_ge(w1_loaded[kv], 32)
                    pe.wait_ge(pos_loaded[kv], 32)
                    pe.wait_ge(prompt_in, kv + 1)
                for which, loaded in enumerate((pages_loaded, pool_pages_loaded, act_pages_loaded) if n else (pages_loaded, pool_pages_loaded)):
                    pe.wait_ge(loaded[n], 16 * SHARES[n][which])
                if n >= 2:
                    pe.wait_ge(hidden_in, n - 1)
                for d in range(HD):
                    for h in range(2):
                        rows = slice(h * HD, (h + 1) * HD)
                        last = pe.matmul(ps[rows, 4 + n % 2, 0:width], w1[kv][rows, d, :], slab[r][rows, 0:width, d],
                                         start=(d == 0), stop=(d == HD - 1))
                last.then_inc(hidden_made, 1)
                pe.wait_ge(gelu_dve, 4 * (n + 1))
                if n:
                    pe.wait_ge(second_out, (6, 8, 12)[n - 1])
                if kv == 0:
                    for h in range(2):
                        rows = slice(h * HD, (h + 1) * HD)
                        w = 128 if r else 144
                        last = pe.matmul(ps[0:HD, 6 + h, 0:w], w2[rows, 0, :], hid[rows, 0:w], start=True, stop=True)
                else:
                    for h in range(2):
                        rows = slice(h * HD, (h + 1) * HD)
                        last = pe.matmul(ps[:, 6 + h, 0:HD], hid[rows, 0:128], w2[rows, 1, :], start=True, stop=True)
                        if r == 0:
                            for g in range(G):
                                last = pe.matmul(ps[32 * h:32 * h + NB, 6 + h, HD * (1 + g):HD * (2 + g)], hid[rows, 128 + g:144:2],
                                                 w2[rows, 1, :], start=True, stop=True)
                last.then_inc(second_made, 1)

        @block.scalar
        def _(act):
            for u in range(len(units) + 1):
                if u < len(units):
                    j, t = units[u]
                    act.wait_ge(centered, u + 1)
                    if u >= 2:
                        act.wait_ge(var_made, u - 1)
                    act.activation(sq[u % 2][:], m.mixT[:, j, t * TN:(t + 1) * TN], ACT.Square).then_inc(squared, 1)
                if u:
                    act.wait_ge(var_in, u)
                    act.activation(rs[(u - 1) % 2][:], rs[(u - 1) % 2][:], ACT.Sqrt).then_inc(root_done, 1)
            act.wait_ge(table_loaded, 16)
            load_share(act, 1, 2, act_pages_loaded)
            act.wait_ge(zeroed, 2)
            for n, (kv, r) in enumerate(rounds):
                w = 128 if r else 144
                act.wait_ge(bias_ready, kv + 1)
                act.wait_ge(hidden_made, n + 1)
                if n:
                    act.wait_ge(gelu_dve, 4 * n)
                act.activation(xh[:, 0:w], ps[:, 4 + n % 2, 0:w], ACT.Identity, bias=bias[:, kv:kv + 1]).then_inc(hidden_in, 1)
                act.wait_ge(gelu_dve, 4 * n + 3)
                act.activation(uh[:, 0:w], uh[:, 0:w], ACT.Tanh, scale=math.sqrt(2.0 / math.pi)).then_inc(tanh_done, 1)
                act.wait_ge(second_made, n + 1)
                for h in range(2):
                    src = ps[:, 6 + h, :]
                    if kv == 0:
                        act.activation(m.kcsT[0:HD, (2 * r + h) * P:(2 * r + h + 1) * P], src[0:HD, 0:128], ACT.Copy, scale=0.5).then_inc(second_out, 1)
                        if r == 0:
                            for b in range(2):
                                act.activation(m.kcpT[b * HD:(b + 1) * HD, :, 32 * h:32 * h + NB],
                                               src[0:HD, 128:144].rearrange("p (n g) -> p g n", g=G), ACT.Copy, scale=0.5).then_inc(second_out, 1)
                    else:
                        for b in range(2):
                            act.activation(m.vcs[:, 2 * r + h, b * HD:(b + 1) * HD], src[:, 0:HD], ACT.Copy, scale=0.5).then_inc(second_out, 1)
                        if r == 0:
                            act.activation(m.vcp[32 * h:32 * h + NB, :], src[32 * h:32 * h + NB, HD:3 * HD], ACT.Copy, scale=0.5).then_inc(second_out, 1)
                if n < 2:
                    load_share(act, n + 2, 2, act_pages_loaded)

        @block.vector
        def _(dve):
            def center(u):
                j, t = units[u]
                cols = slice(t * TN, (t + 1) * TN)
                dve.wait_ge(mean_made, u + 1)
                dve.tensor_tensor(m.mixT[:, j, cols], m.mixT[:, j, cols], ps[:, u % 2, 0:TN], ALU.subtract).then_inc(centered, 1)
                dve.tensor_scalar(m.mixT[:, 4 + j, cols], m.mixT[:, 4 + j, cols], m.lnT[:, 32 + j:33 + j], None, ALU.mult).then_inc(gate_scaled, 1)

            center(0)
            for u in range(len(units)):
                j, t = units[u]
                cols = slice(t * TN, (t + 1) * TN)
                o = m.mixT[:, j, cols]
                dve.wait_ge(var_made, u + 1)
                dve.tensor_scalar(rs[u % 2][:], ps[:, 2 + u % 2, 0:TN], EPS, None, ALU.add).then_inc(var_in, 1)
                if u + 1 < len(units):
                    center(u + 1)
                dve.wait_ge(root_done, u + 1)
                dve.reciprocal(rs[u % 2][:], rs[u % 2][:]).then_inc(norm_dve, 1)
                dve.wait_ge(norm_dve, 3 * u + 1)
                dve.tensor_tensor(o, o, rs[u % 2][:], ALU.mult).then_inc(norm_dve, 1)
                dve.wait_ge(norm_dve, 3 * u + 2)
                dve.wait_ge(gate_scaled, u + 1)
                dve.tensor_tensor(o, o, m.mixT[:, 4 + j, cols], ALU.mult).then_inc(norm_dve, 1)
            for n, (kv, r) in enumerate(rounds):
                w = 128 if r else 144
                if r == 0:
                    dve.wait_ge(hidden_made, n + 1)
                    dve.tensor_copy(bias[:, kv:kv + 1], ps[:, 4 + n % 2, 144:145]).then_inc(bias_ready, 1)
                dve.wait_ge(hidden_in, n + 1)
                dve.tensor_tensor(uh[:, 0:w], xh[:, 0:w], xh[:, 0:w], ALU.mult).then_inc(gelu_dve, 1)
                dve.wait_ge(gelu_dve, 4 * n + 1)
                dve.tensor_scalar(uh[:, 0:w], uh[:, 0:w], 0.044715, 1.0, ALU.mult, ALU.add).then_inc(gelu_dve, 1)
                dve.wait_ge(gelu_dve, 4 * n + 2)
                dve.tensor_tensor(uh[:, 0:w], uh[:, 0:w], xh[:, 0:w], ALU.mult).then_inc(gelu_dve, 1)
                dve.wait_ge(tanh_done, n + 1)
                if n:
                    dve.wait_ge(second_made, n)
                dve.scalar_tensor_tensor(hid[:, 0:w], uh[:, 0:w], 1.0, xh[:, 0:w], ALU.add, ALU.mult).then_inc(gelu_dve, 1)


def stage_attend(nc, m, ps, io):
    with Stage(nc, "att") as ctx:
        s = ctx.semaphore
        casts, sel_scores, win_scores, maxima = s("casts"), s("sel_scores"), s("win_scores"), s("maxima")
        exps, coef, scaled = s("exps"), s("coef"), s("scaled")
        k_hi, k_lo, q_hi, q_lo, half_out = s("k_hi"), s("k_lo"), s("q_hi"), s("q_lo"), s("half_out")
        turned, copied = s("turned"), s("copied")
        cmp_turned, cmp_copied, out_made, out_copied = s("cmp_turned"), s("cmp_copied"), s("out_made"), s("out_copied")

        PW = SEQ + WIN + P + CP
        p = [m.place(f"att_p{i}", [P, PW], F32, m.ring + 6816 * i) for i in range(3)]
        pcm = [m.place(f"att_p_cmp{i}", [P, R, CP], F32, m.ring + 20448 + 640 * i) for i in range(2)]
        col = m.place("att_columns", [P, 3, 12], F32, m.ring + 21728)
        bias_bf = m.place("att_cmp_bias", [P, NB, CP], BF16, m.ring + 21888)
        q_split = [m.place(f"att_q_split{i}", [P, NH // 2, 2, P], F32R, m.A + 57344 + 4096 * i) for i in range(2)]
        half = m.place("att_out_half", [HD, 4, P], F32, m.A + 65536)
        tok = (NB + 1) * P * 4
        o = m.N + 8 * TOK * 4
        sel_hi = m.place("sel_kT_hi", [P, G, SEQ], F32R, o)
        win_hi = m.place("win_kT_hi", [P, G, SEQ], F32R, o + 4 * tok)
        sel_lo = m.place("sel_kT_lo", [P, G, TOK], F32R, m.N + 4 * TOK * 4)
        win_lo = m.place("win_kT_lo", [P, G, TOK], F32R, m.N + 6 * TOK * 4)
        pT = [m.place(f"att_pT{i}", [P, 13, R, P], F32, m.A + 26624 * i) for i in range(2)]
        pcT = [m.place(f"att_p_cmpT{i}", [CP, R, P], F32, m.A + 53248 + 2048 * i) for i in range(2)]
        steps = [(i, g, r) for i in range(NB) for g in range(G) for r in range(R)]
        KW = WIN // P + 1

        def window(i):
            return max(0, i - KW + 1), i + 1

        groups, first_group = [], []
        for k, (i, g, r) in enumerate(steps):
            n = i + 1 + min(i + 1, KW)
            first_group.append(len(groups))
            groups += [(k, a, min(a + 4, n)) for a in range(0, n, 4)]
        first_group.append(len(groups))

        def block_cols(i, a):
            return slice(a * P, (a + 1) * P) if a <= i else slice(SEQ + (a - i - 1) * P, SEQ + (a - i) * P)

        block = ctx.enter_context(nc.Block())

        @block.tensor
        def _(pe):
            def keys(bank, g, a, w, hi, lo, q):
                for n, k in enumerate((hi, lo)):
                    if w == P:
                        last = pe.matmul(ps[:, bank, 0:2 * P].rearrange("p (a n) -> p a n", n=P), q,
                                         k[:, g, a:a + P].unsqueeze(1).broadcast_to([P, 2, P]), start=(n == 0), stop=(n == 1))
                    else:
                        last = pe.matmul(ps[:, bank, 0:w], q, k[:, g, a:a + w], start=(n == 0), stop=(n == 1))
                return last

            def sel_keys(k):
                i, g, r = steps[k]
                h = g * R + r
                q = q_split[i % 2][:, h // 2, h % 2, :]
                if g == 0 and r == 0:
                    pe.wait_ge(q_lo, 2 * i + 2)
                if k:
                    pe.wait_ge(exps, 3 * k - 2)
                for a in range(0, (i + 1) * P, 512):
                    keys(a // 512, g, a, min(512, (i + 1) * P - a), sel_hi, sel_lo, q)
                pe.matmul(ps[:, i // 4, (i % 4) * P:(i % 4 + 1) * P], m.ident_bf[:], m.causal_bf[:], start=False, stop=True,
                          skip_group_check=True).then_inc(sel_scores, 1)

            def other_keys(k):
                i, g, r = steps[k]
                h = g * R + r
                q = q_split[i % 2][:, h // 2, h % 2, :]
                if k:
                    pe.wait_ge(exps, 3 * k)
                lo, hi = window(i)
                for a in range(lo, hi, 4):
                    keys(2 + (a - lo) // 4, g, a * P, min(hi - a, 4) * P, win_hi, win_lo, q)
                    if a == lo and i >= KW - 1:
                        pe.matmul(ps[:, 2, 0:P], m.ident_bf[:], m.winlow_bf[:], start=False, stop=True, skip_group_check=True)
                    if a + 4 >= hi:
                        at = hi - 1 - lo
                        pe.matmul(ps[:, 2 + at // 4, (at % 4) * P:(at % 4 + 1) * P], m.ident_bf[:], m.causal_bf[:],
                                  start=False, stop=True, skip_group_check=True)
                rows = slice((h % 2) * HD, (h % 2 + 1) * HD)
                pe.matmul(ps[:, 3, 256:256 + CP], m.nqT[rows, h // 2, i * P:(i + 1) * P], m.kcpT[rows, g, :],
                          start=(i < KW - 1), stop=True, skip_group_check=True)
                pe.matmul(ps[:, 3, 256:256 + CP], m.ident_bf[:], bias_bf[:, i, :], start=False, stop=True,
                          skip_group_check=True).then_inc(win_scores, 1)

            def turn(k):
                i, g, r = steps[k]
                pe.wait_ge(scaled, 3 * (k + 1))
                for n in range(first_group[k], first_group[k + 1]):
                    _, a, b = groups[n]
                    if n >= 2:
                        pe.wait_ge(copied, n - 1)
                    for x in range(a, b):
                        last = pe.transpose(ps[:, 4 + n % 2, (x - a) * P:(x - a + 1) * P], p[k % 3][:, block_cols(i, x)], m.c("ident"))
                    last.then_inc(turned, 1)
                if r == R - 1:
                    grp = k // R
                    if grp >= 2:
                        pe.wait_ge(out_copied, 2 * (grp - 1))
                    for x in range(R):
                        last = pe.transpose(ps[0:CP, 6 + grp % 2, x * P:(x + 1) * P], pcm[grp % 2][:, x, :], m.c("ident"))
                    last.then_inc(cmp_turned, 1)

            def output(grp):
                i, g, _ = steps[grp * R]
                n = i + 1 + min(i + 1, KW)
                lo, _ = window(i)
                pe.wait_ge(copied, first_group[(grp + 1) * R])
                pe.wait_ge(cmp_copied, grp + 1)
                rows = slice(g * HD, (g + 1) * HD)
                out = [ps[e * HD:(e + 1) * HD, 6 + grp % 2, :] for e in range(2)]
                pe.matmul(out[1], m.vcp[:, rows], pcT[grp % 2][:], start=True, stop=False)
                for x in range(n):
                    v = m.sv_tok[:, x, rows] if x <= i else m.wv_tok[:, lo + x - i - 1, rows]
                    last = pe.matmul(out[x % 2], v, pT[grp % 2][:, x, :, :], start=(x == 0), stop=(x >= n - 2))
                last.then_inc(out_made, 1)

            pe.wait_ge(casts, 1)
            pe.wait_ge(k_lo, 2)
            for k in range(len(steps) + 2):
                if k < len(steps):
                    sel_keys(k)
                if k >= 2:
                    turn(k - 2)
                if k < len(steps):
                    other_keys(k)
                if k % R == 3 and k > R:
                    output(k // R - 1)
            output(len(steps) // R - 1)

        @block.scalar
        def _(act):
            def split_q(i):
                for e in range(2):
                    rows = slice(e * HD, (e + 1) * HD)
                    act.activation(q_split[i % 2][rows, :, e, :], m.nqT[rows, :, i * P:(i + 1) * P], ACT.Copy).then_inc(q_hi, 1)

            act.activation(sel_hi[:], m.selkT[:, :, 0:SEQ], ACT.Copy).then_inc(k_hi, 1)
            act.activation(win_hi[:], m.winkT[:, :, 0:SEQ], ACT.Copy).then_inc(k_hi, 1)
            split_q(0)
            for k in range(len(steps) + 2):
                if k % 8 == 2 and k // 8 + 1 < NB:
                    split_q(k // 8 + 1)
                if k >= 2:
                    t = k - 2
                    for n in range(first_group[t], first_group[t + 1]):
                        _, a, b = groups[n]
                        act.wait_ge(turned, n + 1)
                        if t % R == 0 and t // R >= 2:
                            act.wait_ge(out_made, t // R - 1)
                        act.activation(pT[(t // R) % 2][:, a:b, t % R, :],
                                       ps[:, 4 + n % 2, 0:(b - a) * P].rearrange("p (a n) -> p a n", n=P), ACT.Copy).then_inc(copied, 1)
                    if t % R == R - 1:
                        grp = t // R
                        act.wait_ge(cmp_turned, grp + 1)
                        act.activation(pcT[grp % 2][:], ps[0:CP, 6 + grp % 2, :].rearrange("p (a n) -> p a n", n=P), ACT.Copy).then_inc(cmp_copied, 1)
                if k < len(steps):
                    i, g, r = steps[k]
                    grp = k // R
                    if k >= 3:
                        act.wait_ge(turned, first_group[k - 2])
                    if k >= 2 * R and r == 0:
                        act.wait_ge(cmp_turned, grp - 1)
                    c = col[:, k % 3, :]
                    act.wait_ge(maxima, 3 * k + 1)
                    w = (i + 1) * P
                    act.activation(p[k % 3][:, 0:w], ps[:, 0:2, :].rearrange("p a n -> p (a n)")[:, 0:w], ACT.Exp,
                                   bias=c[:, 1:2], accum_out=c[:, 4:5]).then_inc(exps, 1)
                    act.wait_ge(maxima, 3 * k + 3)
                    w = min(i + 1, KW) * P
                    act.activation(p[k % 3][:, SEQ:SEQ + w], ps[:, 2:4, :].rearrange("p a n -> p (a n)")[:, 0:w], ACT.Exp,
                                   bias=c[:, 2:3], accum_out=c[:, 5:6]).then_inc(exps, 1)
                    act.activation(pcm[grp % 2][:, r, :], ps[:, 3, 256:256 + CP], ACT.Exp, bias=c[:, 0:1],
                                   accum_out=c[:, 3:4]).then_inc(exps, 1)

        @block.vector
        def _(dve):
            def split_q(i):
                for e in range(2):
                    rows, other = slice(e * HD, (e + 1) * HD), slice((1 - e) * HD, (2 - e) * HD)
                    dve.wait_ge(q_hi, 2 * i + e + 1)
                    dve.tensor_tensor(q_split[i % 2][other, :, e, :], m.nqT[rows, :, i * P:(i + 1) * P],
                                      q_split[i % 2][rows, :, e, :].bitcast(F32), ALU.subtract).then_inc(q_lo, 1)

            def add_halves(grp):
                i, g, _ = steps[grp * R]
                dve.wait_ge(out_made, grp + 1)
                if grp:
                    dve.wait_ge(out_copied, 2 * grp)
                dve.tensor_copy(half[:], ps[HD:P, 6 + grp % 2, :].rearrange("p (a n) -> p a n", n=P)).then_inc(half_out, 1)
                dve.wait_ge(half_out, grp + 1)
                for e in range(2):
                    dve.tensor_tensor(m.mixT[e * HD:(e + 1) * HD, 4 + 2 * g:6 + 2 * g, i * P:(i + 1) * P],
                                      ps[0:HD, 6 + grp % 2, :].rearrange("p (a e n) -> p e a n", e=2, n=P)[:, e],
                                      half[:].rearrange("p (a e) n -> p e a n", e=2)[:, e], ALU.add).then_inc(out_copied, 1)

            dve.tensor_copy(bias_bf[:], m.c("cmpbias").rearrange("p (a n) -> p a n", n=CP)).then_inc(casts, 1)
            for n, (k, hi, lo) in enumerate(((m.selkT, sel_hi, sel_lo), (m.winkT, win_hi, win_lo))):
                dve.wait_ge(k_hi, n + 1)
                dve.tensor_tensor(lo[:, :, 0:SEQ], k[:, :, 0:SEQ], hi[:].bitcast(F32), ALU.subtract).then_inc(k_lo, 1)
            split_q(0)
            for k in range(len(steps) + 2):
                if k < len(steps):
                    i, g, r = steps[k]
                    c = col[:, k % 3, :]
                    dve.wait_ge(sel_scores, k + 1)
                    if k >= 3:
                        dve.wait_ge(scaled, 3 * (k - 2))
                    dve.tensor_reduce(c[:, 1:2], ps[:, 0:2, :].rearrange("p a n -> p (a n)")[:, 0:(i + 1) * P], AX.X, ALU.max, negate=True).then_inc(maxima, 1)
                if 1 <= k <= len(steps):
                    t = k - 1
                    i, g, r = steps[t]
                    h = g * R + r
                    c = col[:, t % 3, :]
                    dve.wait_ge(exps, 3 * (t + 1))
                    dve.reciprocal(c[:, 6:9], c[:, 3:6]).then_inc(coef, 1)
                    dve.wait_ge(coef, 2 * t + 1)
                    dve.tensor_tensor(c[:, 9:12], c[:, 6:9], m.gate_tok[:, i, 3 * h:3 * h + 3], ALU.mult).then_inc(coef, 1)
                    dve.wait_ge(coef, 2 * t + 2)
                    w = (i + 1) * P
                    dve.tensor_scalar(p[t % 3][:, 0:w], p[t % 3][:, 0:w], c[:, 10:11], None, ALU.mult).then_inc(scaled, 1)
                    w = min(i + 1, KW) * P
                    dve.tensor_scalar(p[t % 3][:, SEQ:SEQ + w], p[t % 3][:, SEQ:SEQ + w], c[:, 11:12], None, ALU.mult).then_inc(scaled, 1)
                    pc = pcm[(t // R) % 2][:, r, :]
                    dve.scalar_tensor_tensor(pc, pc, c[:, 9:10], m.c("cmpvalid")[:, i * CP:(i + 1) * CP], ALU.mult, ALU.mult).then_inc(scaled, 1)
                if k % 8 == 3 and k // 8 + 1 < NB:
                    split_q(k // 8 + 1)
                if k < len(steps):
                    i, g, r = steps[k]
                    c = col[:, k % 3, :]
                    dve.wait_ge(win_scores, k + 1)
                    dve.tensor_reduce(c[:, 2:3], ps[:, 2:4, :].rearrange("p a n -> p (a n)")[:, 0:min(i + 1, KW) * P], AX.X, ALU.max, negate=True).then_inc(maxima, 1)
                    dve.tensor_reduce(c[:, 0:1], ps[:, 3, 256:256 + CP], AX.X, ALU.max, negate=True).then_inc(maxima, 1)
                if k % R == 0 and k > R:
                    add_halves(k // R - 2)
            add_halves(len(steps) // R - 1)


def rstd_tiles(m, ps, bank, acc, rep, sums_in, spread, mean_in, root, ready):

    def pe_part(pe):
        for t in range(3):
            sums_in(pe, t)
            pe.matmul(ps[:, bank + t, 0:TN], m.c("ones"), acc[:, t * TN:(t + 1) * TN], start=True, stop=True).then_inc(spread, 1)

    def dve_part(dve):
        for t in range(3):
            dve.wait_ge(spread, t + 1)
            dve.tensor_scalar(rep[:, t * TN:(t + 1) * TN], ps[:, bank + t, 0:TN], 1.0 / D_MODEL, EPS, ALU.mult,
                              ALU.add).then_inc(mean_in, 1)
        for t in range(3):
            dve.wait_ge(root, t + 1)
            dve.reciprocal(rep[:, t * TN:(t + 1) * TN], rep[:, t * TN:(t + 1) * TN]).then_inc(ready, 1)

    def act_part(act):
        for t in range(3):
            act.wait_ge(mean_in, t + 1)
            act.activation(rep[:, t * TN:(t + 1) * TN], rep[:, t * TN:(t + 1) * TN], ACT.Sqrt).then_inc(root, 1)

    return pe_part, act_part, dve_part


def stage_mix(nc, m, ps, io, h_rows):
    with Stage(nc, "mix") as ctx:
        s = ctx.semaphore
        w = Stream(ctx, m, ps)
        mix_hi, mix_lo = s("mix_hi"), s("mix_lo")
        x_loaded, xs_loaded = s("x_loaded"), s("xs_loaded")
        squared, summed = s("squared"), s("summed")
        spread1, mean1, root1, ready1 = s("spread1"), s("mean1"), s("root1"), s("ready1")
        x_turned, normed, h_ready, h_squared, h_summed = s("x_turned"), s("normed"), s("h_ready"), s("h_squared"), s("h_summed")
        cleared, n_hi, n_lo, h_stored = s("cleared"), s("n_hi"), s("n_lo"), s("h_stored")

        hT = m.place("mixed_then_h", [P, KT, TOK], F32, m.M)
        x = m.place("x_rows_again", [P, NB, D_MODEL], F32, m.N)
        xs = m.place("x_decoded_again", [DEC, D_MODEL], F32, m.N + 32768)
        o = m.N + 36864
        acc = m.place("square_sums", [P, TOK], F32, o)
        rep = m.place("rstd_everywhere", [P, TOK], F32, o + 4128)
        sq = [m.place(f"squares{i}", [P, TN], F32, o + 8256 + 1376 * i) for i in range(3)]
        acc2 = m.h_squares = m.place("h_square_sums", [P, TOK], F32, o + 12384)
        tmp = [m.place(f"h_squares{i}", [P, 512], F32, o + 16512 + 2048 * i) for i in range(3)]
        src = io["w_o"][0].rearrange("(kt p) n -> p kt n", p=P)
        units = [(kt, h) for h in (2, 0, 1) for kt in range(KT)]
        CH = KT

        def span(h):
            return (slice(0, 512), slice(512, 1024), slice(SEQ, TOK))[h]

        pe_rstd1, act_rstd1, dve_rstd1 = rstd_tiles(m, ps, 3, acc, rep, lambda pe, t: pe.wait_ge(summed, 3 * KT + 3),
                                                    spread1, mean1, root1, ready1)
        block = ctx.enter_context(nc.Block())

        @block.sync
        def _(sp):
            with sp.Fori(0, CH // 2) as i:
                for t in range(2):
                    w.load(sp, i * 2 + t, t, src[:, :, bass.ds(i * (2 * P) + t * P, P)])
            for kt in range(KT):
                sp.wait_ge(h_ready, 2 * KT + kt + 1)
                sp.dma_start(h_rows[:, kt], hT[:, kt, :]).then_inc(h_stored, 16)
            sp.wait_ge(h_stored, 16 * KT)

        @block.tensor
        def _(pe):
            w.start(pe)
            pe.wait_ge(mix_lo, KT)
            with pe.Fori(0, CH // 2) as i:
                for t in range(2):
                    w.multiply(pe, i * 2 + t, t)
            pe_rstd1(pe)
            pe.wait_ge(x_loaded, 16)
            pe.wait_ge(xs_loaded, 16)
            for u, (kt, h) in enumerate(units):
                if u >= 2:
                    pe.wait_ge(h_ready, u - 1)
                if h < 2:
                    for i in range(4):
                        last = pe.transpose(ps[:, 6 + u % 2, i * P:(i + 1) * P], x[:, 4 * h + i, kt * P:(kt + 1) * P], m.c("ident"))
                else:
                    last = pe.transpose(ps[:, 6 + u % 2, 0:DEC], xs[:, kt * P:(kt + 1) * P], m.c("ident")[0:DEC, 0:DEC])
                last.then_inc(x_turned, 1)

        @block.gpsimd
        def _(pool):
            pool.wait_ge(w.lo_ready, 4)
            pool.dma_start(x[:], io["x_prompt"][0].rearrange("(t p) d -> p t d", p=P)).then_inc(x_loaded, 16)
            pool.dma_start(xs[:], io["x_sample"][:, 0, :]).then_inc(xs_loaded, 16)
            pool.memset(acc2[:], 0.0).then_inc(cleared, 1)
            pool.wait_ge(cleared, 1)
            for u, (kt, h) in enumerate(units):
                cols = span(h)
                pool.wait_ge(h_squared, u + 1)
                if u:
                    pool.wait_ge(h_summed, u)
                pool.tensor_tensor(acc2[:, cols], acc2[:, cols], tmp[u % 3][:, 0:cols.stop - cols.start], ALU.add).then_inc(h_summed, 1)

        @block.scalar
        def _(act):
            for kt in range(KT):
                act.activation(m.hi[:, kt, :], m.mixT[:, kt, :], ACT.Copy).then_inc(mix_hi, 1)
            w.round_hi(act, 0, 0, 0)

            def evacuate(n, kt):
                dst = hT[:, kt, :] if isinstance(kt, int) else hT[:, bass.ds(kt, 1), :].rearrange("p a n -> p (a n)")
                for t, cols, tile in w.tiles(act, n):
                    act.wait_ge(summed, n * 3 + (t + 1))
                    act.activation(sq[t][:], tile, ACT.Square).then_inc(squared, 1)
                    act.activation(dst[:, cols], tile, ACT.Copy).then_inc(w.bank_free, 1)

            act.wait_ge(mix_lo, KT)
            with act.Fori(0, CH // 2 - 1) as i:
                for t in range(2):
                    w.round_hi(act, i * 2 + (t + 1), 1 - t, i + t)
                    evacuate(i * 2 + t, i * 2 + t)
            w.round_hi(act, CH - 1, 1, CH // 2 - 1)
            evacuate(CH - 2, CH - 2)
            evacuate(CH - 1, CH - 1)
            act_rstd1(act)
            for u, (kt, h) in enumerate(units):
                cols = span(h)
                act.wait_ge(h_ready, u + 1)
                act.activation(m.hi[:, kt, cols], hT[:, kt, cols], ACT.Copy, scale=m.lnT[:, 16 + kt:17 + kt]).then_inc(n_hi, 1)
                if u >= 3:
                    act.wait_ge(h_summed, u - 2)
                act.activation(tmp[u % 3][:, 0:cols.stop - cols.start], hT[:, kt, cols], ACT.Square).then_inc(h_squared, 1)

        @block.vector
        def _(dve):
            w.start_loads(dve)
            dve.sem_inc(summed, 3)
            for kt in range(KT):
                dve.wait_ge(mix_hi, kt + 1)
                dve.tensor_tensor(m.lo[:, kt, :], m.mixT[:, kt, :], m.hi[:, kt, :].bitcast(F32), ALU.subtract).then_inc(mix_lo, 1)
            w.reduce_lo(dve, 0, 0, 0)

            def add_squares(n):
                for t in range(3):
                    cols = slice(t * TN, (t + 1) * TN)
                    dve.wait_ge(squared, n * 3 + (t + 1))
                    dve.wait_ge(summed, n * 3 + (t + 1))
                    dve.tensor_tensor(acc[:, cols], acc[:, cols], sq[t][:], ALU.add).then_inc(summed, 1)

            dve.memset(acc[:], 0.0).then_inc(normed, 1)
            dve.wait_ge(normed, 1)
            with dve.Fori(0, CH // 2 - 1) as i:
                for t in range(2):
                    w.reduce_lo(dve, i * 2 + (t + 1), 1 - t, i + t)
                    add_squares(i * 2 + t)
            w.reduce_lo(dve, CH - 1, 1, CH // 2 - 1)
            add_squares(CH - 2)
            add_squares(CH - 1)
            dve_rstd1(dve)
            dve.wait_ge(ready1, 3)
            dve.wait_ge(w.bank_free, 3 + 3 * CH)

            def reduce_h(u):
                kt, h = units[u]
                cols = span(h)
                dve.wait_ge(n_hi, u + 1)
                dve.scalar_tensor_tensor(m.lo[:, kt, cols], hT[:, kt, cols], m.lnT[:, 16 + kt:17 + kt],
                                         m.hi[:, kt, cols].bitcast(F32), ALU.mult, ALU.subtract).then_inc(n_lo, 1)

            for u, (kt, h) in enumerate(units):
                cols = span(h)
                dve.scalar_tensor_tensor(hT[:, kt, cols], hT[:, kt, cols], m.lnT[:, 8 + kt:9 + kt], rep[:, cols],
                                         ALU.mult, ALU.mult).then_inc(normed, 1)
                if u:
                    reduce_h(u - 1)
                dve.wait_ge(normed, 2 + u)
                dve.wait_ge(x_turned, u + 1)
                dve.tensor_tensor(hT[:, kt, cols], hT[:, kt, cols], ps[:, 6 + u % 2, 0:cols.stop - cols.start], ALU.add).then_inc(h_ready, 1)
            reduce_h(len(units) - 1)


def stage_mlp(nc, m, ps, io, h_rows):
    with Stage(nc, "mlp") as ctx:
        s = ctx.semaphore
        w = Stream(ctx, m, ps)
        cleared, squared, f_hi, f_lo = s("cleared"), s("squared"), s("f_hi"), s("f_lo")
        y_squared, y_summed, sums_cleared, h_loaded = s("y_squared"), s("y_summed"), s("sums_cleared"), s("h_loaded")
        spread, mean, root, ready = s("spread"), s("mean"), s("root"), s("ready")
        pe_rstd, act_rstd, dve_rstd = rstd_tiles(m, ps, 3, m.h_squares, m.rstd_ffn, lambda pe, t: None, spread, mean, root, ready)
        T8 = KT * TOK * 4
        fhi = m.place("hidden_hi", [P, KT, TOK], F32R, m.M)
        flo = m.place("hidden_lo", [P, KT, TOK], F32R, m.A + 2 * T8)
        y = m.y_handle = m.place("mlp_out", [P, KT, TOK], F32, m.A + 3 * T8)
        assert m.A + 4 * T8 <= int(nc.sbuf_usable_end)
        r = [m.place(f"relu{i}", [P, TN], F32, m.tables + 1376 * i) for i in range(3)]
        f = [m.place(f"relu_squared{i}", [P, TN], F32, m.tables + 4128 + 1376 * i) for i in range(3)]
        up = io["w_up"][0].rearrange("(kt p) n -> p kt n", p=P)
        down = io["w_down"][0].rearrange("(kt p) n -> p kt n", p=P)
        PAIRS = KT // 2
        block = ctx.enter_context(nc.Block())

        def quarters(eng, up_chunk, down_chunk):
            def quarter(q, last):
                with eng.Fori(0, PAIRS) as i:
                    for t in range(2):
                        up_chunk(q, i, t)
                with eng.Fori(0, PAIRS - last) as i:
                    for t in range(2):
                        down_chunk(q, i, t, False)
                if last:
                    for t in range(2):
                        down_chunk(q, PAIRS - 1, t, t == 1)

            with eng.Fori(0, QUARTERS - 1) as q:
                quarter(q, False)
            quarter(QUARTERS - 1, 1)

        def n_up(q, i, t):
            return q * 16 + (i * 2 + t)

        def n_down(q, i, t):
            return q * 16 + (i * 2 + (8 + t))

        def tile_of(buf, i, t, cols):
            return buf[:, bass.ds(i * 2 + t, 1), cols].rearrange("p a n -> p (a n)")

        @block.sync
        def _(sp):
            def load_up(q, i, t):
                w.load(sp, n_up(q, i, t), t, up[:, :, bass.ds(q * D_MODEL + i * (2 * P) + t * P, P)])

            def load_down(q, i, t, last):
                w.load(sp, n_down(q, i, t), t, down[:, bass.ds(q * KT, KT), bass.ds(i * (2 * P) + t * P, P)])

            quarters(sp, load_up, load_down)
            sp.wait_ge(w.tile_done, 6 + 3 * (16 * (QUARTERS - 1) + 8))
            sp.dma_start(m.h_again[:], h_rows).then_inc(h_loaded, 16)
            sp.wait_ge(h_loaded, 16)

        @block.tensor
        def _(pe):
            w.start(pe)
            pe_rstd(pe)

            def down_chunk(q, i, t, last):
                pe.wait_ge(f_lo, q * 24 + 27)
                w.multiply(pe, n_down(q, i, t), t, fhi, flo)

            quarters(pe, lambda q, i, t: w.multiply(pe, n_up(q, i, t), t), down_chunk)

        @block.scalar
        def _(act):
            w.round_hi(act, 0, 0, 0)
            act_rstd(act)

            def up_chunk(q, i, t):
                w.round_hi(act, n_up(q, i, t + 1), 1 - t, q * 8 + (i + t))
                for x in range(3):
                    cols = slice(x * TN, (x + 1) * TN)
                    done = q * 24 + (i * 6 + (3 * t + x + 1))
                    act.wait_ge(w.bank_free, q * 48 + (i * 6 + (3 * t + x + 4)))
                    act.wait_ge(f_lo, done)
                    act.activation(f[x][:], r[x][:], ACT.Square).then_inc(squared, 1)
                    act.wait_ge(squared, done)
                    act.activation(tile_of(fhi, i, t, cols), f[x][:], ACT.Copy).then_inc(f_hi, 1)

            def down_chunk(q, i, t, last):
                if not last:
                    w.round_hi(act, n_down(q, i, t + 1), 1 - t, q * 8 + (i + (4 + t)))
                if isinstance(q, int):
                    for x in range(3):
                        act.wait_ge(w.bank_free, n_down(q, i, t) * 3 + (3 + x + 1))
                        act.wait_ge(y_summed, i * 6 + (3 * t + x + 1))
                        act.activation(f[x][:], tile_of(y, i, t, slice(x * TN, (x + 1) * TN)), ACT.Square).then_inc(y_squared, 1)

            quarters(act, up_chunk, down_chunk)

        @block.gpsimd
        def _(pool):
            def add_squares(i, t):
                for x in range(3):
                    sums = m.y_squares[:, x * TN:(x + 1) * TN]
                    pool.wait_ge(y_squared, i * 6 + (3 * t + x + 1))
                    pool.wait_ge(y_summed, i * 6 + (3 * t + x + 1))
                    pool.tensor_tensor(sums, sums, f[x][:], ALU.add).then_inc(y_summed, 1)

            pool.wait_ge(spread, 3)
            pool.memset(y[:], 0.0).then_inc(cleared, 1)
            pool.sem_inc(y_summed, 3)
            pool.wait_ge(squared, 24 * QUARTERS)
            pool.memset(m.y_squares[:], 0.0).then_inc(sums_cleared, 1)
            pool.wait_ge(sums_cleared, 1)
            with pool.Fori(0, PAIRS) as i:
                for t in range(2):
                    add_squares(i, t)

        @block.vector
        def _(dve):
            w.start_loads(dve)
            dve.sem_inc(f_lo, 3)
            w.reduce_lo(dve, 0, 0, 0)
            dve_rstd(dve)
            dve.wait_ge(ready, 3)
            dve.wait_ge(cleared, 1)

            def up_chunk(q, i, t):
                w.reduce_lo(dve, n_up(q, i, t + 1), 1 - t, q * 8 + (i + t))
                for x in range(4):
                    if x < 3:
                        dve.wait_ge(w.tile_done, q * 48 + (i * 6 + (3 * t + x + 7)))
                        dve.scalar_tensor_tensor(r[x][:], ps[:, x, 0:TN], 0.0, m.rstd_ffn[:, x * TN:(x + 1) * TN], ALU.max, ALU.mult).then_inc(w.bank_free, 1)
                    if x:
                        cols = slice((x - 1) * TN, x * TN)
                        dve.wait_ge(f_hi, q * 24 + (i * 6 + (3 * t + x)))
                        dve.tensor_tensor(tile_of(flo, i, t, cols), f[x - 1][:], tile_of(fhi, i, t, cols).bitcast(F32),
                                          ALU.subtract).then_inc(f_lo, 1)

            def down_chunk(q, i, t, last):
                if not last:
                    w.reduce_lo(dve, n_down(q, i, t + 1), 1 - t, q * 8 + (i + (4 + t)))
                for x, cols, tile in w.tiles(dve, n_down(q, i, t)):
                    dst = tile_of(y, i, t, cols)
                    dve.wait_ge(w.bank_free, q * 48 + (i * 6 + (3 * t + x + 25)))
                    dve.tensor_tensor(dst, dst, tile, ALU.add).then_inc(w.bank_free, 1)

            quarters(dve, up_chunk, down_chunk)


def stage_out(nc, m, ps, io):
    with Stage(nc, "out") as ctx:
        s = ctx.semaphore
        spread, mean, root, ready = s("spread"), s("mean"), s("root"), s("ready")
        normed, y_ready, turned, copied, stored = s("normed"), s("y_ready"), s("turned"), [s("copied_act"), s("copied_dve")], s("stored")
        T8 = KT * TOK * 4
        y, h = m.y_handle, m.h_again
        rep = m.place("out_rstd", [P, TOK], F32, m.A + T8)
        rows = m.place("y_rows", [P, NB, D_MODEL], F32, m.M)
        rows_dec = m.place("y_rows_decoded", [DEC, D_MODEL], F32, m.A + T8 + 4128)
        pe_rstd, act_rstd, dve_rstd = rstd_tiles(m, ps, 0, m.y_squares, rep, lambda pe, t: None, spread, mean, root, ready)
        units = [(b, c) for b in range(NB + 1) for c in range(2)]
        HALVES = (slice(0, SEQ // 2), slice(SEQ // 2, TOK))
        block = ctx.enter_context(nc.Block())

        @block.sync
        def _(sp):
            for b in range(NB + 1):
                for e in range(2):
                    sp.wait_ge(copied[e], b + 1)
                if b < NB:
                    sp.dma_start(io["y_prompt"][0, b * P:(b + 1) * P, :], rows[:, b, :]).then_inc(stored, 16)
                else:
                    sp.dma_start(io["y_sample"][:, 0, :], rows_dec[:]).then_inc(stored, 16)
            sp.wait_ge(stored, 16 * (NB + 1))

        @block.scalar
        def _(act):
            act_rstd(act)
            for b in range(NB + 1):
                act.wait_ge(turned, 2 * b + 1)
                n = P if b < NB else DEC
                act.activation(rows[:, b, 0:512] if b < NB else rows_dec[:, 0:512], ps[0:n, 3 + (2 * b) % 4, :], ACT.Copy).then_inc(copied[0], 1)

        @block.vector
        def _(dve):
            def add_h(n):
                kt, cols = n % KT, HALVES[n // KT]
                dve.wait_ge(normed, n + 1)
                dve.tensor_tensor(y[:, kt, cols], y[:, kt, cols], h[:, kt, cols], ALU.add).then_inc(y_ready, 1)

            dve_rstd(dve)
            dve.wait_ge(ready, 3)
            for n in range(2 * KT):
                kt, cols = n % KT, HALVES[n // KT]
                dve.scalar_tensor_tensor(y[:, kt, cols], y[:, kt, cols], m.lnT[:, 24 + kt:25 + kt], rep[:, cols], ALU.mult, ALU.mult).then_inc(normed, 1)
                if n:
                    add_h(n - 1)
            add_h(2 * KT - 1)
            for b in range(NB + 1):
                dve.wait_ge(turned, 2 * b + 2)
                n = P if b < NB else DEC
                dve.tensor_copy(rows[:, b, 512:1024] if b < NB else rows_dec[:, 512:1024], ps[0:n, 3 + (2 * b + 1) % 4, :]).then_inc(copied[1], 1)

        @block.tensor
        def _(pe):
            pe_rstd(pe)
            for u, (b, c) in enumerate(units):
                pe.wait_ge(y_ready, (b // 4 > 0) * KT + 4 * c + 4)
                if u >= 4:
                    pe.wait_ge(copied[c], b - 1)
                cols = slice(b * P, (b + 1) * P) if b < NB else slice(SEQ, TOK)
                n = P if b < NB else DEC
                for i in range(4):
                    last = pe.transpose(ps[0:n, 3 + u % 4, i * P:(i + 1) * P], y[:, 4 * c + i, cols], m.c("ident"))
                last.then_inc(turned, 1)


def build(nc, io):
    m = Memory(nc)
    h_rows = nc.dram_tensor("h_features", [P, KT, TOK], F32, kind="Internal").ap()
    with ExitStack() as ctx:
        ps = ctx.enter_context(nc.psum_tensor("psum", [P, 8, 512], F32))
        stage_prepare(nc, m, ps, io)
        stage_project(nc, m, ps, io)
        stage_compress(nc, m, ps, io)
        stage_decode(nc, m, ps, io)
        stage_attend(nc, m, ps, io)
        stage_mix(nc, m, ps, io, h_rows)
        stage_mlp(nc, m, ps, io, h_rows)
        stage_out(nc, m, ps, io)


_INS = ["x_prompt", "x_sample", "state_ret", "cache_cmp_k", "cache_cmp_v", "cache_sel_k", "cache_sel_v",
        "cache_win_k", "cache_win_v", "page_table", "ln_pre_mix", "w_in", "ret_gn_w", "cmp_pos_k", "cmp_w1_k",
        "cmp_w2_k", "cmp_pos_v", "cmp_w1_v", "cmp_w2_v", "w_o", "ln_post_mix", "ln_pre_ffn", "w_up", "w_down",
        "ln_post_ffn"]
_ROWS_P, _ROWS_S = (1, 1, SEQ, G, HD), (1, DEC, 1, G, HD)
_OUTS = [("y_prompt", (1, SEQ, D_MODEL)), ("y_sample", (DEC, 1, D_MODEL)),
         ("ret_state_prompt", (1, 1, RH, HD, HD)),
         ("cmp_k_prompt", _ROWS_P), ("cmp_v_prompt", _ROWS_P), ("sel_k_prompt", _ROWS_P), ("sel_v_prompt", _ROWS_P),
         ("win_k_prompt", (1, 1, WIN, G, HD)), ("win_v_prompt", (1, 1, WIN, G, HD)),
         ("ret_state_sample", (1, DEC, RH, HD, HD)),
         ("cmp_k_sample", _ROWS_S), ("cmp_v_sample", _ROWS_S), ("sel_k_sample", _ROWS_S), ("sel_v_sample", _ROWS_S),
         ("win_k_sample", (1, DEC, WIN, G, HD)), ("win_v_sample", (1, DEC, WIN, G, HD))]


def kernel(**inputs):
    import numpy as _np
    import concourse.bacc as _bacc
    from concourse import mybir as _mybir
    from concourse.bass_utils import run_bass_kernel_spmd as _run

    nc = _bacc.Bacc("TRN2", target_bir_lowering=False, num_devices=1)
    arrays, io = {}, {}
    for name in _INS:
        a = _np.ascontiguousarray(inputs[name])
        arrays[f"in_{name}"] = a
        io[name] = nc.dram_tensor(f"in_{name}", a.shape, _mybir.dt.from_np(a.dtype), kind="ExternalInput").ap()
    arrays["in_const"], arrays["in_dec_const"] = constants()
    io["const"] = nc.dram_tensor("in_const", (P, CW), F32, kind="ExternalInput").ap()
    io["dec_const"] = nc.dram_tensor("in_dec_const", (ROWS, DW), F32, kind="ExternalInput").ap()
    for name, shape in _OUTS:
        io[name] = nc.dram_tensor(f"out_{name}", shape, F32, kind="ExternalOutput").ap()
    build(nc, io)
    r = _run(nc, [arrays], core_ids=[0])
    return tuple(r.results[0][f"out_{name}"] for name, _ in _OUTS)
```
